# Optimizing a Trainium2 kernel written in Bass

```python
import math
import jax, jax.numpy as jnp
from jax import lax
import numpy as np

D_MODEL = 1024
BATCH = 1
SEQ = 1024
DEPTH = 2

HEAD_DIM = 64
GRID_W = 64
NA_HEADS = 4
NA_ROWS_MAX = 8
NA_COLS = 16
SWA_Q_HEADS = 6
SWA_KV_HEADS = 2
SWA_GROUP = SWA_Q_HEADS // SWA_KV_HEADS
SWA_HALF_WINDOW = 128
DIL_HEADS = 6
DIL_BRANCHES = ((128, 1), (512, 4), (2048, 16))
ATTN_BLOCK = 128
NA_W = NA_HEADS * HEAD_DIM
SWA_QW = SWA_Q_HEADS * HEAD_DIM
SWA_KVW = SWA_KV_HEADS * HEAD_DIM
DIL_W = DIL_HEADS * HEAD_DIM
IN_W = 3 * NA_W + SWA_QW + 2 * SWA_KVW + 3 * DIL_W
MIX_W = NA_W + SWA_QW + DIL_W
FFN_HIDDEN = -(-8 * D_MODEL // (3 * 256)) * 256
NORM_EPS = 1e-6
NEG_INF = -1e30

kernel_name = "hymba_style_natten_swa_dilated_encoder"

def rms_norm(x, g):
    xf = x.astype(jnp.float32)
    y = xf * lax.rsqrt(jnp.mean(xf * xf, axis=-1, keepdims=True) + NORM_EPS)
    return (y * g.astype(jnp.float32)).astype(x.dtype)

def alibi_slopes(n):
    return 2.0 ** (-8.0 * (jnp.arange(n, dtype=jnp.float32) + 1.0) / n)

def split_heads(t, n):
    b, s, _ = t.shape
    return t.reshape(b, s, n, HEAD_DIM).transpose(0, 2, 1, 3)

def merge_heads(t):
    b, h, s, d = t.shape
    return t.transpose(0, 2, 1, 3).reshape(b, s, h * d)

def neighbourhood_attention(q, k, v, rpb):
    b, h, s, hd = q.shape
    rows = s // GRID_W
    kr = min(NA_ROWS_MAX, rows)
    qg = q.reshape(b, h, rows, GRID_W, hd)
    kg = k.reshape(b, h, rows, GRID_W, hd)
    vg = v.reshape(b, h, rows, GRID_W, hd)
    r = jnp.arange(rows)
    row_start = jnp.clip(r - kr // 2, 0, rows - kr)
    row_idx = row_start[:, None] + jnp.arange(kr)[None, :]
    kb = kg[:, :, row_idx]
    vb = vg[:, :, row_idx]
    sc = jnp.einsum("bhrqd,bhrkcd->bhrqkc", qg, kb).astype(jnp.float32) * (hd ** -0.5)
    c = jnp.arange(GRID_W)
    col_start = jnp.clip(c - NA_COLS // 2, 0, GRID_W - NA_COLS)
    col_valid = (c[None, :] >= col_start[:, None]) & (c[None, :] < col_start[:, None] + NA_COLS)
    col_idx = jnp.clip(c[None, :] - c[:, None] + NA_COLS - 1, 0, 2 * NA_COLS - 2)
    row_off = row_idx - r[:, None]
    bias = rpb[:, row_off + NA_ROWS_MAX - 1]
    bias = bias[..., col_idx].transpose(0, 1, 3, 2, 4)
    sc = jnp.where(col_valid[:, None, :], sc + bias.astype(jnp.float32), NEG_INF)
    p = jax.nn.softmax(sc.reshape(b, h, rows, GRID_W, kr * GRID_W), axis=-1)
    p = p.reshape(b, h, rows, GRID_W, kr, GRID_W).astype(v.dtype)
    o = jnp.einsum("bhrqkc,bhrkcd->bhrqd", p, vb)
    return o.reshape(b, h, s, hd)

def banded_attention(q, k, v, half_w, slopes, dilation, sink=None):
    b, g, rq, L, hd = q.shape
    bq = math.gcd(L, ATTN_BLOCK)
    nb = L // bq
    kw = bq + 2 * half_w
    pad = ((0, 0), (0, 0), (half_w, half_w), (0, 0))
    kp = jnp.pad(k, pad)
    vp = jnp.pad(v, pad)
    idx = jnp.arange(nb)[:, None] * bq + jnp.arange(kw)[None, :]
    kb = kp[:, :, idx]
    vb = vp[:, :, idx]
    qb = q.reshape(b, g, rq, nb, bq, hd)
    sc = jnp.einsum("bgrnqd,bgnkd->bgrnqk", qb, kb).astype(jnp.float32) * (hd ** -0.5)
    qpos = jnp.arange(nb)[:, None] * bq + jnp.arange(bq)[None, :]
    kpos = (idx - half_w)[:, None, :]
    dist = jnp.abs(kpos - qpos[:, :, None])
    valid = (dist <= half_w) & (kpos >= 0) & (kpos < L)
    bias = -slopes.astype(jnp.float32)[:, :, None, None, None] * (dist * dilation).astype(jnp.float32)
    sc = jnp.where(valid, sc + bias, NEG_INF)
    m = jnp.max(sc, axis=-1, keepdims=True)
    if sink is not None:
        sink_f = sink.astype(jnp.float32)[:, :, None, None, None]
        m = jnp.maximum(m, sink_f)
    p = jnp.exp(sc - m)
    den = jnp.sum(p, axis=-1, keepdims=True)
    if sink is not None:
        den = den + jnp.exp(sink_f - m)
    o = jnp.einsum("bgrnqk,bgnkd->bgrnqd", p.astype(v.dtype), vb).astype(jnp.float32) / den
    lse = (m + jnp.log(den))[..., 0]
    return o.astype(v.dtype).reshape(b, g, rq, L, hd), lse.reshape(b, g, rq, L)

def dilated_attention(q, k, v, slopes):
    b, h, s, hd = q.shape
    outs, lses = [], []
    for window, d in DIL_BRANCHES:
        L = s // d

        def to_sub(t):
            return t.reshape(b, h, L, d, hd).transpose(0, 3, 1, 2, 4).reshape(b * d, h, L, hd)

        o, lse = banded_attention(to_sub(q)[:, :, None], to_sub(k), to_sub(v),
                                  window // (2 * d), slopes[:, None], d)
        outs.append(o[:, :, 0].reshape(b, d, h, L, hd).transpose(0, 2, 3, 1, 4).reshape(b, h, s, hd))
        lses.append(lse[:, :, 0].reshape(b, d, h, L).transpose(0, 2, 3, 1).reshape(b, h, s))
    w = jax.nn.softmax(jnp.stack(lses), axis=0)
    o = jnp.einsum("nbhs,nbhsd->bhsd", w, jnp.stack(outs).astype(jnp.float32))
    return o.astype(q.dtype)

def hybrid_mixer(h, w_in, qk_gain, rpb, sink, out_gain, w_out):
    sizes = (NA_W, NA_W, NA_W, SWA_QW, SWA_KVW, SWA_KVW, DIL_W, DIL_W, DIL_W)
    cuts = [int(c) for c in np.cumsum(sizes)[:-1]]
    proj = h @ w_in
    qa, ka, va, qb, kb, vb, qc, kc, vc = jnp.split(proj, cuts, axis=-1)
    b, s, _ = h.shape
    slopes = alibi_slopes(SWA_Q_HEADS + DIL_HEADS)
    oa = neighbourhood_attention(rms_norm(split_heads(qa, NA_HEADS), qk_gain[0, 0]),
                                 rms_norm(split_heads(ka, NA_HEADS), qk_gain[0, 1]),
                                 split_heads(va, NA_HEADS), rpb)
    qbh = rms_norm(split_heads(qb, SWA_Q_HEADS), qk_gain[1, 0]).reshape(b, SWA_KV_HEADS, SWA_GROUP, s, HEAD_DIM)
    kbh = rms_norm(split_heads(kb, SWA_KV_HEADS), qk_gain[1, 1])
    ob, _ = banded_attention(qbh, kbh, split_heads(vb, SWA_KV_HEADS), SWA_HALF_WINDOW,
                             slopes[:SWA_Q_HEADS].reshape(SWA_KV_HEADS, SWA_GROUP), 1,
                             sink.reshape(SWA_KV_HEADS, SWA_GROUP))
    ob = ob.reshape(b, SWA_Q_HEADS, s, HEAD_DIM)
    oc = dilated_attention(rms_norm(split_heads(qc, DIL_HEADS), qk_gain[2, 0]),
                           rms_norm(split_heads(kc, DIL_HEADS), qk_gain[2, 1]),
                           split_heads(vc, DIL_HEADS), slopes[SWA_Q_HEADS:])
    ga, gb, gc = jnp.split(out_gain, [NA_W, NA_W + SWA_QW])
    y = jnp.concatenate([rms_norm(merge_heads(oa), ga),
                         rms_norm(merge_heads(ob), gb),
                         rms_norm(merge_heads(oc), gc)], axis=-1)
    return y @ w_out

def swiglu(h, w_gu, w_down):
    gu = h @ w_gu
    gate, up = jnp.split(gu, 2, axis=-1)
    return (jax.nn.silu(gate) * up) @ w_down

def setup_inputs(seed: int = 0) -> dict:
    key = jax.random.key(seed)
    ks = jax.random.split(key, 12)
    f32 = jnp.float32
    x = jax.random.normal(ks[0], (BATCH, SEQ, D_MODEL), f32)
    attn_norm = 1.0 + 0.05 * jax.random.normal(ks[1], (DEPTH, D_MODEL), f32)
    w_in = jax.random.normal(ks[2], (DEPTH, D_MODEL, IN_W), f32) * D_MODEL ** -0.5
    qk_gain = 1.0 + 0.05 * jax.random.normal(ks[3], (DEPTH, 3, 2, HEAD_DIM), f32)
    rpb = 0.1 * jax.random.normal(ks[4], (DEPTH, NA_HEADS, 2 * NA_ROWS_MAX - 1, 2 * NA_COLS - 1), f32)
    sink = 0.5 * jax.random.normal(ks[5], (DEPTH, SWA_Q_HEADS), f32)
    out_gain = 1.0 + 0.05 * jax.random.normal(ks[6], (DEPTH, MIX_W), f32)
    w_out = jax.random.normal(ks[7], (DEPTH, MIX_W, D_MODEL), f32) * MIX_W ** -0.5
    ffn_norm = 1.0 + 0.05 * jax.random.normal(ks[8], (DEPTH, D_MODEL), f32)
    w_gu = jax.random.normal(ks[9], (DEPTH, D_MODEL, 2 * FFN_HIDDEN), f32) * D_MODEL ** -0.5
    w_down = jax.random.normal(ks[10], (DEPTH, FFN_HIDDEN, D_MODEL), f32) * FFN_HIDDEN ** -0.5
    return {"x": x, "attn_norm": attn_norm, "w_in": w_in, "qk_gain": qk_gain, "rpb": rpb,
            "sink": sink, "out_gain": out_gain, "w_out": w_out, "ffn_norm": ffn_norm,
            "w_gu": w_gu, "w_down": w_down}

def reference(x, attn_norm, w_in, qk_gain, rpb, sink, out_gain, w_out, ffn_norm, w_gu, w_down):
    for l in range(DEPTH):
        h = rms_norm(x, attn_norm[l])
        x = x + hybrid_mixer(h, w_in[l], qk_gain[l], rpb[l], sink[l], out_gain[l], w_out[l])
        h = rms_norm(x, ffn_norm[l])
        x = x + swiglu(h, w_gu[l], w_down[l])
    return x


_drawn_inputs = setup_inputs


def setup_inputs(seed=0):
    import zlib

    import numpy as np

    out = dict(_drawn_inputs(seed))
    spreads = {}
    factors = {}
    for name, (base, spread) in spreads.items():
        noise = np.random.default_rng([zlib.crc32(name.encode()), seed]).standard_normal(out[name].shape)
        drawn = base * np.exp(spread * noise) if base else spread * noise
        out[name] = __import__('jax').numpy.asarray(drawn.astype(out[name].dtype))
    for name, factor in factors.items():
        out[name] = (out[name] * factor).astype(out[name].dtype)
    return out
```

```python
from contextlib import ExitStack

import concourse.bass as bass
from concourse import mybir

F32, F32R = mybir.dt.float32, mybir.dt.float32r
ALU = mybir.AluOpType
ACT = mybir.ActivationFunctionType
P = 128


def build_program(nc, x, attn_norm, w_in, qk_gain, rpb, sink, out_gain, w_out, ffn_norm, w_gu, w_down, out):
    depth, D = attn_norm.shape
    S = x.shape[1]
    MT = S // P
    KD = D // P
    IN_W, HID = w_in.shape[2], w_down.shape[1]
    HD = 64
    V1 = HD + 1
    A_H, B_H, C_H = 4, 6, 6
    GW = 64
    EPS = 1e-6
    BIG, BIGD = 1e30, 1e34
    SLOPES = [2.0 ** (-8.0 * (i + 1) / (B_H + C_H)) for i in range(B_H + C_H)]
    B_ORDER = [0, 3, 1, 4, 2, 5]
    AQ, AV, BQ, BV, CQ, CV = 0, 512, 768, 1280, 1408, 2176
    T_AQ, T_AK, T_BQ, T_BK, T_CQ, T_CK = 0, 2, 4, 7, 8, 11
    QT = 14
    Y_TILE = [0, 1, 4, 5, 6, 8, 9, 10]
    NCH = HID // P
    NG = NCH // 2
    GR = 6 * V1 + 6
    TA_S = 23

    xr = x.rearrange("b (m p) d -> p (b m) d", p=P)
    outr = out.rearrange("b (m p) d -> p (b m) d", p=P)
    dram = lambda n, s: nc.dram_tensor(n, s, F32, kind="Internal").ap()
    x_res = dram("x_res", (S, D)).rearrange("(m p) d -> p m d", p=P)
    v_c = dram("v_c", (S, C_H * V1))
    g_dil = [dram("g_d4", (S, GR)), dram("g_d16", (S, GR))]
    t_a = dram("t_a", (depth, P, A_H * TA_S * GW))
    t_b = dram("t_b", (P, B_H * 384))
    t_c = dram("t_c", (P, C_H * (128 + 256 + 256)))

    ctx = ExitStack()
    with ctx:
        base = -(-nc.sbuf_base // 64) * 64
        place = {}
        for name, size in (("CONST", 4096), ("H", 65536), ("R", 24576), ("U", 24576),
                           ("X", 32768), ("F", 57344), ("W", 10240), ("Q", 8192)):
            place[name] = base
            base += size
        at = dict(place)

        def sb(name, shape, dt, region, offset=None):
            if offset is None:
                offset = at[region] - place[region]
                n = 4
                for d in shape[1:]:
                    n *= d
                at[region] += -(-n // 32) * 32
            return nc.alloc_sbuf_tensor_at(name, shape, dt, offset=place[region] + offset)

        ident = sb("ident", [P, P], F32, "CONST")
        bones = sb("bones", [P, P], F32, "CONST")
        g_attn = sb("g_attn", [P, depth * KD], F32, "CONST")
        g_ffn = sb("g_ffn", [P, depth * KD], F32, "CONST")
        g_out = sb("g_out", [P, depth * KD], F32, "CONST")
        g_raw = sb("g_raw", [P, depth * 6], F32, "CONST")
        g_qk = sb("g_qk", [P, depth * QT], F32, "CONST")
        eps = sb("eps", [P, 1], F32, "CONST")
        neghalf = sb("neghalf", [P, 1], F32, "CONST")
        col_mask = sb("col_mask", [P, GW], F32, "CONST")
        sinks = sb("sinks", [P, depth * B_H], F32, "CONST")
        nsink = sb("nsink", [P, depth * B_H], F32, "CONST")
        sumsq = sb("sumsq", [P, MT], F32, "CONST")
        rms = sb("rms", [P, MT], F32, "CONST")
        rstd = sb("rstd", [P, MT], F32, "CONST")
        nmin = sb("nmin", [P, 6], F32, "CONST")
        shift_b = sb("shift_b", [P, 2, 6], F32, "CONST")
        shift_c = sb("shift_c", [P, 3, 6], F32, "CONST")
        fac_b = sb("fac_b", [P, 2, 6], F32, "CONST")
        fac_c = sb("fac_c", [P, 3, 6], F32, "CONST")
        den = sb("den", [P, 3, 6], F32, "CONST")
        coef = sb("coef", [P, 3, 6], F32, "CONST")
        gvar = sb("gvar", [P, 3], F32, "CONST")
        gvare = sb("gvare", [P, 3], F32, "CONST")
        grstd = sb("grstd", [P, 3], F32, "CONST")

        HH = sb("HH", [P, KD, S], F32R, "H", 0)
        HL = sb("HL", [P, KD, S], F32R, "H", 32768)
        TA = sb("TA", [P, A_H, TA_S, GW], F32, "H")
        TB = sb("TB", [P, B_H, 384], F32, "H")
        VC = sb("VC", [P, MT + 1, C_H, V1], F32, "H")
        KS = sb("KS", [P, 2, 3, 192], F32, "H")
        PT = sb("PT", [P, 2, 640], F32, "H")
        junk = sb("junk", [P, 384], F32, "H")
        TA1 = sb("TA1", [P, A_H, TA_S, GW], F32, "H", 32768)
        RAW0 = sb("RAW0", [P, A_H, TA_S, GW], F32, "F", 32768)
        RAW1 = sb("RAW1", [P, A_H, TA_S, GW], F32, "R", 0)
        PR = sb("PR", [P, 4, 512], F32, "R")
        PH = sb("PH", [P, 4, 512], F32R, "R")
        PL = sb("PL", [P, 4, 512], F32R, "R")
        UR = sb("UR", [P, 2, KD, P], F32, "U")
        UH = sb("UH", [P, 2, KD, P], F32R, "U")
        UL = sb("UL", [P, 2, KD, P], F32R, "U")
        TC3 = sb("TC3", [P, C_H, 128], F32, "U", 8192)
        TC2 = sb("TC2", [P, C_H, 256], F32, "U", 8192 + 3072)
        TC1 = sb("TC1", [P, C_H, 256], F32, "U", 8192 + 3072 + 6144)
        X = sb("X", [P, MT, D], F32, "X", 0)
        VA = sb("VA", [P, MT, A_H, V1], F32, "X")
        VB = sb("VB", [P, MT, 2, V1], F32, "X")
        VR = sb("VR", [P, 2, 2, C_H * V1], F32, "X")
        GB = sb("GB", [P, GR], F32, "X")
        GC = sb("GC", [P, 3, GR], F32, "X")
        GA = sb("GA", [P, GR], F32, "X")
        Y = sb("Y", [P, D], F32, "X")
        QK = sb("QK", [P, QT, S], F32, "F", 0)
        VS = sb("VS", [P, MT, C_H, V1], F32, "F", 40960)
        XN = sb("XN", [P, MT, D], F32, "F", 24576)
        GH = sb("GH", [P, 2, 2, S], F32R, "F", 0)
        GL = sb("GL", [P, 2, 2, S], F32R, "F", 16384)
        D_B = sb("D_B", [P, 384], F32, "F", 0)
        D_N = sb("D_N", [P, 384], F32, "F", 2048)
        D_C = sb("D_C", [P, 256], F32, "F", 4096)
        D_C3 = sb("D_C3", [P, 128], F32, "F", 6144)
        TBs = sb("TBs", [P, B_H, 384], F32, "F", 8192)
        TCs = sb("TCs", [P, C_H * 640], F32, "F", 8192 + 9216)
        SQ = sb("SQ", [P, 2, 512], F32, "W", 0)
        RM = sb("RM", [P, 2, 512], F32, "W", 4096)
        SI = sb("SI", [P, 2, 512], F32, "W", 0)
        GT = sb("GT", [P, 2, 512], F32, "W", 4096)
        T = sb("T", [P, 4, 640], F32, "W", 0)
        QS = sb("QS", [P, 16, P], F32, "Q")

        psum = ctx.enter_context(nc.psum_tensor("psum", [P, 8 * 512], F32))
        bank = [psum[:, 512 * i:512 * i + 512] for i in range(8)]
        score2 = [psum[:, 1024 * i:1024 * i + 1024] for i in range(2)]

        with ExitStack() as setup:
            sem = lambda n: setup.enter_context(nc.semaphore(n))
            x_in, gains_in, rpb_in, tabs_out = sem("x_in"), sem("gains_in"), sem("rpb_in"), sem("tabs_out")
            pool_seq, dve_seq = sem("pool_seq"), sem("dve_seq")
            tab_done = sem("tab_done")
            block = setup.enter_context(nc.Block())
            MASK_AT, DIST_AT = [], []

            @block.sync
            def _(sp):
                sp.dma_start(X[:, :, :], xr).then_inc(x_in, 16)
                for l, raw in ((0, RAW0), (1, RAW1)):
                    for h in range(A_H):
                        for half in range(2):
                            lo = 64 * half
                            for s0, n, dr in ((0, 14, 1 - half), (14, 9, 3 - half)):
                                src = bass.AP(rpb.tensor, ((l * A_H + h) * 15 + dr) * 127,
                                              [[1, GW], [127, n], [1, GW]])
                                sp.dma_start(raw[lo:lo + 64, h, s0:s0 + n, :], src).then_inc(rpb_in, 16)
                sp.wait_ge(tab_done, 3)
                sp.dma_start(t_b, TBs[:, :, :].rearrange("p h j -> p (h j)")).then_inc(tabs_out, 16)
                sp.dma_start(t_c, TCs[:, :]).then_inc(tabs_out, 16)
                for l, ta in ((0, TA), (1, TA1)):
                    sp.dma_start(t_a[l], ta[:, :, :, :].rearrange("p h s c -> p (h s c)")).then_inc(tabs_out, 16)
                sp.wait_ge(tabs_out, 64)
                sp.wait_ge(x_in, 16)

            @block.scalar
            def _(act):
                with nc.allow_non_contiguous_dma(reason="gain vectors, a few KB"):
                    act.dma_start(g_attn[:, :].rearrange("p (l k) -> p l k", l=depth),
                                  attn_norm.rearrange("l (k p) -> p l k", p=P)).then_inc(gains_in, 16)
                    act.dma_start(g_ffn[:, :].rearrange("p (l k) -> p l k", l=depth),
                                  ffn_norm.rearrange("l (k p) -> p l k", p=P)).then_inc(gains_in, 16)
                    act.dma_start(g_out[:, :].rearrange("p (l k) -> p l k", l=depth),
                                  out_gain.rearrange("l (k p) -> p l k", p=P)).then_inc(gains_in, 16)
                    for half in range(2):
                        act.dma_start(g_raw[64 * half:64 * half + 64, :],
                                      qk_gain.rearrange("l f q d -> d (l f q)")).then_inc(gains_in, 16)
                    act.dma_start(sinks[:, :], sink.rearrange("l h -> (l h)").partition_broadcast(P)).then_inc(gains_in, 16)
                act.wait_ge(gains_in, 96)

            @block.gpsimd
            def _(pool):
                count = [0]

                def step(ins):
                    count[0] += 1
                    ins.then_inc(pool_seq, 1)
                    pool.wait_ge(pool_seq, count[0])

                g = nc.gpsimd
                step(g.memset(QS[:, :, :], 0.0))
                step(g.memset(ident[:, :], 0.0))
                step(g.affine_select(out=ident[:, :], in_=ident[:, :], compare_op=ALU.not_equal, fill=1.0,
                                     base=0, pattern=[[-1, P]], channel_multiplier=1))
                step(g.memset(bones[:, :], 0.0))
                step(g.memset(bones[0:64, 0:64], 1.0))
                step(g.memset(bones[64:128, 64:128], 1.0))
                step(g.memset(eps[:, :], EPS))
                step(g.memset(neghalf[:, :], -0.5))
                step(g.memset(col_mask[:, :], 0.0))
                for half in range(2):
                    low, high = col_mask[64 * half:64 * half + 64, 0:48], col_mask[64 * half:64 * half + 64, 16:64]
                    step(g.affine_select(out=low, in_=low, compare_op=ALU.is_ge, fill=BIG, base=8,
                                         pattern=[[1, 48]], channel_multiplier=-1))
                    step(g.affine_select(out=high, in_=high, compare_op=ALU.is_ge, fill=BIG, base=-9,
                                         pattern=[[-1, 48]], channel_multiplier=1))
                MASK_AT.append(count[0])
                for dist, w, hw in ((D_B, 384, 128), (D_C, 256, 64), (D_C3, 128, 0)):
                    step(g.iota(dist[:, :], pattern=[[1, w]], base=-hw, channel_multiplier=-1,
                                allow_small_or_imprecise_dtypes=True))
                    step(g.tensor_scalar(D_N[:, 0:w], dist[:, :], -1.0, None, ALU.mult))
                    step(g.affine_select(out=dist[:, :], in_=dist[:, :], compare_op=ALU.is_ge, fill=0.0,
                                         base=-hw, pattern=[[1, w]], channel_multiplier=-1))
                    step(g.affine_select(out=D_N[:, 0:w], in_=D_N[:, 0:w], compare_op=ALU.is_ge, fill=0.0,
                                         base=hw, pattern=[[-1, w]], channel_multiplier=1))
                    step(g.tensor_tensor(dist[:, :], dist[:, :], D_N[:, 0:w], ALU.add))
                    if hw:
                        step(g.affine_select(out=dist[:, :], in_=dist[:, :], compare_op=ALU.is_ge, fill=BIGD,
                                             base=0, pattern=[[1, w]], channel_multiplier=-1))
                        step(g.affine_select(out=dist[:, :], in_=dist[:, :], compare_op=ALU.is_ge, fill=BIGD,
                                             base=2 * hw, pattern=[[-1, w]], channel_multiplier=1))
                step(g.memset(D_C3[0:64, 64:128], BIGD))
                step(g.memset(D_C3[64:128, 0:64], BIGD))
                DIST_AT.append(count[0])

            @block.vector
            def _(dve):
                v = nc.vector
                v.memset(T[:, :, :], 0.0)
                dve.wait_ge(gains_in, 96)
                v.tensor_scalar(nsink[:, :].rearrange("p (l a g) -> p l a g", l=depth, a=3),
                                sinks[:, :].rearrange("p (l g a) -> p l a g", l=depth, a=3), -1.0, None, ALU.mult)
                for l in range(depth):
                    for fam, q0, nq, nk in ((0, T_AQ, 2, 2), (1, T_BQ, 3, 1), (2, T_CQ, 3, 3)):
                        for i in range(nq + nk):
                            src = g_raw[:, l * 6 + fam * 2 + (i >= nq):l * 6 + fam * 2 + (i >= nq) + 1]
                            v.tensor_scalar(g_qk[:, l * QT + q0 + i:l * QT + q0 + i + 1], src,
                                            -(HD ** -0.5) if i < nq else 1.0, None, ALU.mult)
                dve.wait_ge(pool_seq, DIST_AT[0])
                for s in range(B_H):
                    v.tensor_scalar(TBs[:, s, :], D_B[:, :], SLOPES[B_ORDER[s]], None, ALU.mult)
                for h in range(C_H):
                    sl = SLOPES[B_H + h]
                    v.tensor_scalar(TCs[:, h * 128:h * 128 + 128], D_C3[:, :], 16 * sl, None, ALU.mult)
                    v.tensor_scalar(TCs[:, 768 + h * 256:768 + h * 256 + 256], D_C[:, :], 4 * sl, None, ALU.mult)
                    last = v.tensor_scalar(TCs[:, 2304 + h * 256:2304 + h * 256 + 256], D_C[:, :], sl, None, ALU.mult)
                last.then_inc(tab_done, 1)
                dve.wait_ge(rpb_in, 16 * 2 * A_H * 2 * 2)
                for n, (ta, raw) in enumerate(((TA, RAW0), (TA1, RAW1))):
                    v.tensor_tensor(ta[:, :, :, :].rearrange("p h s c -> p (h s) c"),
                                    col_mask[:, :].unsqueeze(1).broadcast_to([P, A_H * TA_S, GW]),
                                    raw[:, :, :, :].rearrange("p h s c -> p (h s) c")[:, :, ::-1],
                                    ALU.subtract).then_inc(dve_seq, 1)
                    dve.wait_ge(dve_seq, n + 1)
                    v.memset(ta[0:64, :, 22, :], BIG)
                    v.memset(ta[64:128, :, 14, :], BIG).then_inc(tab_done, 1)

        with nc.Fori(0, depth) as l, ExitStack() as layer:
            sems = []

            def sem(name):
                sems.append(layer.enter_context(nc.semaphore(name)))
                return sems[-1]

            x_stored, x_back = sem("x_stored"), sem("x_back")
            piece_raw = [sem(f"piece_raw{i}") for i in range(4)]
            unit_raw = [sem(f"unit_raw{i}") for i in range(2)]
            piece_hi, piece_lo, unit_hi, unit_lo = sem("piece_hi"), sem("piece_lo"), sem("unit_hi"), sem("unit_lo")
            moved = sem("moved")
            stat = sem("stat")
            sumsq_s, rms_s, rstd_s, xn_s = sem("sumsq_s"), sem("rms_s"), sem("rstd_s"), sem("xn_s")
            xt_s, h_hi, h_lo = sem("xt_s"), sem("h_hi"), sem("h_lo")
            v_stored, v_ones, vs_out = sem("v_stored"), sem("v_ones"), sem("vs_out")
            sq_s, ss_s, rmsq_s, rec_s, qk_s = sem("sq_s"), sem("ss_s"), sem("rmsq_s"), sem("rec_s"), sem("qk_s")
            x_add = sem("x_add")
            silu_s, mul_s, g_hi, g_lo = sem("silu_s"), sem("mul_s"), sem("g_hi"), sem("g_lo")
            tab_c3, tab_c, tab_ab, vc_in = sem("tab_c3"), sem("tab_c"), sem("tab_ab"), sem("vc_in")
            vr_in = [sem(f"vr_in{i}") for i in range(2)]
            g_out_s = [sem(f"g_out{i}") for i in range(2)]
            g_back = sem("g_back")
            staged, scored, tmin_s, exp_s = sem("staged"), sem("scored"), sem("tmin_s"), sem("exp_s")
            pt_made, pt_copied, pv_s, grp_s = sem("pt_made"), sem("pt_copied"), sem("pv_s"), sem("grp_s")
            b_shift, b_fac, c_shift, c_fac, c_merged = (sem(n) for n in ("b_shift", "b_fac", "c_shift", "c_fac", "c_merged"))
            gvar_s, grstd_s, y_s = ([sem(f"{n}_{f}") for f in "abc"] for n in ("gvar_s", "grstd_s", "y_s"))
            dve_seq = sem("dve_seq")
            dve_gate, pool_gate = sem("dve_gate"), sem("pool_gate")

            def needed(value):
                return not isinstance(value, int) or value > 0

            def loop(eng, n0, n1):
                return eng.Fori(n0, n1)

            programs = ExitStack()
            block = programs.enter_context(nc.Block())

            def raw_need(p):
                extra = p // 4 - 1
                if isinstance(p, int):
                    extra = max(0, min(2, extra))
                    return 16 * (p // 4 + 1) + 16 * extra
                raise ValueError

            def piece_done(p):
                if p < 0:
                    return 0
                if p < 32:
                    ch, k = p // 8, p % 8
                    return 15 * ch + (k + 1 if k < 7 else 15)
                g, c = (p - 32) // 4, (p - 32) % 4 // 2
                return 60 + 16 * g + 8 * c + 8

            def hi_piece(act, p, n=512):
                act.wait_ge(piece_raw[p % 4], raw_need(p))
                if needed(piece_done(p - 4)):
                    act.wait_ge(moved, piece_done(p - 4))
                nc.scalar.activation(PH[:, p % 4, 0:n], PR[:, p % 4, 0:n], ACT.Copy).then_inc(piece_hi, 1)

            def lo_piece(dve, p, n=512):
                dve.wait_ge(piece_hi, p + 1)
                nc.vector.tensor_tensor(PL[:, p % 4, 0:n], PR[:, p % 4, 0:n], PH[:, p % 4, 0:n].bitcast(F32),
                                        ALU.subtract).then_inc(piece_lo, 1)

            def hi_unit(act, u, slot):
                act.wait_ge(unit_raw[slot], (u - slot) * 16 + 32)
                if needed(2 * u - 2):
                    act.wait_ge(stat, 2 * u - 2)
                nc.scalar.activation(UH[:, slot, :, :], UR[:, slot, :, :], ACT.Copy).then_inc(unit_hi, 1)

            def lo_unit(dve, u, slot):
                dve.wait_ge(unit_hi, u + 1)
                nc.vector.tensor_tensor(UL[:, slot, :, :], UR[:, slot, :, :], UH[:, slot, :, :].bitcast(F32),
                                        ALU.subtract).then_inc(unit_lo, 1)

            V_N = 384

            def body(kind, i, T0, U0, G0, Q0, b=None):
                return dict(kind=kind, i=i, T=T0, U=U0, G=G0, Q=Q0, b=b)

            def n_tiles(bd):
                return 12 if bd["kind"] in ("c3", "c2") else 16

            def chunks_of(bd, s):
                k = bd["kind"]
                if k == "c3":
                    return [(0, 128)]
                if k == "c2":
                    return [(0, 128), (128, 64 if s < 6 else 128)]
                if s < 6:
                    return [(0, 128), (128, 128)] + ([] if k in ("b0", "b7") else [(256, 128)])
                if s < 12:
                    return [(0, 128), (128, 64 if k == "b7" else 128)]
                return [(128 * c, 128) for c in range(4)] + ([(512, 64)] if k == "mid" else [])

            def units_of(bd, s):
                ch = chunks_of(bd, s)
                return [ch[0:4], ch[4:]] if len(ch) > 4 else [ch]

            def events(bd):
                ev = []
                for s in range(n_tiles(bd)):
                    for u in units_of(bd, s):
                        ev.append((s, "p", u))
                    if bd["kind"] in ("c3", "c2"):
                        continue
                    if s == 15:
                        ev += [(s, "y", ("b", 0, 2)), (s, "y", ("b", 2, 1))]
                    if bd["kind"] != "b0" and s == 5:
                        ev.append((s, "y", ("c", 0, 3)))
                    if bd["kind"] != "b0" and s == 6:
                        ev.append((s, "y", ("a", 0, 2)))
                return ev

            def last_unit(bd, s):
                return max(i for i, e in enumerate(events(bd)) if e[0] == s and e[1] == "p")

            plan = []
            t0 = u0 = g0 = q0 = 0
            for kind, rounds, b0 in (("c3", 3, 0), ("c3", 1, 3), ("c2", 3, 0), ("c2", 1, 3), ("b0", 1, 0),
                                     ("b1", 1, 1), ("mid", 4, 2), ("b6", 1, 6), ("b7", 1, 7)):
                bd = body(kind, b0, t0, u0, g0, q0)
                nt, nu = n_tiles(bd), len(events(bd))
                ng, nq = (2, 6) if kind in ("c3", "c2") else (3, 6)
                plan.append((bd, rounds, (nt, nu, ng, nq)))
                t0, u0, g0, q0 = t0 + rounds * nt, u0 + rounds * nu, g0 + rounds * ng, q0 + rounds * nq
            TILES, UNITS, GROUPS = t0, u0 + 2, g0
            C_GROUPS = 16

            def shifted(entry, r):
                bd, _, (nt, nu, ng, nq) = entry
                if isinstance(r, int) and r == 0:
                    return bd
                return dict(bd, i=bd["i"] + r, T=bd["T"] + r * nt, U=bd["U"] + r * nu, G=bd["G"] + r * ng,
                            Q=bd["Q"] + r * nq)

            def width(bd, s):
                k = bd["kind"]
                if k == "c3":
                    return 128, 0
                if k == "c2":
                    return 192, (0 if s < 6 else 64)
                if s < 6:
                    return (256 if k in ("b0", "b7") else 384), 0
                if s < 12:
                    return (192 if k in ("b0", "b7") else 256), (64 if k == "b0" else 0)
                return (576 if k == "mid" else 512), 0

            def a_row0(bd):
                k = bd["kind"]
                if k == "mid":
                    return 2 * bd["i"] - 4, 14
                row0 = 0 if k in ("b0", "b1") else MT * 2 - 8
                return row0, row0 - 2 * bd["i"] + 6

            def keys(bd, s):
                k, b, (w, _) = bd["kind"], bd["i"], width(bd, s)
                if k == "c3":
                    return [KS[:, s // 6, s % 6 // 2, 0:128]]
                if k == "c2":
                    return [KS[:, s // 6, s % 6 // 2, 0:192]]
                if s < 6:
                    return [QK[:, T_BK, bass.ds(0 if k == "b0" else b * P - P, w)]]
                if s < 12:
                    return [QK[:, T_CK + (s - 6) // 2, bass.ds(0 if k == "b0" else b * P - 64, w)]]
                t0 = a_row0(bd)[0] * GW
                return [QK[:, T_AK + (s - 12) // 2, bass.ds(t0 + j, min(512, w - j))] for j in range(0, w, 512)]

            def table(bd, s):
                k, (w, _) = bd["kind"], width(bd, s)
                if k == "c3":
                    return TC3[:, s % 6, :]
                if k == "c2":
                    return TC2[:, s % 6, 64:256] if s < 6 else TC2[:, s % 6, 0:192]
                if s < 6:
                    j0 = 128 if k == "b0" else 0
                    return TB[:, s, j0:j0 + w]
                if s < 12:
                    j0 = 64 if k == "b0" else 0
                    return TC1[:, s - 6, j0:j0 + w]
                s0 = a_row0(bd)[1]
                return TA[:, s - 12, s0:s0 + w // GW, :].rearrange("p s c -> p (s c)")

            def group_buf(bd, s):
                if bd["kind"] in ("c3", "c2"):
                    return GC[:, s // 6, :], s % 6
                return (GB[:, :], s) if s < 6 else (GC[:, 0, :], s - 6) if s < 12 else (GA[:, :], s - 12)

            def group_bank(bd, s):
                if bd["kind"] in ("c3", "c2"):
                    return bank[6 + s // 6]
                return bank[7] if 6 <= s < 12 else bank[6]

            def values(bd, s, c, n):
                k, b = bd["kind"], bd["i"]
                if k in ("c3", "c2"):
                    return VR[0:n, s // 6, c, (s % 6) * V1:(s % 6 + 1) * V1]
                if s < 6:
                    return VB[0:n, bass.ds((0 if k == "b0" else b - 1) + c, 1), s % 2, :].rearrange("p a d -> p (a d)")
                if s < 12:
                    return VC[0:n, bass.ds(b + c, 1), s - 6, :].rearrange("p a d -> p (a d)")
                t0 = b - 2 if k == "mid" else a_row0(bd)[0] // 2
                return VA[0:n, bass.ds(t0 + c, 1), s - 12, :].rearrange("p a d -> p (a d)")

            FAM = {"a": (0, 2, 0), "b": (2, 3, 1), "c": (5, 3, 2)}

            @block.sync
            def _(sp):
                def piece(p, parts):
                    if needed(p - 3):
                        sp.wait_ge(piece_lo, p - 3)
                    for dst, src in parts:
                        sp.dma_start(PR[:, p % 4, dst[0]:dst[1]], src).then_inc(piece_raw[p % 4], 16)

                def unit(u, slot, parts):
                    if needed(u - 1):
                        sp.wait_ge(unit_lo, u - 1)
                    for dst, src in parts:
                        sp.dma_start(dst, src).then_inc(unit_raw[slot], 16)

                def halves(slot, src):
                    return [(UR[:, slot, 4 * i:4 * i + 4, :], src[:, 4 * i:4 * i + 4, :]) for i in range(2)]

                wi = w_in[bass.ds(l, 1)].rearrange("a (k p) n -> p (a k) n", p=P)
                wo = w_out[bass.ds(l, 1)].rearrange("a (k p) n -> p (a k) n", p=P)
                wg = w_gu[bass.ds(l, 1)].rearrange("a (k p) n -> p (a k) n", p=P)
                wd = w_down[bass.ds(l, 1)].rearrange("a (k p) n -> p (a k) n", p=P)
                for k in range(8):
                    if k == 4:
                        sp.dma_start(x_res, X[:, :, :]).then_inc(x_stored, 16)
                    piece(k, [((0, 384), wi[:, k, CV:CV + 384])])
                for k in range(8):
                    piece(8 + k, [((0, 256), wi[:, k, AV:AV + 256]), ((256, 384), wi[:, k, BV:BV + 128])])

                def qk_unit(t):
                    if T_BQ <= t < T_BK:
                        a = t - T_BQ
                        unit(t, t % 2, [(UR[:, t % 2, :, 64 * g:64 * g + 64],
                                         wi[:, :, BQ + (3 * g + a) * 64:BQ + (3 * g + a) * 64 + 64]) for g in range(2)])
                    else:
                        col = AQ + t * P if t < T_BQ else BQ + 384 if t == T_BK else CQ + (t - T_CQ) * P
                        unit(t, t % 2, halves(t % 2, wi[:, :, col:col + P]))

                qk_unit(0)
                qk_unit(1)
                sp.wait_ge(v_stored, 8)
                sp.wait_ge(v_ones, 1)
                sp.dma_start(v_c.rearrange("(m p) c -> p m c", p=P),
                             VS[:, :, :, :].rearrange("p m h d -> p m (h d)")).then_inc(vs_out, 16)
                for t in range(2, QT):
                    qk_unit(t)
                for k in range(4):
                    piece(16 + k, [((0, 512), wo[:, k, 0:512])])
                for u in range(2):
                    unit(QT + u, u, halves(u, wg[:, :, u * HID:u * HID + P]))
                sp.wait_ge(stat, 2 * QT)
                sp.dma_start(TC3[:, :, :].rearrange("p h j -> p (h j)"), t_c[:, 0:768]).then_inc(tab_c3, 16)
                sp.wait_ge(vs_out, 16)

                def load_values(gi):
                    slot = gi % 2
                    if needed(6 * (gi - 1)):
                        sp.wait_ge(pv_s, 6 * (gi - 1))
                    if gi < 8:
                        v16 = v_c.rearrange("(j r) c -> r j c", r=16)
                        for rr in range(2):
                            sp.dma_start(VR[64 * rr:64 * rr + 64, slot, 0, :], v16[2 * gi + rr]).then_inc(vr_in[slot], 16)
                    else:
                        v4 = v_c.rearrange("(t p r) c -> r p t c", p=P, r=4)
                        sp.dma_start(VR[:, slot, :, :], v4[(gi - 8) // 2]).then_inc(vr_in[slot], 16)

                def store_group(gi):
                    sp.wait_ge(grp_s, gi + 1)
                    slot = gi % 2
                    if gi < 8:
                        g16 = g_dil[1].rearrange("(j r) c -> r j c", r=16)
                        for rr in range(2):
                            sp.dma_start(g16[2 * gi + rr], GC[64 * rr:64 * rr + 64, slot, :]).then_inc(g_out_s[slot], 16)
                    else:
                        g4 = g_dil[0].rearrange("(t p r) c -> r t p c", p=P, r=4)
                        sp.dma_start(g4[(gi - 8) // 2, slot], GC[:, slot, :]).then_inc(g_out_s[slot], 16)

                load_values(0)
                load_values(1)
                sp.dma_start(TC2[:, :, :].rearrange("p h j -> p (h j)"), t_c[:, 768:2304]).then_inc(tab_c, 16)
                sp.dma_start(TC1[:, :, :].rearrange("p h j -> p (h j)"), t_c[:, 2304:3840]).then_inc(tab_c, 16)
                sp.dma_start(TB[:, :, :].rearrange("p h j -> p (h j)"), t_b).then_inc(tab_ab, 16)
                vsh = v_c[64:S - 64, :].rearrange("(m p) c -> p m c", p=P)
                sp.dma_start(VC[:, 1:MT, :, :].rearrange("p m h d -> p m (h d)"), vsh).then_inc(vc_in, 16)
                sp.dma_start(VC[64:128, 0, :, :].rearrange("p h d -> p (h d)"), v_c[0:64, :]).then_inc(vc_in, 16)
                sp.dma_start(VC[0:64, MT, :, :].rearrange("p h d -> p (h d)"), v_c[S - 64:S, :]).then_inc(vc_in, 16)
                sp.dma_start(TA[:, :, :, :].rearrange("p h s c -> p (h s c)"),
                             t_a[bass.ds(l, 1)].rearrange("a p n -> (a p) n")).then_inc(tab_ab, 16)
                for gi in range(C_GROUPS):
                    store_group(gi)
                    if gi + 2 < C_GROUPS:
                        load_values(gi + 2)
                for slot in range(2):
                    sp.wait_ge(g_out_s[slot], 16 * 12)
                for b in range(MT):
                    if needed(b):
                        sp.wait_ge(c_merged, b)
                    for n in range(2):
                        sp.dma_start(GC[:, 1 + n, :], g_dil[n][b * P:b * P + P, :]).then_inc(g_back, 16)
                sp.wait_ge(pt_copied, UNITS)
                sp.dma_start(X[:, :, :], x_res).then_inc(x_back, 16)
                for p in range(20, 32):
                    piece(p, [((0, 512), wo[:, p % 8, 512 * (p // 8 - 2):512 * (p // 8 - 1)])])

                def down_pieces(g):
                    for i in range(4):
                        sp.wait_ge(piece_lo, 32 + 4 * g + i - 3)
                        sp.dma_start(PR[:, i, :], wd[:, bass.ds(2 * g + i % 2, 1), 512 * (i // 2):512 * (i // 2) + 512]
                                     .rearrange("p a n -> p (a n)")).then_inc(piece_raw[i], 16)

                def gu_units(j):
                    for u in range(2):
                        sp.wait_ge(unit_lo, QT + 2 * j + u - 1)
                        for i in range(2):
                            sp.dma_start(UR[:, u, 4 * i:4 * i + 4, :],
                                         wg[:, 4 * i:4 * i + 4, bass.ds(j * P + u * HID, P)]).then_inc(unit_raw[u], 16)

                gu_units(1)
                down_pieces(0)
                with loop(sp, 0, NG // 2) as i:
                    gu_units(4 * i + 2)
                    gu_units(4 * i + 3)
                    down_pieces(2 * i + 1)
                    gu_units(4 * i + 4)
                    gu_units(4 * i + 5)
                    down_pieces(2 * i + 2)

            @block.scalar
            def _(act):
                a = nc.scalar

                def norm(n, gain):
                    for m in range(MT):
                        if n:
                            act.wait_ge(x_add, 8 + m + 1)
                        a.activation(XN[:, m, :], X[:, m, :], ACT.Square, accum_out=sumsq[:, m:m + 1]).then_inc(sumsq_s, 1)
                        act.wait_ge(sumsq_s, 8 * n + m + 1)
                        a.activation(rms[:, m:m + 1], sumsq[:, m:m + 1], ACT.Sqrt, bias=eps[:, :],
                                     scale=1.0 / D).then_inc(rms_s, 1)
                    for j in range(16):
                        hf, k = j // 8, j % 8
                        act.wait_ge(xt_s, 16 * n + j + 1)
                        a.activation(HH[:, k, 512 * hf:512 * hf + 512], bank[j % 8][:, :], ACT.Identity,
                                     scale=gain[:, bass.ds(l * KD + k, 1)]).then_inc(h_hi, 1)

                for p in range(4):
                    hi_piece(act, p, V_N)
                norm(0, g_attn)
                for p in range(4, 11):
                    hi_piece(act, p, V_N)
                for m in range(MT):
                    act.wait_ge(moved, 8 + m)
                    a.activation(VS[:, m, :, 0:HD], bank[m][:, 0:384].rearrange("p (h d) -> p h d", d=HD),
                                 ACT.Copy).then_inc(v_stored, 1)
                for p in range(11, 16):
                    hi_piece(act, p, V_N)
                for u in range(2):
                    hi_unit(act, u, u)
                act.wait_ge(x_stored, 16)
                for m in range(MT):
                    act.wait_ge(moved, 15 + 8 + m)
                    a.activation(VA[:, m, :, 0:HD], bank[m][:, 0:256].rearrange("p (h d) -> p h d", d=HD), ACT.Copy)
                    a.activation(VB[:, m, :, 0:HD], bank[m][:, 256:384].rearrange("p (h d) -> p h d", d=HD),
                                 ACT.Copy).then_inc(v_stored, 1)

                def qk_square(u, hf, par):
                    i = 2 * u + hf
                    act.wait_ge(stat, i + 1)
                    if needed(i - 1):
                        act.wait_ge(ss_s, i - 1)
                    a.activation(SQ[:, hf, :], bank[2 * par + hf][:, :], ACT.Square).then_inc(sq_s, 1)

                def qk_rms(i, slot):
                    act.wait_ge(ss_s, i + 1)
                    if needed(i - 1):
                        act.wait_ge(qk_s, i - 1)
                    a.activation(RM[:, slot, :], bank[4 + slot][:, :], ACT.Sqrt, bias=eps[:, :],
                                 scale=1.0 / HD).then_inc(rmsq_s, 1)

                def qk_unit_steps(u, par, first=False, last=False):
                    qk_square(u, 0, par)
                    if not first:
                        qk_rms(2 * u - 1, 1)
                    qk_square(u, 1, par)
                    if not last:
                        hi_unit(act, u + 2, par)
                    qk_rms(2 * u, 0)

                qk_unit_steps(0, 0, first=True)
                qk_unit_steps(1, 1)
                with loop(act, 1, QT // 2 - 1) as i:
                    qk_unit_steps(2 * i, 0)
                    qk_unit_steps(2 * i + 1, 1)
                qk_unit_steps(QT - 2, 0, last=True)
                qk_unit_steps(QT - 1, 1, last=True)
                qk_rms(2 * QT - 1, 1)
                for p in range(16, 20):
                    hi_piece(act, p)

                def store_result(bd, s):
                    k = bd["kind"]
                    G, n = group_buf(bd, s)
                    act.wait_ge(pv_s, bd["T"] + s + 1)
                    if k in ("c3", "c2"):
                        per = 32 if k == "c3" else 16
                        base = 0 if k == "c3" else 128
                        if needed(base + per * bd["i"]):
                            act.wait_ge(g_out_s[s // 6], base + per * bd["i"])
                    elif 6 <= s < 12:
                        if k == "b0":
                            act.wait_ge(g_out_s[0], 192)
                        else:
                            act.wait_ge(c_merged, bd["i"])
                    elif s < 6:
                        if needed(bd["i"]):
                            act.wait_ge(y_s[1], bd["i"])
                    else:
                        if needed(bd["i"]):
                            act.wait_ge(y_s[0], bd["i"])
                    w = V1 * (n + 1)
                    a.activation(G[:, 0:w], group_bank(bd, s)[:, 0:w], ACT.Copy).then_inc(grp_s, 1)

                prev = [None]

                def act_body(bd, nxt):
                    k = bd["kind"]
                    blocks = k not in ("c3", "c2")
                    for s in range(n_tiles(bd)):
                        n = bd["T"] + s
                        w, off = width(bd, s)
                        G, place_ = group_buf(bd, s)
                        act.wait_ge(tmin_s, n + 1)
                        a.activation(T[:, s % 4, off:off + w], T[:, s % 4, off:off + w], ACT.Exp, scale=-1.0,
                                     bias=G[:, 6 * V1 + place_:6 * V1 + place_ + 1]).then_inc(exp_s, 1)
                        if s == 1 and prev[0] is not None:
                            p_bd = prev[0](bd)
                            store_result(p_bd, n_tiles(p_bd) - 1)
                            if blocks and k != "b0":
                                act.wait_ge(c_shift, bd["i"])
                                a.activation(fac_c[:, :, :], shift_c[:, :, :], ACT.Exp).then_inc(c_fac, 1)
                        if s == 7:
                            store_result(bd, 5)
                        if s == 11 and blocks:
                            act.wait_ge(b_shift, bd["i"] + 1)
                            a.activation(fac_b[:, :, :], shift_b[:, :, :], ACT.Exp).then_inc(b_fac, 1)
                        if s == 13 and blocks:
                            store_result(bd, 11)

                def run_act():
                    for n, entry in enumerate(plan):
                        bd0, rounds, (nt, nu, ng, nq) = entry

                        def before(bd, d=(nt, nu, ng, nq)):
                            return dict(bd, i=bd["i"] - 1, T=bd["T"] - d[0], U=bd["U"] - d[1], G=bd["G"] - d[2])

                        def first_before(bd, n=n):
                            e = plan[n - 1]
                            return shifted(e, e[1] - 1)

                        prev[0] = first_before if n else None
                        act_body(bd0, None)
                        prev[0] = before
                        if rounds > 1:
                            with loop(act, 1, rounds) as r:
                                act_body(shifted(entry, r), None)
                    last_bd = shifted(plan[-1], 0)
                    store_result(last_bd, 15)
                    act.wait_ge(c_shift, MT)
                    a.activation(fac_c[:, :, :], shift_c[:, :, :], ACT.Exp).then_inc(c_fac, 1)

                run_act()

                act.wait_ge(pt_copied, UNITS)
                for f in range(KD):
                    a.activation(HH[:, f, :], QK[:, Y_TILE[f], :], ACT.Identity,
                                 scale=g_out[:, bass.ds(l * KD + f, 1)]).then_inc(h_hi, 1)
                for u in range(2):
                    hi_unit(act, QT + u, u)
                for p in range(20, 35):
                    hi_piece(act, p)
                norm(1, g_ffn)
                hi_piece(act, 35)

                def gate_up(j, par, cc, more=True):
                    u = QT + 2 * j
                    for hf in range(2):
                        act.wait_ge(stat, 2 * u + hf + 1)
                        if needed(2 * (j - 1) + hf + 1):
                            act.wait_ge(mul_s, 2 * (j - 1) + hf + 1)
                        a.activation(SI[:, hf, :], bank[hf][:, :], ACT.Silu).then_inc(silu_s, 1)
                    if more:
                        hi_unit(act, u + 2, 0)
                        hi_unit(act, u + 3, 1)
                    for hf in range(2):
                        act.wait_ge(mul_s, 2 * j + hf + 1)
                        a.activation(GH[:, par, cc, 512 * hf:512 * hf + 512], GT[:, hf, :], ACT.Copy).then_inc(g_hi, 1)

                def down_hi(g):
                    for i in range(4):
                        act.wait_ge(piece_raw[i], 16 * (9 + g + 1) + 32)
                        act.wait_ge(moved, 60 + 16 * g + 8 * (i // 2) + 8)
                        a.activation(PH[:, i, :], PR[:, i, :], ACT.Copy).then_inc(piece_hi, 1)

                gate_up(0, 0, 0)
                gate_up(1, 0, 1)
                with loop(act, 0, NG // 2 - 1) as i:
                    gate_up(4 * i + 2, 1, 0)
                    gate_up(4 * i + 3, 1, 1)
                    down_hi(2 * i)
                    gate_up(4 * i + 4, 0, 0)
                    gate_up(4 * i + 5, 0, 1)
                    down_hi(2 * i + 1)
                gate_up(NCH - 4, 1, 0)
                gate_up(NCH - 3, 1, 1)
                down_hi(NG - 3)
                gate_up(NCH - 2, 0, 0)
                gate_up(NCH - 1, 0, 1, more=False)
                down_hi(NG - 2)

            @block.vector
            def _(dve):
                v = nc.vector

                def norm(n, gain, hb):
                    for m in range(MT):
                        dve.wait_ge(rms_s, 8 * n + m + 1)
                        v.reciprocal(rstd[:, m:m + 1], rms[:, m:m + 1]).then_inc(rstd_s, 1)
                        dve.wait_ge(rstd_s, 8 * n + m + 1)
                        v.tensor_scalar(XN[:, m, :], X[:, m, :], rstd[:, m:m + 1], None, ALU.mult).then_inc(xn_s, 1)
                    for j in range(16):
                        hf, k = j // 8, j % 8
                        dve.wait_ge(h_hi, hb + j + 1)
                        v.scalar_tensor_tensor(HL[:, k, 512 * hf:512 * hf + 512], bank[j % 8][:, :],
                                               gain[:, bass.ds(l * KD + k, 1)],
                                               HH[:, k, 512 * hf:512 * hf + 512].bitcast(F32),
                                               op0=ALU.mult, op1=ALU.subtract).then_inc(h_lo, 1)

                for p in range(4):
                    lo_piece(dve, p, V_N)
                norm(0, g_attn, 0)
                for p in range(4, 16):
                    lo_piece(dve, p, V_N)
                for u in range(2):
                    lo_unit(dve, u, u)

                def qk_finish(u, hf, par):
                    i = 2 * u + hf
                    dve.wait_ge(rmsq_s, i + 1)
                    v.reciprocal(RM[:, hf, :], RM[:, hf, :]).then_inc(rec_s, 1)
                    dve.wait_ge(rec_s, i + 1)
                    v.scalar_tensor_tensor(QK[:, bass.ds(u, 1), 512 * hf:512 * hf + 512].rearrange("p a n -> p (a n)"),
                                           bank[2 * par + hf][:, :], g_qk[:, bass.ds(l * QT + u, 1)], RM[:, hf, :],
                                           op0=ALU.mult, op1=ALU.mult).then_inc(qk_s, 1)

                def qk_unit_steps(u, par, first=False, last=False):
                    if not first:
                        qk_finish(u - 1, 1, 1 - par)
                    if not last:
                        lo_unit(dve, u + 2, par)
                    qk_finish(u, 0, par)

                qk_unit_steps(0, 0, first=True)
                qk_unit_steps(1, 1)
                dve.wait_ge(vs_out, 16)
                with loop(dve, 1, QT // 2 - 1) as i:
                    qk_unit_steps(2 * i, 0)
                    qk_unit_steps(2 * i + 1, 1)
                qk_unit_steps(QT - 2, 0, last=True)
                qk_unit_steps(QT - 1, 1, last=True)
                qk_finish(QT - 1, 1, 1)
                for p in range(16, 20):
                    lo_piece(dve, p)

                def tmin(bd, s, carrier):
                    n = bd["T"] + s
                    w, off = width(bd, s)
                    G, place_ = group_buf(bd, s)
                    k = bd["kind"]
                    if carrier:
                        dve.wait_ge(scored, n + 1)
                        dve.sem_inc(dve_gate, 1)
                    if place_ == 0 and k in ("c3", "c2"):
                        if needed((0 if k == "c3" else 128) + (32 if k == "c3" else 16) * bd["i"]):
                            dve.wait_ge(g_out_s[s // 6], (0 if k == "c3" else 128) + (32 if k == "c3" else 16) * bd["i"])
                        dve.sem_inc(dve_gate, 1)
                    if k == "b0" and s == 6:
                        dve.wait_ge(g_out_s[0], 192)
                        dve.sem_inc(dve_gate, 1)
                    if off:
                        v.memset(T[:, s % 4, 0:off], 0.0)
                    slot = s % 2
                    tb = table(bd, s)
                    acc = G[:, 6 * V1 + place_:6 * V1 + place_ + 1]
                    src = score2[slot][:, 0:w]
                    v.tensor_tensor_reduce(out=T[:, s % 4, off:off + w], in0=tb, in1=src, scale=1.0, scalar=3.0e38,
                                           op0=ALU.add, op1=ALU.min, accum_out=acc).then_inc(tmin_s, 1)

                seq = dict(base=0, n=0)

                def link(ins):
                    seq["n"] += 1
                    ins.then_inc(dve_seq, 1)
                    dve.wait_ge(dve_seq, seq["base"] + seq["n"])

                def heads(G, n):
                    return G[:, 0:n * V1].rearrange("p (h d) -> p h d", d=V1)

                def spread(c, n):
                    return c.unsqueeze(2).broadcast_to([P, n, HD])

                def mean_square(fam, n, cols):
                    link(v.tensor_tensor_reduce(out=junk[:, 0:n], in0=cols, in1=cols, scale=1.0, scalar=0.0,
                                                op0=ALU.mult, op1=ALU.add, accum_out=gvar[:, fam:fam + 1]))
                    v.tensor_scalar(gvare[:, fam:fam + 1], gvar[:, fam:fam + 1], 1.0 / n, EPS, ALU.mult,
                                    ALU.add).then_inc(gvar_s[fam], 1)

                NS = l * B_H

                def fin_b1(b):
                    dve.wait_ge(grp_s, C_GROUPS + 3 * b + 1)
                    nm, sk = GB[:, 6 * V1:6 * V1 + 6], nsink[:, bass.ds(NS, 6)]
                    link(v.tensor_tensor(nmin[:, :], nm, sk, ALU.min))
                    v.tensor_tensor(shift_b[:, 0, :], nmin[:, :], nm, ALU.subtract)
                    v.tensor_tensor(shift_b[:, 1, :], nmin[:, :], sk, ALU.subtract).then_inc(b_shift, 1)

                def fin_b2(b):
                    dve.wait_ge(b_fac, b + 1)
                    g = heads(GB[:, :], 6)
                    link(v.tensor_tensor(den[:, 0, :].unsqueeze(2), g[:, :, HD:V1], fac_b[:, 0, :].unsqueeze(2), ALU.mult))
                    link(v.tensor_tensor(den[:, 0, :], den[:, 0, :], fac_b[:, 1, :], ALU.add))
                    link(v.reciprocal(den[:, 0, :], den[:, 0, :]))
                    link(v.tensor_tensor(coef[:, 0, :], den[:, 0, :], fac_b[:, 0, :], ALU.mult))
                    yb = Y[:, 256:640].rearrange("p (g a d) -> p a g d", g=2, a=3)
                    link(v.tensor_tensor(yb, g[:, :, 0:HD].rearrange("p (a g) d -> p a g d", g=2),
                                         coef[:, 0, :].rearrange("p (a g) -> p a g", g=2).unsqueeze(3).broadcast_to([P, 3, 2, HD]),
                                         ALU.mult))
                    mean_square(1, 384, Y[:, 256:640])

                def fin_c1(b):
                    dve.wait_ge(grp_s, C_GROUPS + 3 * b + 2)
                    dve.wait_ge(g_back, 32 * (b + 1))
                    nm = GC[:, :, 6 * V1:6 * V1 + 6]
                    link(v.tensor_tensor(nmin[:, :], GC[:, 0, 6 * V1:6 * V1 + 6], GC[:, 1, 6 * V1:6 * V1 + 6], ALU.min))
                    link(v.tensor_tensor(nmin[:, :], nmin[:, :], GC[:, 2, 6 * V1:6 * V1 + 6], ALU.min))
                    v.tensor_tensor(shift_c[:, :, :], nmin[:, :].unsqueeze(1).broadcast_to([P, 3, 6]), nm,
                                    ALU.subtract).then_inc(c_shift, 1)

                def fin_c2(b):
                    dve.wait_ge(c_fac, b + 1)
                    g = GC[:, :, 0:6 * V1].rearrange("p n (h d) -> p n h d", d=V1)
                    link(v.tensor_tensor(g, g, fac_c[:, :, :].unsqueeze(3).broadcast_to([P, 3, 6, V1]), ALU.mult))
                    link(v.tensor_tensor(GC[:, 0, 0:6 * V1], GC[:, 0, 0:6 * V1], GC[:, 1, 0:6 * V1], ALU.add))
                    link(v.tensor_tensor(GC[:, 0, 0:6 * V1], GC[:, 0, 0:6 * V1], GC[:, 2, 0:6 * V1], ALU.add))
                    g0_ = heads(GC[:, 0, :], 6)
                    link(v.reciprocal(den[:, 2, :].unsqueeze(2), g0_[:, :, HD:V1]))
                    seq["n"] += 1
                    v.tensor_tensor(Y[:, 640:1024].rearrange("p (h d) -> p h d", d=HD), g0_[:, :, 0:HD],
                                    spread(den[:, 2, :], 6), ALU.mult).then_inc(dve_seq, 1)
                    dve.wait_ge(dve_seq, seq["base"] + seq["n"])
                    dve.sem_inc(c_merged, 1)
                    mean_square(2, 384, Y[:, 640:1024])

                def fin_a(b):
                    dve.wait_ge(grp_s, C_GROUPS + 3 * b + 3)
                    g = heads(GA[:, :], 4)
                    link(v.reciprocal(den[:, 1, 0:4].unsqueeze(2), g[:, :, HD:V1]))
                    link(v.tensor_tensor(Y[:, 0:256].rearrange("p (h d) -> p h d", d=HD), g[:, :, 0:HD],
                                         spread(den[:, 1, 0:4], 4), ALU.mult))
                    mean_square(0, 256, Y[:, 0:256])

                def scale_y(fam, b):
                    t, n, i = FAM[fam]
                    dve.wait_ge(grstd_s[i], b + 1)
                    v.tensor_scalar(Y[:, t * P:(t + n) * P], Y[:, t * P:(t + n) * P], grstd[:, i:i + 1], None,
                                    ALU.mult).then_inc(y_s[i], 1)

                def copy_unit(bd, idx, ev, b_now):
                    u = bd["U"] + idx
                    src = bank[4 + idx % 2]
                    dve.wait_ge(pt_made, u + 1)
                    if ev[1] == "p":
                        if needed(bd["T"] + ev[0] - 1):
                            dve.wait_ge(pv_s, bd["T"] + ev[0] - 1)
                        chs = ev[2]
                        w = P * len(chs)
                        v.tensor_copy(PT[:, ev[0] % 2, chs[0][0]:chs[0][0] + w], src[:, 0:w]).then_inc(pt_copied, 1)
                    else:
                        fam, c0, n = ev[2]
                        t0_ = Y_TILE[FAM[fam][0] + c0]
                        v.tensor_scalar(QK[:, t0_:t0_ + n, bass.ds(b_now * P, P)],
                                        src[:, 0:n * P].rearrange("p (t n) -> p t n", n=P), 1.0, None,
                                        ALU.mult).then_inc(pt_copied, 1)

                def dve_body(bd, nxt):
                    k = bd["kind"]
                    blocks = k not in ("c3", "c2")
                    b = bd["i"]
                    evs = events(bd)
                    nt = n_tiles(bd)
                    for s in range(nt):
                        for idx, ev in enumerate(evs):
                            if ev[0] == s:
                                copy_unit(bd, idx, ev, b if ev[1] == "p" or ev[2][0] == "b" else b - 1)
                        if s + 2 < nt:
                            tmin(bd, s + 2, False)
                        elif nxt is not None:
                            if s + 2 == nt and k != nxt["kind"]:
                                if nxt["kind"] == "c2":
                                    dve.wait_ge(tab_c, 32)
                                    dve.sem_inc(dve_gate, 1)
                                if nxt["kind"] == "b0":
                                    dve.wait_ge(tab_ab, 32)
                                    dve.sem_inc(dve_gate, 1)
                            tmin(nxt, s + 2 - nt, False)
                        if not blocks:
                            continue
                        if k != "b0":
                            if s == 2:
                                fin_c2(b - 1)
                            if s == 3:
                                fin_a(b - 1)
                            if s == 4:
                                scale_y("c", b - 1)
                            if s == 5:
                                scale_y("a", b - 1)
                        if s == 9:
                            fin_b1(b)
                        if s == 12:
                            fin_b2(b)
                        if s == 14:
                            scale_y("b", b)
                        if s == 15:
                            fin_c1(b)

                tmin_first = plan[0][0]
                dve.wait_ge(tab_c3, 16)
                dve.sem_inc(dve_gate, 1)
                tmin(tmin_first, 0, True)
                tmin(tmin_first, 1, True)
                LB0, LB = 9, 18
                for n, entry in enumerate(plan):
                    bd0, rounds, _ = entry
                    after = plan[n + 1][0] if n + 1 < len(plan) else None
                    seq["n"] = 0
                    if bd0["kind"] in ("c3", "c2", "b0"):
                        seq["base"] = 0
                    else:
                        seq["base"] = LB0 + LB * (bd0["i"] - 1)
                    if rounds == 1:
                        dve_body(bd0, after)
                    else:
                        dve_body(bd0, shifted(entry, 1))
                        seq["n"] = 0
                        with loop(dve, 1, rounds) as r:
                            if bd0["kind"] == "mid":
                                seq["base"] = LB * r + (LB0 + LB * (bd0["i"] - 1))
                            dve_body(shifted(entry, r), shifted(entry, r + 1))
                    if bd0["kind"] == "b0":
                        assert seq["n"] == LB0, seq
                    elif bd0["kind"] not in ("c3", "c2"):
                        assert seq["n"] == LB, seq
                seq["base"], seq["n"] = LB0 + LB * (MT - 1), 0
                fin_c2(MT - 1)
                fin_a(MT - 1)
                scale_y("c", MT - 1)
                scale_y("a", MT - 1)
                tail = dict(plan[-1][0], U=UNITS - 2)
                copy_unit(tail, 0, (16, "y", ("c", 0, 3)), MT - 1)
                copy_unit(tail, 1, (16, "y", ("a", 0, 2)), MT - 1)

                for f in range(KD):
                    dve.wait_ge(h_hi, 16 + f + 1)
                    v.scalar_tensor_tensor(HL[:, f, :], QK[:, Y_TILE[f], :], g_out[:, bass.ds(l * KD + f, 1)],
                                           HH[:, f, :].bitcast(F32), op0=ALU.mult, op1=ALU.subtract).then_inc(h_lo, 1)
                for u in range(2):
                    lo_unit(dve, QT + u, u)
                for p in range(20, 27):
                    lo_piece(dve, p)

                def add_out(ch):
                    for m in range(MT):
                        dve.wait_ge(moved, 15 * ch + 8 + m)
                        xs = X[:, m, 512 * (ch - 2):512 * (ch - 1)]
                        v.tensor_tensor(xs, xs, bank[m][:, :], ALU.add).then_inc(x_add, 1)

                dve.wait_ge(x_back, 16)
                add_out(2)
                for p in range(27, 35):
                    lo_piece(dve, p)
                add_out(3)
                norm(1, g_ffn, 24)
                lo_piece(dve, 35)

                def gate_up(j, par, cc, more=True):
                    u = QT + 2 * j
                    if more:
                        lo_unit(dve, u + 2, 0)
                        lo_unit(dve, u + 3, 1)
                    for hf in range(2):
                        dve.wait_ge(stat, 2 * u + 2 + hf + 1)
                        dve.wait_ge(silu_s, 2 * j + hf + 1)
                        if needed(2 * (j - 1) + hf + 1):
                            dve.wait_ge(g_lo, 2 * (j - 1) + hf + 1)
                        v.tensor_tensor(GT[:, hf, :], SI[:, hf, :], bank[2 + hf][:, :], ALU.mult).then_inc(mul_s, 1)
                    for hf in range(2):
                        dve.wait_ge(g_hi, 2 * j + hf + 1)
                        v.tensor_tensor(GL[:, par, cc, 512 * hf:512 * hf + 512], GT[:, hf, :],
                                        GH[:, par, cc, 512 * hf:512 * hf + 512].bitcast(F32),
                                        ALU.subtract).then_inc(g_lo, 1)

                def down(g, more=True):
                    for c in range(2):
                        for m in range(MT):
                            dve.wait_ge(moved, 60 + 16 * g + 8 * c + m + 1)
                            xs = X[:, m, 512 * c:512 * c + 512]
                            v.tensor_tensor(xs, xs, bank[4 + m % 4][:, :], ALU.add).then_inc(x_add, 1)
                        for i in range(2):
                            if more:
                                dve.wait_ge(piece_hi, 32 + 4 * (g + 1) + 2 * c + i + 1)
                                v.tensor_tensor(PL[:, 2 * c + i, :], PR[:, 2 * c + i, :],
                                                PH[:, 2 * c + i, :].bitcast(F32), ALU.subtract).then_inc(piece_lo, 1)

                gate_up(0, 0, 0)
                gate_up(1, 0, 1)
                with loop(dve, 0, NG // 2 - 1) as i:
                    gate_up(4 * i + 2, 1, 0)
                    gate_up(4 * i + 3, 1, 1)
                    down(2 * i)
                    gate_up(4 * i + 4, 0, 0)
                    gate_up(4 * i + 5, 0, 1)
                    down(2 * i + 1)
                gate_up(NCH - 4, 1, 0)
                gate_up(NCH - 3, 1, 1)
                down(NG - 3)
                gate_up(NCH - 2, 0, 0)
                gate_up(NCH - 1, 0, 1, more=False)
                down(NG - 2)
                down(NG - 1, more=False)

            @block.gpsimd
            def _(pool):
                g = nc.gpsimd
                pool.wait_ge(xt_s, 16)
                g.memset(VS[:, :, :, HD:V1], 1.0).then_inc(v_ones, 1)
                pool.wait_ge(x_stored, 16)
                pool.wait_ge(xn_s, 8)
                g.memset(VA[:, :, :, HD:V1], 1.0)
                g.memset(VB[:, :, :, HD:V1], 1.0).then_inc(v_ones, 1)
                pool.wait_ge(stat, 2 * QT)
                g.memset(VC[0:64, 0, :, :], 0.0).then_inc(v_ones, 1)

                def carrier():
                    pool.sem_inc(pool_gate, 1)

                def stage(bd, before, q, after_powers):
                    k, i = bd["kind"], bd["i"]
                    nh = 4 if q == 2 else 6
                    if before is not None:
                        pool.wait_ge(scored, before["T"] + min(6 * q + nh, n_tiles(before)))
                    ops = 3 if k in ("c3", "c2") else 2
                    done = bd["Q"] + ops * q
                    if needed(done):
                        pool.wait_ge(staged, done)
                    after_powers()
                    carrier()
                    if k == "c3":
                        qt = QK[:, T_CQ:T_CQ + 3, :].rearrange("p t (j r) -> p t r j", r=16)[:, :, bass.ds(4 * i + 2 * q, 2), :]
                        kt = QK[:, T_CK:T_CK + 3, :].rearrange("p t (j r) -> p t r j", r=16)[:, :, bass.ds(4 * i + 2 * q, 2), :]
                        kd = KS[:, q, :, 0:128].rearrange("p t (r j) -> p t r j", r=2)
                    elif k == "c2":
                        v4 = lambda t: QK[:, t:t + 3, :].rearrange("p t (j r) -> p t r j", r=4)[:, :, bass.ds(i, 1), :]\
                            .rearrange("p t a j -> p t (a j)")
                        qt = v4(T_CQ)[:, :, P * q:P * q + P]
                        kt = v4(T_CK)[:, :, 64 * q:64 * q + 192]
                        kd = KS[:, q, :, :]
                    else:
                        t0_ = (T_BQ, T_CQ, T_AQ)[q]
                        qt = QK[:, t0_:t0_ + nh // 2, bass.ds(i * P, P)]
                        kt = None
                    for par in (1, 0):
                        dst = QS[64 * par:64 * par + 64, 6 * q + par:6 * q + nh:2, :]
                        if k == "c3":
                            dst = dst.rearrange("p t (r j) -> p t r j", r=2)
                        g.tensor_copy(dst, qt[64 * par:64 * par + 64]).then_inc(staged, 1)
                    if kt is not None:
                        pool.wait_ge(staged, done + 2)
                        carrier()
                        g.tensor_copy(kd, kt).then_inc(staged, 1)

                def mean_powers(fam, b, copies):
                    pool.wait_ge(gvar_s[fam], b + 1)
                    pool.wait_ge(staged, copies)
                    carrier()
                    g.tensor_tensor(grstd[:, fam:fam + 1], gvare[:, fam:fam + 1], neghalf[:, :],
                                    ALU.pow).then_inc(grstd_s[fam], 1)

                def pool_body(bd, before):
                    powers = bd["kind"] in ("b1", "mid", "b6", "b7")
                    b = bd["i"]

                    def none_before():
                        pool.wait_ge(v_ones, 3)

                    stage(bd, before, 0, (lambda: pool.wait_ge(grstd_s[0], b - 1)) if powers else none_before)
                    stage(bd, before, 1, lambda: None)
                    if powers:
                        mean_powers(1, b - 1, bd["Q"] + 4)
                    if bd["kind"] not in ("c3", "c2"):
                        stage(bd, before, 2, (lambda: pool.wait_ge(grstd_s[1], b)) if powers else none_before)
                    if powers:
                        mean_powers(2, b - 1, bd["Q"] + 6)
                        mean_powers(0, b - 1, bd["Q"] + 6)

                pool.wait_ge(qk_s, 2 * QT)
                before = None
                for entry in plan:
                    pool_body(entry[0], before)
                    if entry[1] > 1:
                        with loop(pool, 1, entry[1]) as r:
                            pool_body(shifted(entry, r), shifted(entry, r - 1))
                    before = shifted(entry, entry[1] - 1)
                for fam in (1, 2, 0):
                    mean_powers(fam, MT - 1, before["Q"] + 6)

            @block.tensor
            def _(pe):
                t = nc.tensor

                def three(dst, sh, sl, mh, ml, start, stop):
                    t.matmul(dst, sh, mh, start=start, stop=False)
                    t.matmul(dst, sh, ml, start=False, stop=False)
                    return t.matmul(dst, sl, mh, start=False, stop=stop)

                def norm(n, hb):
                    for j in range(16):
                        hf, k = j // 8, j % 8
                        if k == 0:
                            pe.wait_ge(xn_s, 8 * n + 4 * hf + 4)
                        if hf:
                            pe.wait_ge(h_lo, hb + j - 8 + 1)
                        elif n and k >= 4:
                            pe.wait_ge(x_add, 8 + k + 1)
                        for i in range(4):
                            last = t.transpose(bank[j % 8][:, P * i:P * i + P], XN[:, 4 * hf + i, P * k:P * k + P], ident[:, :])
                        last.then_inc(xt_s, 1)

                def moving(ch, n, hb, bank_wait):
                    for k in range(KD):
                        p = 8 * ch + k
                        pe.wait_ge(piece_lo, p + 1)
                        for m in range(MT):
                            if hb is not None and (m == 0 or hb == 8 and k == 0):
                                pe.wait_ge(h_lo, hb + max(k, m) + 1)
                            if k == 0 and bank_wait:
                                bank_wait(m)
                            ins = three(bank[m][:, 0:n], HH[:, k, P * m:P * m + P], HL[:, k, P * m:P * m + P],
                                        PH[:, p % 4, 0:n], PL[:, p % 4, 0:n], k == 0, k == KD - 1)
                            if k == KD - 1 or m == MT - 1:
                                ins.then_inc(moved, 1)

                norm(0, 0)
                moving(0, V_N, 8, None)
                moving(1, V_N, None, lambda m: pe.wait_ge(v_stored, m + 1))

                def half_unit(u, slot, hf, dst):
                    for k in range(KD):
                        last = three(dst, UH[:, slot, k, :], UL[:, slot, k, :], HH[:, k, 512 * hf:512 * hf + 512],
                                     HL[:, k, 512 * hf:512 * hf + 512], k == 0, k == KD - 1)
                    last.then_inc(stat, 1)

                def square_sums(i, slot):
                    pe.wait_ge(sq_s, i + 1)
                    if needed(i - 1):
                        pe.wait_ge(rmsq_s, i - 1)
                    t.matmul(bank[4 + slot][:, :], bones[:, :], SQ[:, slot, :], start=True, stop=True).then_inc(ss_s, 1)

                def qk_unit_steps(u, par, first=False):
                    pe.wait_ge(unit_lo, u + 1)
                    if needed(2 * u - 3):
                        pe.wait_ge(qk_s, 2 * u - 3)
                    half_unit(u, par, 0, bank[2 * par][:, :])
                    if not first:
                        square_sums(2 * u - 1, 1)
                    if needed(2 * u - 2):
                        pe.wait_ge(qk_s, 2 * u - 2)
                    half_unit(u, par, 1, bank[2 * par + 1][:, :])
                    square_sums(2 * u, 0)

                pe.wait_ge(v_stored, 16)
                qk_unit_steps(0, 0, first=True)
                qk_unit_steps(1, 1)
                with loop(pe, 1, QT // 2) as i:
                    qk_unit_steps(2 * i, 0)
                    qk_unit_steps(2 * i + 1, 1)
                square_sums(2 * QT - 1, 1)

                def score(bd, s):
                    n = bd["T"] + s
                    ops = 3 if bd["kind"] in ("c3", "c2") else 2
                    pe.wait_ge(staged, bd["Q"] + ops * (s // 6 + 1))
                    if needed(n - 1):
                        pe.wait_ge(tmin_s, n - 1)
                    slot = s % 2
                    for j, kk in enumerate(keys(bd, s)):
                        w = kk.shape[-1]
                        last = t.matmul(score2[slot][:, 512 * j:512 * j + w], QS[:, s, :], kk, start=True, stop=True)
                    last.then_inc(scored, 1)

                def unit(bd, idx, ev, b_now):
                    u = bd["U"] + idx
                    dst = bank[4 + idx % 2]
                    if ev[1] == "p":
                        pe.wait_ge(exp_s, bd["T"] + ev[0] + 1)
                        srcs = [T[:, ev[0] % 4, c:c + P] for c, _ in ev[2]]
                    else:
                        fam, c0, n = ev[2]
                        t0_, _, fi = FAM[fam]
                        pe.wait_ge(y_s[fi], b_now + 1)
                        srcs = [Y[:, (t0_ + c0 + i) * P:(t0_ + c0 + i + 1) * P] for i in range(n)]
                    if needed(u - 1):
                        pe.wait_ge(pt_copied, u - 1)
                    for i, src in enumerate(srcs):
                        last = t.transpose(dst[0:src.shape[-1], P * i:P * i + P], src, ident[:, :])
                    last.then_inc(pt_made, 1)

                def weigh(bd, s):
                    k = bd["kind"]
                    pe.wait_ge(pt_copied, bd["U"] + last_unit(bd, s) + 1)
                    if s % 6 == 0:
                        if k == "c3":
                            pe.wait_ge(vr_in[s // 6], 32 * bd["i"] + 32)
                            if needed(bd["G"] + s // 6 - 1):
                                pe.wait_ge(grp_s, bd["G"] + s // 6 - 1)
                        elif k == "c2":
                            pe.wait_ge(vr_in[s // 6], 128 + 16 * bd["i"] + 16)
                            pe.wait_ge(grp_s, bd["G"] + s // 6 - 1)
                        elif s == 0:
                            pe.wait_ge(grp_s, bd["G"] - (1 if k == "b0" else 0))
                        else:
                            pe.wait_ge(grp_s, bd["G"] + s // 6 - 1)
                            if k == "b0" and s == 6:
                                pe.wait_ge(vc_in, 48)
                                pe.wait_ge(v_ones, 3)
                    place_ = group_buf(bd, s)[1]
                    chs = chunks_of(bd, s)
                    for c, (col, n) in enumerate(chs):
                        last = t.matmul(group_bank(bd, s)[:, place_ * V1:place_ * V1 + V1],
                                        PT[0:n, s % 2, P * c:P * c + P], values(bd, s, c, n),
                                        start=(c == 0), stop=(c == len(chs) - 1))
                    last.then_inc(pv_s, 1)

                def pe_body(bd, nxt, prev):
                    evs = events(bd)
                    nt = n_tiles(bd)
                    for s in range(nt):
                        if s + 2 < nt:
                            score(bd, s + 2)
                        elif nxt is not None:
                            score(nxt, s + 2 - nt)
                        for idx, ev in enumerate(evs):
                            if ev[0] == s:
                                unit(bd, idx, ev, bd["i"] if ev[1] == "p" or ev[2][0] == "b" else bd["i"] - 1)
                        if s:
                            weigh(bd, s - 1)
                        elif prev is not None:
                            weigh(prev, n_tiles(prev) - 1)

                score(plan[0][0], 0)
                score(plan[0][0], 1)
                for n, entry in enumerate(plan):
                    bd0, rounds, (nt, nu, ng, nq) = entry
                    after = plan[n + 1][0] if n + 1 < len(plan) else None
                    prev = shifted(plan[n - 1], plan[n - 1][1] - 1) if n else None
                    if rounds == 1:
                        pe_body(bd0, after, prev)
                    else:
                        pe_body(bd0, shifted(entry, 1), prev)
                        with loop(pe, 1, rounds) as r:
                            pe_body(shifted(entry, r), shifted(entry, r + 1), shifted(entry, r - 1))
                weigh(plan[-1][0], 15)
                tail = dict(plan[-1][0], U=UNITS - 2)
                unit(tail, 0, (16, "y", ("c", 0, 3)), MT - 1)
                unit(tail, 1, (16, "y", ("a", 0, 2)), MT - 1)

                moving(2, 512, 16, None)
                moving(3, 512, None, lambda m: pe.wait_ge(x_add, m + 1))
                norm(1, 24)
                pe.wait_ge(h_lo, 40)

                def gate_up(j):
                    u = QT + 2 * j
                    for gu in range(2):
                        pe.wait_ge(unit_lo, u + gu + 1)
                        for hf in range(2):
                            if needed(2 * (j - 1) + hf + 1):
                                pe.wait_ge(mul_s if gu else silu_s, 2 * (j - 1) + hf + 1)
                            half_unit(u + gu, gu, hf, bank[2 * gu + hf][:, :])

                def down(g, par):
                    pe.wait_ge(g_lo, 4 * g + 4)
                    for c in range(2):
                        pe.wait_ge(piece_lo, 32 + 4 * g + 2 * c + 2)
                        for m in range(MT):
                            pe.wait_ge(x_add, 16 + 16 * g + 8 * c + m - 4 + 1)
                            for kk in range(2):
                                i = 2 * c + kk
                                last = three(bank[4 + m % 4][:, :], GH[:, par, kk, P * m:P * m + P],
                                             GL[:, par, kk, P * m:P * m + P], PH[:, i, :], PL[:, i, :], kk == 0, kk == 1)
                            last.then_inc(moved, 1)

                gate_up(0)
                gate_up(1)
                with loop(pe, 0, NG // 2) as i:
                    gate_up(4 * i + 2)
                    gate_up(4 * i + 3)
                    down(2 * i, 0)
                    gate_up(4 * i + 4)
                    gate_up(4 * i + 5)
                    down(2 * i + 1, 1)
                down(NG - 1, 0)

            programs.close()
            nc.all_engine_barrier(sems_to_clear=range(sems[0].num, sems[-1].num + 1))

        with ExitStack() as end:
            out_s = end.enter_context(nc.semaphore("out_written"))
            block = end.enter_context(nc.Block())

            @block.sync
            def _(sp):
                sp.dma_start(outr, X[:, :, :]).then_inc(out_s, 16)
                sp.wait_ge(out_s, 16)


def kernel(x, attn_norm, w_in, qk_gain, rpb, sink, out_gain, w_out, ffn_norm, w_gu, w_down):
    import numpy as np
    import concourse.bacc as bacc
    from concourse import mybir as mb
    from concourse.bass_utils import run_bass_kernel_spmd as run

    nc = bacc.Bacc("TRN2", target_bir_lowering=False, num_devices=1, dynamic_dma_scratch_size=1024)
    rpb = np.asarray(rpb)
    padded = np.zeros(rpb.shape[:3] + (127,), rpb.dtype)
    padded[..., 48:79] = rpb[..., ::-1]
    ins = dict(x=x, attn_norm=attn_norm, w_in=w_in, qk_gain=qk_gain, rpb=padded, sink=sink, out_gain=out_gain,
               w_out=w_out, ffn_norm=ffn_norm, w_gu=w_gu, w_down=w_down)
    arrays, args = {}, []
    for name, a in ins.items():
        a = np.ascontiguousarray(a)
        arrays[f"in_{name}"] = a
        args.append(nc.dram_tensor(f"in_{name}", a.shape, mb.dt.from_np(a.dtype), kind="ExternalInput").ap())
    args.append(nc.dram_tensor("result", x.shape, mb.dt.float32, kind="ExternalOutput").ap())
    build_program(nc, *args)
    return run(nc, [arrays], core_ids=[0]).results[0]["result"]
```

```python
from contextlib import ExitStack

import concourse.bass as bass
from concourse import mybir

F32, F32R = mybir.dt.float32, mybir.dt.float32r
ALU = mybir.AluOpType
ACT = mybir.ActivationFunctionType
P = 128


def build_program(nc, x, attn_norm, w_in, qk_gain, rpb, sink, out_gain, w_out, ffn_norm, w_gu, w_down, out):
    depth, D = attn_norm.shape
    S = x.shape[1]
    MT = S // P
    KD = D // P
    IN_W, HID = w_in.shape[2], w_down.shape[1]
    HD = 64
    V1 = HD + 1
    A_H, B_H, C_H = 4, 6, 6
    GW = 64
    EPS = 1e-6
    BIG, BIGD = 1e30, 1e34
    SLOPES = [2.0 ** (-8.0 * (i + 1) / (B_H + C_H)) for i in range(B_H + C_H)]
    B_ORDER = [0, 3, 1, 4, 2, 5]
    AQ, AV, BQ, BV, CQ, CV = 0, 512, 768, 1280, 1408, 2176
    T_AQ, T_AK, T_BQ, T_BK, T_CQ, T_CK = 0, 2, 4, 7, 8, 11
    QT = 14
    Y_TILE = [0, 1, 4, 5, 6, 8, 9, 10]
    NCH = HID // P
    NG = NCH // 2
    GR = 6 * V1 + 6
    TA_S = 23

    xr = x.rearrange("b (m p) d -> p (b m) d", p=P)
    outr = out.rearrange("b (m p) d -> p (b m) d", p=P)
    dram = lambda n, s: nc.dram_tensor(n, s, F32, kind="Internal").ap()
    x_res = dram("x_res", (S, D)).rearrange("(m p) d -> p m d", p=P)
    v_c = dram("v_c", (S, C_H * V1))
    g_dil = [dram("g_d4", (S, GR)), dram("g_d16", (S, GR))]
    t_a = dram("t_a", (depth, P, A_H * TA_S * GW))
    t_b = dram("t_b", (P, B_H * 384))
    t_c = dram("t_c", (P, C_H * (128 + 256 + 256)))

    ctx = ExitStack()
    with ctx:
        base = -(-nc.sbuf_base // 64) * 64
        place = {}
        for name, size in (("CONST", 4096), ("H", 65536), ("R", 24576), ("U", 24576),
                           ("X", 32768), ("F", 57344), ("W", 10240), ("Q", 8192)):
            place[name] = base
            base += size
        at = dict(place)

        def sb(name, shape, dt, region, offset=None):
            if offset is None:
                offset = at[region] - place[region]
                n = 4
                for d in shape[1:]:
                    n *= d
                at[region] += -(-n // 32) * 32
            return nc.alloc_sbuf_tensor_at(name, shape, dt, offset=place[region] + offset)

        ident = sb("ident", [P, P], F32, "CONST")
        bones = sb("bones", [P, P], F32, "CONST")
        g_attn = sb("g_attn", [P, depth * KD], F32, "CONST")
        g_ffn = sb("g_ffn", [P, depth * KD], F32, "CONST")
        g_out = sb("g_out", [P, depth * KD], F32, "CONST")
        g_raw = sb("g_raw", [P, depth * 6], F32, "CONST")
        g_qk = sb("g_qk", [P, depth * QT], F32, "CONST")
        eps = sb("eps", [P, 1], F32, "CONST")
        neghalf = sb("neghalf", [P, 1], F32, "CONST")
        col_mask = sb("col_mask", [P, GW], F32, "CONST")
        sinks = sb("sinks", [P, depth * B_H], F32, "CONST")
        nsink = sb("nsink", [P, depth * B_H], F32, "CONST")
        sumsq = sb("sumsq", [P, MT], F32, "CONST")
        rms = sb("rms", [P, MT], F32, "CONST")
        rstd = sb("rstd", [P, MT], F32, "CONST")
        nmin = sb("nmin", [P, 6], F32, "CONST")
        shift_b = sb("shift_b", [P, 2, 6], F32, "CONST")
        shift_c = sb("shift_c", [P, 3, 6], F32, "CONST")
        fac_b = sb("fac_b", [P, 2, 6], F32, "CONST")
        fac_c = sb("fac_c", [P, 3, 6], F32, "CONST")
        den = sb("den", [P, 3, 6], F32, "CONST")
        coef = sb("coef", [P, 3, 6], F32, "CONST")
        gvar = sb("gvar", [P, 3], F32, "CONST")
        gvare = sb("gvare", [P, 3], F32, "CONST")
        grstd = sb("grstd", [P, 3], F32, "CONST")

        HH = sb("HH", [P, KD, S], F32R, "H", 0)
        HL = sb("HL", [P, KD, S], F32R, "H", 32768)
        TA = sb("TA", [P, A_H, TA_S, GW], F32, "H")
        TB = sb("TB", [P, B_H, 384], F32, "H")
        VC = sb("VC", [P, MT + 1, C_H, V1], F32, "H")
        KS = sb("KS", [P, 2, 3, 192], F32, "H")
        VR = sb("VR", [P, 4, 2, C_H * V1], F32, "H")
        junk = sb("junk", [P, 384], F32, "H")
        TA1 = sb("TA1", [P, A_H, TA_S, GW], F32, "H", 32768)
        RAW0 = sb("RAW0", [P, A_H, TA_S, GW], F32, "F", 32768)
        RAW1 = sb("RAW1", [P, A_H, TA_S, GW], F32, "R", 0)
        PR = sb("PR", [P, 4, 512], F32, "R")
        PH = sb("PH", [P, 4, 512], F32R, "R")
        PL = sb("PL", [P, 4, 512], F32R, "R")
        PT = sb("PT", [P, 4, 640], F32, "R", 8192)
        UR = sb("UR", [P, 2, KD, P], F32, "U")
        UH = sb("UH", [P, 2, KD, P], F32R, "U")
        UL = sb("UL", [P, 2, KD, P], F32R, "U")
        TC3 = sb("TC3", [P, C_H, 128], F32, "U", 8192)
        TC2 = sb("TC2", [P, C_H, 256], F32, "U", 8192 + 3072)
        TC1 = sb("TC1", [P, C_H, 256], F32, "U", 8192 + 3072 + 6144)
        X = sb("X", [P, MT, D], F32, "X", 0)
        VA = sb("VA", [P, MT, A_H, V1], F32, "X")
        VB = sb("VB", [P, MT, 2, V1], F32, "X")
        GB = sb("GB", [P, GR], F32, "X")
        G4 = sb("G4", [P, 4, GR], F32, "X")
        GC, GA = G4[:, 0:3, :], G4[:, 3, :]
        Y = sb("Y", [P, D], F32, "X")
        QK = sb("QK", [P, QT, S], F32, "F", 0)
        VS = sb("VS", [P, MT, C_H, V1], F32, "F", 40960)
        XN = sb("XN", [P, MT, D], F32, "F", 24576)
        GH = sb("GH", [P, 2, 2, S], F32R, "F", 0)
        GL = sb("GL", [P, 2, 2, S], F32R, "F", 16384)
        D_B = sb("D_B", [P, 384], F32, "F", 0)
        D_N = sb("D_N", [P, 384], F32, "F", 2048)
        D_C = sb("D_C", [P, 256], F32, "F", 4096)
        D_C3 = sb("D_C3", [P, 128], F32, "F", 6144)
        TBs = sb("TBs", [P, B_H, 384], F32, "F", 8192)
        TCs = sb("TCs", [P, C_H * 640], F32, "F", 8192 + 9216)
        SQ = sb("SQ", [P, 2, 512], F32, "W", 0)
        RM = sb("RM", [P, 2, 512], F32, "W", 4096)
        SI = sb("SI", [P, 2, 512], F32, "W", 0)
        GT = sb("GT", [P, 2, 512], F32, "W", 4096)
        T = sb("T", [P, 4, 640], F32, "W", 0)
        QS = sb("QS", [P, 16, P], F32, "Q")

        psum = ctx.enter_context(nc.psum_tensor("psum", [P, 8 * 512], F32))
        bank = [psum[:, 512 * i:512 * i + 512] for i in range(8)]
        score2 = [psum[:, 1024 * i:1024 * i + 1024] for i in range(2)]

        with ExitStack() as setup:
            sem = lambda n: setup.enter_context(nc.semaphore(n))
            x_in, gains_in, rpb_in, tabs_out = sem("x_in"), sem("gains_in"), sem("rpb_in"), sem("tabs_out")
            pool_seq, dve_seq = sem("pool_seq"), sem("dve_seq")
            tab_done = sem("tab_done")
            block = setup.enter_context(nc.Block())
            MASK_AT, DIST_AT = [], []

            @block.sync
            def _(sp):
                sp.dma_start(X[:, :, :], xr).then_inc(x_in, 16)
                for l, raw in ((0, RAW0), (1, RAW1)):
                    for h in range(A_H):
                        for half in range(2):
                            lo = 64 * half
                            for s0, n, dr in ((0, 14, 1 - half), (14, 9, 3 - half)):
                                src = bass.AP(rpb.tensor, ((l * A_H + h) * 15 + dr) * 127,
                                              [[1, GW], [127, n], [1, GW]])
                                sp.dma_start(raw[lo:lo + 64, h, s0:s0 + n, :], src).then_inc(rpb_in, 16)
                sp.wait_ge(tab_done, 3)
                sp.dma_start(t_b, TBs[:, :, :].rearrange("p h j -> p (h j)")).then_inc(tabs_out, 16)
                sp.dma_start(t_c, TCs[:, :]).then_inc(tabs_out, 16)
                for l, ta in ((0, TA), (1, TA1)):
                    sp.dma_start(t_a[l], ta[:, :, :, :].rearrange("p h s c -> p (h s c)")).then_inc(tabs_out, 16)
                sp.wait_ge(tabs_out, 64)
                sp.wait_ge(x_in, 16)

            @block.scalar
            def _(act):
                with nc.allow_non_contiguous_dma(reason="gain vectors, a few KB"):
                    act.dma_start(g_attn[:, :].rearrange("p (l k) -> p l k", l=depth),
                                  attn_norm.rearrange("l (k p) -> p l k", p=P)).then_inc(gains_in, 16)
                    act.dma_start(g_ffn[:, :].rearrange("p (l k) -> p l k", l=depth),
                                  ffn_norm.rearrange("l (k p) -> p l k", p=P)).then_inc(gains_in, 16)
                    act.dma_start(g_out[:, :].rearrange("p (l k) -> p l k", l=depth),
                                  out_gain.rearrange("l (k p) -> p l k", p=P)).then_inc(gains_in, 16)
                    for half in range(2):
                        act.dma_start(g_raw[64 * half:64 * half + 64, :],
                                      qk_gain.rearrange("l f q d -> d (l f q)")).then_inc(gains_in, 16)
                    act.dma_start(sinks[:, :], sink.rearrange("l h -> (l h)").partition_broadcast(P)).then_inc(gains_in, 16)
                act.wait_ge(gains_in, 96)

            @block.gpsimd
            def _(pool):
                count = [0]

                def step(ins):
                    count[0] += 1
                    ins.then_inc(pool_seq, 1)
                    pool.wait_ge(pool_seq, count[0])

                g = nc.gpsimd
                step(g.memset(QS[:, :, :], 0.0))
                step(g.memset(ident[:, :], 0.0))
                step(g.affine_select(out=ident[:, :], in_=ident[:, :], compare_op=ALU.not_equal, fill=1.0,
                                     base=0, pattern=[[-1, P]], channel_multiplier=1))
                step(g.memset(bones[:, :], 0.0))
                step(g.memset(bones[0:64, 0:64], 1.0))
                step(g.memset(bones[64:128, 64:128], 1.0))
                step(g.memset(eps[:, :], EPS))
                step(g.memset(neghalf[:, :], -0.5))
                step(g.memset(col_mask[:, :], 0.0))
                for half in range(2):
                    low, high = col_mask[64 * half:64 * half + 64, 0:48], col_mask[64 * half:64 * half + 64, 16:64]
                    step(g.affine_select(out=low, in_=low, compare_op=ALU.is_ge, fill=BIG, base=8,
                                         pattern=[[1, 48]], channel_multiplier=-1))
                    step(g.affine_select(out=high, in_=high, compare_op=ALU.is_ge, fill=BIG, base=-9,
                                         pattern=[[-1, 48]], channel_multiplier=1))
                MASK_AT.append(count[0])
                for dist, w, hw in ((D_B, 384, 128), (D_C, 256, 64), (D_C3, 128, 0)):
                    step(g.iota(dist[:, :], pattern=[[1, w]], base=-hw, channel_multiplier=-1,
                                allow_small_or_imprecise_dtypes=True))
                    step(g.tensor_scalar(D_N[:, 0:w], dist[:, :], -1.0, None, ALU.mult))
                    step(g.affine_select(out=dist[:, :], in_=dist[:, :], compare_op=ALU.is_ge, fill=0.0,
                                         base=-hw, pattern=[[1, w]], channel_multiplier=-1))
                    step(g.affine_select(out=D_N[:, 0:w], in_=D_N[:, 0:w], compare_op=ALU.is_ge, fill=0.0,
                                         base=hw, pattern=[[-1, w]], channel_multiplier=1))
                    step(g.tensor_tensor(dist[:, :], dist[:, :], D_N[:, 0:w], ALU.add))
                    if hw:
                        step(g.affine_select(out=dist[:, :], in_=dist[:, :], compare_op=ALU.is_ge, fill=BIGD,
                                             base=0, pattern=[[1, w]], channel_multiplier=-1))
                        step(g.affine_select(out=dist[:, :], in_=dist[:, :], compare_op=ALU.is_ge, fill=BIGD,
                                             base=2 * hw, pattern=[[-1, w]], channel_multiplier=1))
                step(g.memset(D_C3[0:64, 64:128], BIGD))
                step(g.memset(D_C3[64:128, 0:64], BIGD))
                DIST_AT.append(count[0])

            @block.vector
            def _(dve):
                v = nc.vector
                v.memset(T[:, :, :], 0.0)
                dve.wait_ge(gains_in, 96)
                v.tensor_scalar(nsink[:, :].rearrange("p (l a g) -> p l a g", l=depth, a=3),
                                sinks[:, :].rearrange("p (l g a) -> p l a g", l=depth, a=3), -1.0, None, ALU.mult)
                for l in range(depth):
                    for fam, q0, nq, nk in ((0, T_AQ, 2, 2), (1, T_BQ, 3, 1), (2, T_CQ, 3, 3)):
                        for i in range(nq + nk):
                            src = g_raw[:, l * 6 + fam * 2 + (i >= nq):l * 6 + fam * 2 + (i >= nq) + 1]
                            v.tensor_scalar(g_qk[:, l * QT + q0 + i:l * QT + q0 + i + 1], src,
                                            -(HD ** -0.5) if i < nq else 1.0, None, ALU.mult)
                dve.wait_ge(pool_seq, DIST_AT[0])
                for s in range(B_H):
                    v.tensor_scalar(TBs[:, s, :], D_B[:, :], SLOPES[B_ORDER[s]], None, ALU.mult)
                for h in range(C_H):
                    sl = SLOPES[B_H + h]
                    v.tensor_scalar(TCs[:, h * 128:h * 128 + 128], D_C3[:, :], 16 * sl, None, ALU.mult)
                    v.tensor_scalar(TCs[:, 768 + h * 256:768 + h * 256 + 256], D_C[:, :], 4 * sl, None, ALU.mult)
                    last = v.tensor_scalar(TCs[:, 2304 + h * 256:2304 + h * 256 + 256], D_C[:, :], sl, None, ALU.mult)
                last.then_inc(tab_done, 1)
                dve.wait_ge(rpb_in, 16 * 2 * A_H * 2 * 2)
                for n, (ta, raw) in enumerate(((TA, RAW0), (TA1, RAW1))):
                    v.tensor_tensor(ta[:, :, :, :].rearrange("p h s c -> p (h s) c"),
                                    col_mask[:, :].unsqueeze(1).broadcast_to([P, A_H * TA_S, GW]),
                                    raw[:, :, :, :].rearrange("p h s c -> p (h s) c")[:, :, ::-1],
                                    ALU.subtract).then_inc(dve_seq, 1)
                    dve.wait_ge(dve_seq, n + 1)
                    v.memset(ta[0:64, :, 22, :], BIG)
                    v.memset(ta[64:128, :, 14, :], BIG).then_inc(tab_done, 1)

        with nc.Fori(0, depth) as l, ExitStack() as layer:
            sems = []

            def sem(name):
                sems.append(layer.enter_context(nc.semaphore(name)))
                return sems[-1]

            x_stored, x_back = sem("x_stored"), sem("x_back")
            piece_raw = [sem(f"piece_raw{i}") for i in range(4)]
            unit_raw = [sem(f"unit_raw{i}") for i in range(2)]
            piece_hi, piece_lo, unit_hi, unit_lo = sem("piece_hi"), sem("piece_lo"), sem("unit_hi"), sem("unit_lo")
            moved = sem("moved")
            stat = sem("stat")
            sumsq_s, rms_s, rstd_s, xn_s = sem("sumsq_s"), sem("rms_s"), sem("rstd_s"), sem("xn_s")
            xt_s, h_hi, h_lo = sem("xt_s"), sem("h_hi"), sem("h_lo")
            v_stored, v_ones, vs_out = sem("v_stored"), sem("v_ones"), sem("vs_out")
            sq_s, ss_s, rmsq_s, rec_s, qk_s = sem("sq_s"), sem("ss_s"), sem("rmsq_s"), sem("rec_s"), sem("qk_s")
            x_add = sem("x_add")
            silu_s, mul_s, g_hi, g_lo = sem("silu_s"), sem("mul_s"), sem("g_hi"), sem("g_lo")
            tab_c3, tab_c, tab_ab, vc_in = sem("tab_c3"), sem("tab_c"), sem("tab_ab"), sem("vc_in")
            vr_in = [sem(f"vr_in{i}") for i in range(4)]
            g_out_s = [sem(f"g_out{i}") for i in range(4)]
            g_back = sem("g_back")
            staged, scored, tmin_s, exp_s = sem("staged"), sem("scored"), sem("tmin_s"), sem("exp_s")
            pt_made, pv_s, grp_s = sem("pt_made"), sem("pv_s"), sem("grp_s")
            pt_copied = [sem("pt_copied_dve"), sem("pt_copied_act")]
            staged_low = sem("staged_low")
            b_shift, b_fac, c_shift, c_fac, c_merged = (sem(n) for n in ("b_shift", "b_fac", "c_shift", "c_fac", "c_merged"))
            gvar_s, grstd_s, y_s = ([sem(f"{n}_{f}") for f in "abc"] for n in ("gvar_s", "grstd_s", "y_s"))
            dve_seq = sem("dve_seq")
            dve_gate, pool_gate = sem("dve_gate"), sem("pool_gate")

            def needed(value):
                return not isinstance(value, int) or value > 0

            def loop(eng, n0, n1):
                return eng.Fori(n0, n1)

            programs = ExitStack()
            block = programs.enter_context(nc.Block())

            def raw_need(p):
                extra = p // 4 - 1
                if isinstance(p, int):
                    extra = max(0, min(2, extra))
                    return 16 * (p // 4 + 1) + 16 * extra
                raise ValueError

            def piece_done(p):
                if p < 0:
                    return 0
                if p < 32:
                    ch, k = p // 8, p % 8
                    return 15 * ch + (k + 1 if k < 7 else 15)
                g, c = (p - 32) // 4, (p - 32) % 4 // 2
                return 60 + 16 * g + 8 * c + 8

            def hi_piece(act, p, n=512):
                act.wait_ge(piece_raw[p % 4], raw_need(p))
                if needed(piece_done(p - 4)):
                    act.wait_ge(moved, piece_done(p - 4))
                nc.scalar.activation(PH[:, p % 4, 0:n], PR[:, p % 4, 0:n], ACT.Copy).then_inc(piece_hi, 1)

            def lo_piece(dve, p, n=512):
                dve.wait_ge(piece_hi, p + 1)
                nc.vector.tensor_tensor(PL[:, p % 4, 0:n], PR[:, p % 4, 0:n], PH[:, p % 4, 0:n].bitcast(F32),
                                        ALU.subtract).then_inc(piece_lo, 1)

            def hi_unit(act, u, slot):
                act.wait_ge(unit_raw[slot], (u - slot) * 16 + 32)
                if needed(2 * u - 2):
                    act.wait_ge(stat, 2 * u - 2)
                nc.scalar.activation(UH[:, slot, :, :], UR[:, slot, :, :], ACT.Copy).then_inc(unit_hi, 1)

            def lo_unit(dve, u, slot):
                dve.wait_ge(unit_hi, u + 1)
                nc.vector.tensor_tensor(UL[:, slot, :, :], UR[:, slot, :, :], UH[:, slot, :, :].bitcast(F32),
                                        ALU.subtract).then_inc(unit_lo, 1)

            V_N = 384

            def body(kind, i, T0, U0, G0, Q0):
                return dict(kind=kind, i=i, T=T0, U=U0, G=G0, Q=Q0, half_U=U0 // 2)

            def dilated(bd):
                return bd["kind"] in ("c3", "c2")

            def n_tiles(bd):
                return 24 if dilated(bd) else 16

            def chunks_of(bd, s):
                k = bd["kind"]
                if k == "c3":
                    return [(0, 128)]
                if k == "c2":
                    return [(0, 128), (128, 64 if s // 6 % 2 == 0 else 128)]
                if s < 6:
                    return [(0, 128), (128, 128)] + ([] if k in ("b0", "b7") else [(256, 128)])
                if s < 12:
                    return [(0, 128), (128, 64 if k == "b7" else 128)]
                return [(128 * c, 128) for c in range(4)] + ([(512, 64)] if k == "mid" else [])

            def units_of(bd, s):
                ch = chunks_of(bd, s)
                return [ch[0:4], ch[4:]] if len(ch) > 4 else [ch]

            Y_AT = {"b": 6, "a": 10, "c": 14}
            Y_TAIL = [(16, "y", ("b", 0, 2)), (16, "y", ("b", 2, 1)), (16, "y", ("a", 0, 2)), (16, "y", ("c", 0, 3))]

            def events(bd):
                ev = []
                for s in range(n_tiles(bd)):
                    for u in units_of(bd, s):
                        ev.append((s, "p", u))
                    if dilated(bd) or bd["kind"] == "b0":
                        continue
                    if s == Y_AT["b"]:
                        ev += [(s, "y", ("b", 0, 2)), (s, "y", ("b", 2, 1))]
                    if s == Y_AT["a"]:
                        ev.append((s, "y", ("a", 0, 2)))
                    if s == Y_AT["c"]:
                        ev.append((s, "y", ("c", 0, 3)))
                return ev

            def tile_units(bd, s):
                return [i for i, e in enumerate(events(bd)) if e[0] == s and e[1] == "p"]

            plan = []
            t0 = u0 = g0 = q0 = 0
            for kind, rounds, b0 in (("c3", 2, 0), ("c2", 2, 0), ("b0", 1, 0), ("b1", 1, 1), ("mid", 4, 2),
                                     ("b6", 1, 6), ("b7", 1, 7)):
                bd = body(kind, b0, t0, u0, g0, q0)
                nt, nu = n_tiles(bd), len(events(bd))
                ng, nq = (4, 8) if kind in ("c3", "c2") else (3, 6)
                plan.append((bd, rounds, (nt, nu, ng, nq)))
                t0, u0, g0, q0 = t0 + rounds * nt, u0 + rounds * nu, g0 + rounds * ng, q0 + rounds * nq
            TILES, UNITS = t0, u0 + len(Y_TAIL)
            C_GROUPS = 16

            def shifted(entry, r):
                bd, _, (nt, nu, ng, nq) = entry
                if isinstance(r, int) and r == 0:
                    return bd
                return dict(bd, i=bd["i"] + r, T=bd["T"] + r * nt, U=bd["U"] + r * nu, G=bd["G"] + r * ng,
                            Q=bd["Q"] + r * nq, half_U=bd["half_U"] + r * (nu // 2))

            def run(eng, program):
                for n, entry in enumerate(plan):
                    rounds = entry[1]
                    after = plan[n + 1][0] if n + 1 < len(plan) else None
                    before = shifted(plan[n - 1], plan[n - 1][1] - 1) if n else None
                    if rounds == 1:
                        program(entry[0], after, before)
                    elif dilated(entry[0]):
                        program(entry[0], shifted(entry, 1), before)
                        program(shifted(entry, 1), after, entry[0])
                    else:
                        program(entry[0], shifted(entry, 1), before)
                        with loop(eng, 1, rounds) as r:
                            program(shifted(entry, r), shifted(entry, r + 1), shifted(entry, r - 1))

            def width(bd, s):
                k = bd["kind"]
                if k == "c3":
                    return 128, 0
                if k == "c2":
                    return 192, (0 if s // 6 % 2 == 0 else 64)
                if s < 6:
                    return (256 if k in ("b0", "b7") else 384), 0
                if s < 12:
                    return (192 if k in ("b0", "b7") else 256), (64 if k == "b0" else 0)
                return (576 if k == "mid" else 512), 0

            def a_row0(bd):
                k = bd["kind"]
                if k == "mid":
                    return 2 * bd["i"] - 4, 14
                row0 = 0 if k in ("b0", "b1") else MT * 2 - 8
                return row0, row0 - 2 * bd["i"] + 6

            def keys(bd, s):
                k, b, (w, _) = bd["kind"], bd["i"], width(bd, s)
                if k == "c3":
                    return [KS[:, s // 6 % 2, s % 6 // 2, 0:128]]
                if k == "c2":
                    return [KS[:, s // 6 % 2, s % 6 // 2, 0:192]]
                if s < 6:
                    return [QK[:, T_BK, bass.ds(0 if k == "b0" else b * P - P, w)]]
                if s < 12:
                    return [QK[:, T_CK + (s - 6) // 2, bass.ds(0 if k == "b0" else b * P - 64, w)]]
                t0 = a_row0(bd)[0] * GW
                return [QK[:, T_AK + (s - 12) // 2, bass.ds(t0 + j, min(512, w - j))] for j in range(0, w, 512)]

            def table(bd, s):
                k, (w, _) = bd["kind"], width(bd, s)
                if k == "c3":
                    return TC3[:, s % 6, :]
                if k == "c2":
                    return TC2[:, s % 6, 64:256] if s // 6 % 2 == 0 else TC2[:, s % 6, 0:192]
                if s < 6:
                    j0 = 128 if k == "b0" else 0
                    return TB[:, s, j0:j0 + w]
                if s < 12:
                    j0 = 64 if k == "b0" else 0
                    return TC1[:, s - 6, j0:j0 + w]
                s0 = a_row0(bd)[1]
                return TA[:, s - 12, s0:s0 + w // GW, :].rearrange("p s c -> p (s c)")

            def group_buf(bd, s):
                if bd["kind"] in ("c3", "c2"):
                    return G4[:, s // 6, :], s % 6
                return (GB[:, :], s) if s < 6 else (GC[:, 0, :], s - 6) if s < 12 else (GA, s - 12)

            def group_bank(bd, s):
                if bd["kind"] in ("c3", "c2"):
                    return bank[6 + s // 6 % 2]
                return bank[7] if 6 <= s < 12 else bank[6]

            def values(bd, s, c, n):
                k, b = bd["kind"], bd["i"]
                if k in ("c3", "c2"):
                    return VR[0:n, s // 6, c, (s % 6) * V1:(s % 6 + 1) * V1]
                if s < 6:
                    return VB[0:n, bass.ds((0 if k == "b0" else b - 1) + c, 1), s % 2, :].rearrange("p a d -> p (a d)")
                if s < 12:
                    return VC[0:n, bass.ds(b + c, 1), s - 6, :].rearrange("p a d -> p (a d)")
                t0 = b - 2 if k == "mid" else a_row0(bd)[0] // 2
                return VA[0:n, bass.ds(t0 + c, 1), s - 12, :].rearrange("p a d -> p (a d)")

            def dilated_rows(bd, t, q, n):
                i = bd["i"]
                if bd["kind"] == "c3":
                    return QK[:, t:t + 3, :].rearrange("p t (j r) -> p t r j", r=16)[:, :, bass.ds(8 * i + 2 * q, 2), :]
                seq_ = QK[:, t:t + 3, :].rearrange("p t (j r) -> p t r j", r=4)[:, :, bass.ds(2 * i + q // 2, 1), :]
                first = (S // 4 - n) * (q % 2)
                return seq_.rearrange("p t a j -> p t (a j)")[:, :, first:first + n]

            FAM = {"a": (0, 2, 0), "b": (2, 3, 1), "c": (5, 3, 2)}

            @block.sync
            def _(sp):
                def piece(p, parts):
                    if needed(p - 3):
                        sp.wait_ge(piece_lo, p - 3)
                    for dst, src in parts:
                        sp.dma_start(PR[:, p % 4, dst[0]:dst[1]], src).then_inc(piece_raw[p % 4], 16)

                def unit(u, slot, parts):
                    if needed(u - 1):
                        sp.wait_ge(unit_lo, u - 1)
                    for dst, src in parts:
                        sp.dma_start(dst, src).then_inc(unit_raw[slot], 16)

                def halves(slot, src):
                    return [(UR[:, slot, 4 * i:4 * i + 4, :], src[:, 4 * i:4 * i + 4, :]) for i in range(2)]

                wi = w_in[bass.ds(l, 1)].rearrange("a (k p) n -> p (a k) n", p=P)
                wo = w_out[bass.ds(l, 1)].rearrange("a (k p) n -> p (a k) n", p=P)
                wg = w_gu[bass.ds(l, 1)].rearrange("a (k p) n -> p (a k) n", p=P)
                wd = w_down[bass.ds(l, 1)].rearrange("a (k p) n -> p (a k) n", p=P)
                for k in range(8):
                    if k == 4:
                        sp.dma_start(x_res, X[:, :, :]).then_inc(x_stored, 16)
                    piece(k, [((0, 384), wi[:, k, CV:CV + 384])])
                for k in range(8):
                    piece(8 + k, [((0, 256), wi[:, k, AV:AV + 256]), ((256, 384), wi[:, k, BV:BV + 128])])

                def qk_unit(t):
                    if T_BQ <= t < T_BK:
                        a = t - T_BQ
                        unit(t, t % 2, [(UR[:, t % 2, :, 64 * g:64 * g + 64],
                                         wi[:, :, BQ + (3 * g + a) * 64:BQ + (3 * g + a) * 64 + 64]) for g in range(2)])
                    else:
                        col = AQ + t * P if t < T_BQ else BQ + 384 if t == T_BK else CQ + (t - T_CQ) * P
                        unit(t, t % 2, halves(t % 2, wi[:, :, col:col + P]))

                qk_unit(0)
                qk_unit(1)
                sp.wait_ge(v_stored, 8)
                sp.wait_ge(v_ones, 1)
                sp.dma_start(v_c.rearrange("(m p) c -> p m c", p=P),
                             VS[:, :, :, :].rearrange("p m h d -> p m (h d)")).then_inc(vs_out, 16)
                for t in range(2, QT):
                    qk_unit(t)
                for k in range(4):
                    piece(16 + k, [((0, 512), wo[:, k, 0:512])])
                for u in range(2):
                    unit(QT + u, u, halves(u, wg[:, :, u * HID:u * HID + P]))
                sp.wait_ge(stat, 2 * QT)
                sp.dma_start(TC3[:, :, :].rearrange("p h j -> p (h j)"), t_c[:, 0:768]).then_inc(tab_c3, 16)
                sp.wait_ge(vs_out, 16)

                def load_values(gi):
                    slot = gi % 4
                    if gi >= 4:
                        sp.wait_ge(pv_s, 6 * (gi - 3))
                    if gi < 8:
                        v16 = v_c.rearrange("(j r) c -> r j c", r=16)
                        for rr in range(2):
                            sp.dma_start(VR[64 * rr:64 * rr + 64, slot, 0, :], v16[2 * gi + rr]).then_inc(vr_in[slot], 16)
                    else:
                        v4 = v_c.rearrange("(t p r) c -> r p t c", p=P, r=4)
                        sp.dma_start(VR[:, slot, :, :], v4[(gi - 8) // 2]).then_inc(vr_in[slot], 16)

                def store_group(gi):
                    sp.wait_ge(grp_s, gi + 1)
                    slot = gi % 4
                    if gi < 8:
                        g16 = g_dil[1].rearrange("(j r) c -> r j c", r=16)
                        for rr in range(2):
                            sp.dma_start(g16[2 * gi + rr], G4[64 * rr:64 * rr + 64, slot, :]).then_inc(g_out_s[slot], 16)
                    else:
                        g4 = g_dil[0].rearrange("(t p r) c -> r t p c", p=P, r=4)
                        sp.dma_start(g4[(gi - 8) // 2, gi % 2], G4[:, slot, :]).then_inc(g_out_s[slot], 16)

                for gi in range(4):
                    load_values(gi)
                sp.dma_start(TC2[:, :, :].rearrange("p h j -> p (h j)"), t_c[:, 768:2304]).then_inc(tab_c, 16)
                sp.dma_start(TC1[:, :, :].rearrange("p h j -> p (h j)"), t_c[:, 2304:3840]).then_inc(tab_c, 16)
                sp.dma_start(TB[:, :, :].rearrange("p h j -> p (h j)"), t_b).then_inc(tab_ab, 16)
                vsh = v_c[64:S - 64, :].rearrange("(m p) c -> p m c", p=P)
                sp.dma_start(VC[:, 1:MT, :, :].rearrange("p m h d -> p m (h d)"), vsh).then_inc(vc_in, 16)
                sp.dma_start(VC[64:128, 0, :, :].rearrange("p h d -> p (h d)"), v_c[0:64, :]).then_inc(vc_in, 16)
                sp.dma_start(VC[0:64, MT, :, :].rearrange("p h d -> p (h d)"), v_c[S - 64:S, :]).then_inc(vc_in, 16)
                sp.dma_start(TA[:, :, :, :].rearrange("p h s c -> p (h s c)"),
                             t_a[bass.ds(l, 1)].rearrange("a p n -> (a p) n")).then_inc(tab_ab, 16)
                for gi in range(C_GROUPS):
                    store_group(gi)
                    if gi + 4 < C_GROUPS:
                        load_values(gi + 4)
                for slot in range(4):
                    sp.wait_ge(g_out_s[slot], 16 * 6)
                for b in range(MT):
                    if needed(b):
                        sp.wait_ge(c_merged, b)
                    for n in range(2):
                        sp.dma_start(GC[:, 1 + n, :], g_dil[n][b * P:b * P + P, :]).then_inc(g_back, 16)
                for parity in range(2):
                    sp.wait_ge(pt_copied[parity], UNITS // 2)
                sp.dma_start(X[:, :, :], x_res).then_inc(x_back, 16)
                for p in range(20, 32):
                    piece(p, [((0, 512), wo[:, p % 8, 512 * (p // 8 - 2):512 * (p // 8 - 1)])])

                def down_pieces(g):
                    for i in range(4):
                        sp.wait_ge(piece_lo, 32 + 4 * g + i - 3)
                        sp.dma_start(PR[:, i, :], wd[:, bass.ds(2 * g + i % 2, 1), 512 * (i // 2):512 * (i // 2) + 512]
                                     .rearrange("p a n -> p (a n)")).then_inc(piece_raw[i], 16)

                def gu_units(j):
                    for u in range(2):
                        sp.wait_ge(unit_lo, QT + 2 * j + u - 1)
                        for i in range(2):
                            sp.dma_start(UR[:, u, 4 * i:4 * i + 4, :],
                                         wg[:, 4 * i:4 * i + 4, bass.ds(j * P + u * HID, P)]).then_inc(unit_raw[u], 16)

                gu_units(1)
                down_pieces(0)
                with loop(sp, 0, NG // 2) as i:
                    gu_units(4 * i + 2)
                    gu_units(4 * i + 3)
                    down_pieces(2 * i + 1)
                    gu_units(4 * i + 4)
                    gu_units(4 * i + 5)
                    down_pieces(2 * i + 2)

            @block.scalar
            def _(act):
                a = nc.scalar

                def norm(n, gain):
                    for m in range(MT):
                        if n:
                            act.wait_ge(x_add, 8 + m + 1)
                        a.activation(XN[:, m, :], X[:, m, :], ACT.Square, accum_out=sumsq[:, m:m + 1]).then_inc(sumsq_s, 1)
                        act.wait_ge(sumsq_s, 8 * n + m + 1)
                        a.activation(rms[:, m:m + 1], sumsq[:, m:m + 1], ACT.Sqrt, bias=eps[:, :],
                                     scale=1.0 / D).then_inc(rms_s, 1)
                    for j in range(16):
                        hf, k = j // 8, j % 8
                        act.wait_ge(xt_s, 16 * n + j + 1)
                        a.activation(HH[:, k, 512 * hf:512 * hf + 512], bank[j % 8][:, :], ACT.Identity,
                                     scale=gain[:, bass.ds(l * KD + k, 1)]).then_inc(h_hi, 1)

                for p in range(4):
                    hi_piece(act, p, V_N)
                norm(0, g_attn)
                for p in range(4, 11):
                    hi_piece(act, p, V_N)
                for m in range(MT):
                    act.wait_ge(moved, 8 + m)
                    a.activation(VS[:, m, :, 0:HD], bank[m][:, 0:384].rearrange("p (h d) -> p h d", d=HD),
                                 ACT.Copy).then_inc(v_stored, 1)
                for p in range(11, 16):
                    hi_piece(act, p, V_N)
                for u in range(2):
                    hi_unit(act, u, u)
                act.wait_ge(x_stored, 16)
                for m in range(MT):
                    act.wait_ge(moved, 15 + 8 + m)
                    a.activation(VA[:, m, :, 0:HD], bank[m][:, 0:256].rearrange("p (h d) -> p h d", d=HD), ACT.Copy)
                    a.activation(VB[:, m, :, 0:HD], bank[m][:, 256:384].rearrange("p (h d) -> p h d", d=HD),
                                 ACT.Copy).then_inc(v_stored, 1)

                def qk_square(u, hf, par):
                    i = 2 * u + hf
                    act.wait_ge(stat, i + 1)
                    if needed(i - 1):
                        act.wait_ge(ss_s, i - 1)
                    a.activation(SQ[:, hf, :], bank[2 * par + hf][:, :], ACT.Square).then_inc(sq_s, 1)

                def qk_rms(i, slot):
                    act.wait_ge(ss_s, i + 1)
                    if needed(i - 1):
                        act.wait_ge(qk_s, i - 1)
                    a.activation(RM[:, slot, :], bank[4 + slot][:, :], ACT.Sqrt, bias=eps[:, :],
                                 scale=1.0 / HD).then_inc(rmsq_s, 1)

                def qk_unit_steps(u, par, first=False, last=False):
                    qk_square(u, 0, par)
                    if not first:
                        qk_rms(2 * u - 1, 1)
                    qk_square(u, 1, par)
                    if not last:
                        hi_unit(act, u + 2, par)
                    qk_rms(2 * u, 0)

                qk_unit_steps(0, 0, first=True)
                qk_unit_steps(1, 1)
                with loop(act, 1, QT // 2 - 1) as i:
                    qk_unit_steps(2 * i, 0)
                    qk_unit_steps(2 * i + 1, 1)
                qk_unit_steps(QT - 2, 0, last=True)
                qk_unit_steps(QT - 1, 1, last=True)
                qk_rms(2 * QT - 1, 1)

                def store_result(bd, s):
                    G, n = group_buf(bd, s)
                    act.wait_ge(pv_s, bd["T"] + s + 1)
                    w = V1 * (n + 1)
                    a.activation(G[:, 0:w], group_bank(bd, s)[:, 0:w], ACT.Copy).then_inc(grp_s, 1)

                def exponential(bd, s):
                    n = bd["T"] + s
                    w, off = width(bd, s)
                    G, place_ = group_buf(bd, s)
                    act.wait_ge(tmin_s, n + 1)
                    a.activation(T[:, s % 4, off:off + w], T[:, s % 4, off:off + w], ACT.Exp, scale=-1.0,
                                 bias=G[:, 6 * V1 + place_:6 * V1 + place_ + 1]).then_inc(exp_s, 1)

                def branch_factors(b):
                    act.wait_ge(c_shift, b + 1)
                    a.activation(fac_c[:, :, :], shift_c[:, :, :], ACT.Exp).then_inc(c_fac, 1)

                def copy_unit(bd, idx, ev, b_now):
                    act.wait_ge(pt_made, bd["U"] + idx + 1)
                    if ev[1] == "p":
                        c0, w = ev[2][0][0], P * len(ev[2])
                        a.activation(PT[:, ev[0] % 4, c0:c0 + w], bank[5][:, 0:w], ACT.Copy).then_inc(pt_copied[1], 1)
                    else:
                        fam, c0, n = ev[2]
                        t0_ = Y_TILE[FAM[fam][0] + c0]
                        a.activation(QK[:, t0_:t0_ + n, bass.ds(b_now * P, P)],
                                     bank[5][:, 0:n * P].rearrange("p (t n) -> p t n", n=P),
                                     ACT.Copy).then_inc(pt_copied[1], 1)

                def act_body(bd, nxt, prev):
                    blocks = not dilated(bd)
                    for s in range(n_tiles(bd)):
                        if s + 1 < n_tiles(bd):
                            exponential(bd, s + 1)
                        elif nxt is not None:
                            exponential(nxt, 0)
                        if s == 2 and prev is not None:
                            store_result(prev, n_tiles(prev) - 1)
                        if s in ((8, 14) if blocks else (8, 14, 20)):
                            store_result(bd, s - 3)
                        if s == 3 and blocks and bd["kind"] != "b0":
                            branch_factors(bd["i"] - 1)
                        if s == 12 and blocks:
                            act.wait_ge(b_shift, bd["i"] + 1)
                            a.activation(fac_b[:, :, :], shift_b[:, :, :], ACT.Exp).then_inc(b_fac, 1)
                        for idx, ev in enumerate(events(bd)):
                            if ev[0] == s and idx % 2 == 1:
                                copy_unit(bd, idx, ev, bd["i"] - 1)

                exponential(plan[0][0], 0)
                run(act, act_body)
                last_bd = shifted(plan[-1], 0)
                store_result(last_bd, 15)
                branch_factors(MT - 1)
                tail = dict(last_bd, U=UNITS - len(Y_TAIL))
                for p in range(16, 20):
                    hi_piece(act, p)
                for idx, ev in enumerate(Y_TAIL):
                    if idx % 2 == 1:
                        copy_unit(tail, idx, ev, MT - 1)

                for parity in range(2):
                    act.wait_ge(pt_copied[parity], UNITS // 2)
                for f in range(KD):
                    a.activation(HH[:, f, :], QK[:, Y_TILE[f], :], ACT.Identity,
                                 scale=g_out[:, bass.ds(l * KD + f, 1)]).then_inc(h_hi, 1)
                for u in range(2):
                    hi_unit(act, QT + u, u)
                for p in range(20, 35):
                    hi_piece(act, p)
                norm(1, g_ffn)
                hi_piece(act, 35)

                def gate_up(j, par, cc, more=True):
                    u = QT + 2 * j
                    for hf in range(2):
                        act.wait_ge(stat, 2 * u + hf + 1)
                        if needed(2 * (j - 1) + hf + 1):
                            act.wait_ge(mul_s, 2 * (j - 1) + hf + 1)
                        a.activation(SI[:, hf, :], bank[hf][:, :], ACT.Silu).then_inc(silu_s, 1)
                    if more:
                        hi_unit(act, u + 2, 0)
                        hi_unit(act, u + 3, 1)
                    for hf in range(2):
                        act.wait_ge(mul_s, 2 * j + hf + 1)
                        a.activation(GH[:, par, cc, 512 * hf:512 * hf + 512], GT[:, hf, :], ACT.Copy).then_inc(g_hi, 1)

                def down_hi(g):
                    for i in range(4):
                        act.wait_ge(piece_raw[i], 16 * (9 + g + 1) + 32)
                        act.wait_ge(moved, 60 + 16 * g + 8 * (i // 2) + 8)
                        a.activation(PH[:, i, :], PR[:, i, :], ACT.Copy).then_inc(piece_hi, 1)

                gate_up(0, 0, 0)
                gate_up(1, 0, 1)
                with loop(act, 0, NG // 2 - 1) as i:
                    gate_up(4 * i + 2, 1, 0)
                    gate_up(4 * i + 3, 1, 1)
                    down_hi(2 * i)
                    gate_up(4 * i + 4, 0, 0)
                    gate_up(4 * i + 5, 0, 1)
                    down_hi(2 * i + 1)
                gate_up(NCH - 4, 1, 0)
                gate_up(NCH - 3, 1, 1)
                down_hi(NG - 3)
                gate_up(NCH - 2, 0, 0)
                gate_up(NCH - 1, 0, 1, more=False)
                down_hi(NG - 2)

            @block.vector
            def _(dve):
                v = nc.vector

                def norm(n, gain, hb):
                    for m in range(MT):
                        dve.wait_ge(rms_s, 8 * n + m + 1)
                        v.reciprocal(rstd[:, m:m + 1], rms[:, m:m + 1]).then_inc(rstd_s, 1)
                        dve.wait_ge(rstd_s, 8 * n + m + 1)
                        v.tensor_scalar(XN[:, m, :], X[:, m, :], rstd[:, m:m + 1], None, ALU.mult).then_inc(xn_s, 1)
                    for j in range(16):
                        hf, k = j // 8, j % 8
                        dve.wait_ge(h_hi, hb + j + 1)
                        v.scalar_tensor_tensor(HL[:, k, 512 * hf:512 * hf + 512], bank[j % 8][:, :],
                                               gain[:, bass.ds(l * KD + k, 1)],
                                               HH[:, k, 512 * hf:512 * hf + 512].bitcast(F32),
                                               op0=ALU.mult, op1=ALU.subtract).then_inc(h_lo, 1)

                for p in range(4):
                    lo_piece(dve, p, V_N)
                norm(0, g_attn, 0)
                for p in range(4, 16):
                    lo_piece(dve, p, V_N)
                for u in range(2):
                    lo_unit(dve, u, u)

                def qk_finish(u, hf, par):
                    i = 2 * u + hf
                    dve.wait_ge(rmsq_s, i + 1)
                    v.reciprocal(RM[:, hf, :], RM[:, hf, :]).then_inc(rec_s, 1)
                    dve.wait_ge(rec_s, i + 1)
                    v.scalar_tensor_tensor(QK[:, bass.ds(u, 1), 512 * hf:512 * hf + 512].rearrange("p a n -> p (a n)"),
                                           bank[2 * par + hf][:, :], g_qk[:, bass.ds(l * QT + u, 1)], RM[:, hf, :],
                                           op0=ALU.mult, op1=ALU.mult).then_inc(qk_s, 1)

                def qk_unit_steps(u, par, first=False, last=False):
                    if not first:
                        qk_finish(u - 1, 1, 1 - par)
                    if not last:
                        lo_unit(dve, u + 2, par)
                    qk_finish(u, 0, par)

                qk_unit_steps(0, 0, first=True)
                qk_unit_steps(1, 1)
                dve.wait_ge(vs_out, 16)
                with loop(dve, 1, QT // 2 - 1) as i:
                    qk_unit_steps(2 * i, 0)
                    qk_unit_steps(2 * i + 1, 1)
                qk_unit_steps(QT - 2, 0, last=True)
                qk_unit_steps(QT - 1, 1, last=True)
                qk_finish(QT - 1, 1, 1)

                def stage_low(bd, q):
                    qt = dilated_rows(bd, T_CQ, q, P)[0:64]
                    dst = QS[0:64, 6 * (q % 2):6 * (q % 2) + 6:2, :]
                    if bd["kind"] == "c3":
                        dst = dst.rearrange("p t (r j) -> p t r j", r=2)
                    v.tensor_scalar(dst, qt, 1.0, None, ALU.mult).then_inc(staged_low, 1)

                def tmin(bd, s, gate):
                    w, off = width(bd, s)
                    G, place_ = group_buf(bd, s)
                    k = bd["kind"]
                    if gate:
                        dve.wait_ge(scored, bd["T"] + s + 1)
                    last_out = None
                    if place_ == 0 and dilated(bd):
                        last_out = 32 * bd["i"] if k == "c3" else 64 + 16 * bd["i"]
                        if needed(last_out):
                            dve.wait_ge(g_out_s[s // 6], last_out)
                    if k == "b0" and s in (6, 12):
                        last_out = 96
                        dve.wait_ge(g_out_s[0 if s == 6 else 3], last_out)
                    if gate or last_out is not None:
                        dve.sem_inc(dve_gate, 1)
                    if off:
                        v.memset(T[:, s % 4, 0:off], 0.0)
                    acc = G[:, 6 * V1 + place_:6 * V1 + place_ + 1]
                    v.tensor_tensor_reduce(out=T[:, s % 4, off:off + w], in0=table(bd, s), in1=score2[s % 2][:, 0:w],
                                           scale=1.0, scalar=3.0e38, op0=ALU.add, op1=ALU.min,
                                           accum_out=acc).then_inc(tmin_s, 1)

                seq = dict(base=0, n=0)

                def links():
                    return seq["base"] + seq["n"]

                def link(ins):
                    seq["n"] += 1
                    ins.then_inc(dve_seq, 1)

                def heads(G, n):
                    return G[:, 0:n * V1].rearrange("p (h d) -> p h d", d=V1)

                def spread(c, n):
                    return c.unsqueeze(2).broadcast_to([P, n, HD])

                NS = l * B_H
                YB, YC, YA = Y[:, 256:640], Y[:, 640:1024], Y[:, 0:256]
                gb, ga, gc0 = heads(GB[:, :], 6), heads(GA, 4), heads(GC[:, 0, :], 6)

                def max_of(i):
                    return GC[:, i, 6 * V1:6 * V1 + 6]

                def squares(fam, cols, n):
                    link(v.tensor_tensor_reduce(out=junk[:, 0:n], in0=cols, in1=cols, scale=1.0, scalar=0.0,
                                                op0=ALU.mult, op1=ALU.add, accum_out=gvar[:, fam:fam + 1]))

                def mean(fam, n):
                    v.tensor_scalar(gvare[:, fam:fam + 1], gvar[:, fam:fam + 1], 1.0 / n, EPS, ALU.mult,
                                    ALU.add).then_inc(gvar_s[fam], 1)

                def scale_y(fam, b):
                    t, n, i = FAM[fam]
                    dve.wait_ge(grstd_s[i], b + 1)
                    v.tensor_scalar(Y[:, t * P:(t + n) * P], Y[:, t * P:(t + n) * P], grstd[:, i:i + 1], None,
                                    ALU.mult).then_inc(y_s[i], 1)

                def own_finish(b, s):
                    nm, sk = GB[:, 6 * V1:6 * V1 + 6], nsink[:, bass.ds(NS, 6)]
                    if s == 10:
                        dve.wait_ge(grp_s, C_GROUPS + 3 * b + 1)
                        if needed(links()):
                            dve.wait_ge(dve_seq, links())
                        link(v.tensor_tensor(nmin[:, :], nm, sk, ALU.min))
                    elif s == 11:
                        dve.wait_ge(dve_seq, links())
                        v.tensor_tensor(shift_b[:, 0, :], nmin[:, :], nm, ALU.subtract)
                        v.tensor_tensor(shift_b[:, 1, :], nmin[:, :], sk, ALU.subtract).then_inc(b_shift, 1)
                    elif s == 13:
                        dve.wait_ge(b_fac, b + 1)
                        link(v.tensor_tensor(den[:, 0, :].unsqueeze(2), gb[:, :, HD:V1],
                                             fac_b[:, 0, :].unsqueeze(2), ALU.mult))
                    elif s == 14:
                        dve.wait_ge(dve_seq, links())
                        link(v.tensor_tensor(den[:, 0, :], den[:, 0, :], fac_b[:, 1, :], ALU.add))
                    elif s == 15:
                        dve.wait_ge(dve_seq, links())
                        link(v.reciprocal(den[:, 0, :], den[:, 0, :]))
                        dve.wait_ge(grp_s, C_GROUPS + 3 * b + 2)
                        dve.wait_ge(g_back, 32 * (b + 1))
                        link(v.tensor_tensor(nmin[:, :], max_of(0), max_of(1), ALU.min))

                def late_finish(b, s):
                    if s in (0, 1, 2, 3, 4, 5, 6, 7, 8, 9, 10, 11):
                        dve.wait_ge(dve_seq, links())
                    if s == 0:
                        link(v.tensor_tensor(coef[:, 0, :], den[:, 0, :], fac_b[:, 0, :], ALU.mult))
                        link(v.tensor_tensor(nmin[:, :], nmin[:, :], max_of(2), ALU.min))
                    elif s == 1:
                        link(v.tensor_tensor(YB.rearrange("p (g a d) -> p a g d", g=2, a=3),
                                             gb[:, :, 0:HD].rearrange("p (a g) d -> p a g d", g=2),
                                             coef[:, 0, :].rearrange("p (a g) -> p a g", g=2).unsqueeze(3)
                                             .broadcast_to([P, 3, 2, HD]), ALU.mult))
                        v.tensor_tensor(shift_c[:, :, :], nmin[:, :].unsqueeze(1).broadcast_to([P, 3, 6]),
                                        GC[:, :, 6 * V1:6 * V1 + 6], ALU.subtract).then_inc(c_shift, 1)
                    elif s == 2:
                        squares(1, YB, 384)
                    elif s == 3:
                        mean(1, 384)
                    elif s in (4, 5):
                        if s == 4:
                            dve.wait_ge(c_fac, b + 1)
                        for i in ((0,) if s == 4 else (1, 2)):
                            link(v.tensor_tensor(heads(GC[:, i, :], 6), heads(GC[:, i, :], 6),
                                                 fac_c[:, i, :].unsqueeze(2).broadcast_to([P, 6, V1]), ALU.mult))
                        if s == 4:
                            dve.wait_ge(grp_s, C_GROUPS + 3 * b + 3)
                            link(v.reciprocal(den[:, 1, 0:4].unsqueeze(2), ga[:, :, HD:V1]))
                        else:
                            link(v.tensor_tensor(YA.rearrange("p (h d) -> p h d", d=HD), ga[:, :, 0:HD],
                                                 spread(den[:, 1, 0:4], 4), ALU.mult))
                            scale_y("b", b)
                    elif s in (6, 7):
                        link(v.tensor_tensor(GC[:, 0, 0:6 * V1], GC[:, 0, 0:6 * V1], GC[:, s - 5, 0:6 * V1], ALU.add))
                        if s == 6:
                            squares(0, YA, 256)
                        else:
                            mean(0, 256)
                    elif s == 8:
                        link(v.reciprocal(den[:, 2, :].unsqueeze(2), gc0[:, :, HD:V1]))
                    elif s == 9:
                        link(v.tensor_tensor(YC.rearrange("p (h d) -> p h d", d=HD), gc0[:, :, 0:HD],
                                             spread(den[:, 2, :], 6), ALU.mult))
                        scale_y("a", b)
                    elif s == 10:
                        dve.sem_inc(c_merged, 1)
                        squares(2, YC, 384)
                    elif s == 11:
                        mean(2, 384)
                    elif s == 13:
                        scale_y("c", b)

                def copy_unit(bd, idx, ev, b_now):
                    dve.wait_ge(pt_made, bd["U"] + idx + 1)
                    if ev[1] == "p":
                        c0, w = ev[2][0][0], P * len(ev[2])
                        v.tensor_copy(PT[:, ev[0] % 4, c0:c0 + w], bank[4][:, 0:w]).then_inc(pt_copied[0], 1)
                    else:
                        fam, c0, n = ev[2]
                        t0_ = Y_TILE[FAM[fam][0] + c0]
                        v.tensor_scalar(QK[:, t0_:t0_ + n, bass.ds(b_now * P, P)],
                                        bank[4][:, 0:n * P].rearrange("p (t n) -> p t n", n=P), 1.0, None,
                                        ALU.mult).then_inc(pt_copied[0], 1)

                def dve_body(bd, nxt):
                    b = bd["i"]
                    for s in range(n_tiles(bd)):
                        even = [(idx, ev) for idx, ev in enumerate(events(bd)) if ev[0] == s and idx % 2 == 0]
                        for idx, ev in even:
                            copy_unit(bd, idx, ev, b - 1)
                        if s + 2 < n_tiles(bd):
                            tmin(bd, s + 2, not even)
                        elif nxt is not None:
                            if s + 2 == n_tiles(bd) and nxt["kind"] in ("c2", "b0") and bd["kind"] != nxt["kind"]:
                                dve.wait_ge(tab_c if nxt["kind"] == "c2" else tab_ab, 32)
                                dve.sem_inc(dve_gate, 1)
                            tmin(nxt, s + 2 - n_tiles(bd), not even)
                        if dilated(bd):
                            if s % 6 == 2:
                                if s < 18:
                                    stage_low(bd, s // 6 + 1)
                                elif dilated(nxt):
                                    stage_low(nxt, 0)
                            continue
                        own_finish(b, s)
                        if bd["kind"] != "b0":
                            late_finish(b - 1, s)

                dve.wait_ge(tab_c3, 16)
                dve.sem_inc(dve_gate, 1)
                dve.wait_ge(qk_s, 2 * QT)
                dve.sem_inc(dve_gate, 1)
                stage_low(plan[0][0], 0)
                tmin(plan[0][0], 0, True)
                tmin(plan[0][0], 1, True)
                LINKS_OWN, LINKS_LATE = 5, 15

                def dve_round(bd, nxt, before):
                    seq["n"] = 0
                    seq["base"] = 0
                    if not dilated(bd) and bd["kind"] != "b0":
                        seq["base"] = (LINKS_OWN + LINKS_LATE) * bd["i"] - LINKS_LATE
                    dve_body(bd, nxt)
                    if not dilated(bd):
                        assert seq["n"] == LINKS_OWN + (LINKS_LATE if bd["kind"] != "b0" else 0), seq

                run(dve, dve_round)
                seq["base"], seq["n"] = (LINKS_OWN + LINKS_LATE) * MT - LINKS_LATE, 0
                tail = dict(plan[-1][0], U=UNITS - len(Y_TAIL))
                for s in range(14):
                    late_finish(MT - 1, s)
                for idx, ev in enumerate(Y_TAIL):
                    if idx % 2 == 0:
                        copy_unit(tail, idx, ev, MT - 1)
                for p in range(16, 20):
                    lo_piece(dve, p)

                for f in range(KD):
                    dve.wait_ge(h_hi, 16 + f + 1)
                    v.scalar_tensor_tensor(HL[:, f, :], QK[:, Y_TILE[f], :], g_out[:, bass.ds(l * KD + f, 1)],
                                           HH[:, f, :].bitcast(F32), op0=ALU.mult, op1=ALU.subtract).then_inc(h_lo, 1)
                for u in range(2):
                    lo_unit(dve, QT + u, u)
                for p in range(20, 27):
                    lo_piece(dve, p)

                def add_out(ch):
                    for m in range(MT):
                        dve.wait_ge(moved, 15 * ch + 8 + m)
                        xs = X[:, m, 512 * (ch - 2):512 * (ch - 1)]
                        v.tensor_tensor(xs, xs, bank[m][:, :], ALU.add).then_inc(x_add, 1)

                dve.wait_ge(x_back, 16)
                add_out(2)
                for p in range(27, 35):
                    lo_piece(dve, p)
                add_out(3)
                norm(1, g_ffn, 24)
                lo_piece(dve, 35)

                def gate_up(j, par, cc, more=True):
                    u = QT + 2 * j
                    if more:
                        lo_unit(dve, u + 2, 0)
                        lo_unit(dve, u + 3, 1)
                    for hf in range(2):
                        dve.wait_ge(stat, 2 * u + 2 + hf + 1)
                        dve.wait_ge(silu_s, 2 * j + hf + 1)
                        if needed(2 * (j - 1) + hf + 1):
                            dve.wait_ge(g_lo, 2 * (j - 1) + hf + 1)
                        v.tensor_tensor(GT[:, hf, :], SI[:, hf, :], bank[2 + hf][:, :], ALU.mult).then_inc(mul_s, 1)
                    for hf in range(2):
                        dve.wait_ge(g_hi, 2 * j + hf + 1)
                        v.tensor_tensor(GL[:, par, cc, 512 * hf:512 * hf + 512], GT[:, hf, :],
                                        GH[:, par, cc, 512 * hf:512 * hf + 512].bitcast(F32),
                                        ALU.subtract).then_inc(g_lo, 1)

                def down(g, more=True):
                    for c in range(2):
                        for m in range(MT):
                            dve.wait_ge(moved, 60 + 16 * g + 8 * c + m + 1)
                            xs = X[:, m, 512 * c:512 * c + 512]
                            v.tensor_tensor(xs, xs, bank[4 + m % 4][:, :], ALU.add).then_inc(x_add, 1)
                        for i in range(2):
                            if more:
                                dve.wait_ge(piece_hi, 32 + 4 * (g + 1) + 2 * c + i + 1)
                                v.tensor_tensor(PL[:, 2 * c + i, :], PR[:, 2 * c + i, :],
                                                PH[:, 2 * c + i, :].bitcast(F32), ALU.subtract).then_inc(piece_lo, 1)

                gate_up(0, 0, 0)
                gate_up(1, 0, 1)
                with loop(dve, 0, NG // 2 - 1) as i:
                    gate_up(4 * i + 2, 1, 0)
                    gate_up(4 * i + 3, 1, 1)
                    down(2 * i)
                    gate_up(4 * i + 4, 0, 0)
                    gate_up(4 * i + 5, 0, 1)
                    down(2 * i + 1)
                gate_up(NCH - 4, 1, 0)
                gate_up(NCH - 3, 1, 1)
                down(NG - 3)
                gate_up(NCH - 2, 0, 0)
                gate_up(NCH - 1, 0, 1, more=False)
                down(NG - 2)
                down(NG - 1, more=False)

            @block.gpsimd
            def _(pool):
                g = nc.gpsimd
                pool.wait_ge(xt_s, 16)
                g.memset(VS[:, :, :, HD:V1], 1.0).then_inc(v_ones, 1)
                pool.wait_ge(x_stored, 16)
                pool.wait_ge(xn_s, 8)
                g.memset(VA[:, :, :, HD:V1], 1.0)
                g.memset(VB[:, :, :, HD:V1], 1.0).then_inc(v_ones, 1)
                pool.wait_ge(stat, 2 * QT)
                g.memset(VC[0:64, 0, :, :], 0.0).then_inc(v_ones, 1)

                def carrier():
                    pool.sem_inc(pool_gate, 1)

                def stage(bd, before, q, after_powers):
                    k, i = bd["kind"], bd["i"]
                    nh = 4 if q == 2 and not dilated(bd) else 6
                    q2 = q % 2 if dilated(bd) else q
                    if dilated(bd) and q >= 2:
                        pool.wait_ge(scored, bd["T"] + 6 * (q - 1))
                    elif before is not None:
                        last = 6 * q + 18 if dilated(before) else 6 * q + nh
                        pool.wait_ge(scored, before["T"] + min(last, n_tiles(before)))
                    done = bd["Q"] + 2 * q
                    if needed(done):
                        pool.wait_ge(staged, done)
                    after_powers()
                    carrier()
                    if dilated(bd):
                        dst = QS[64:128, 6 * q2 + 1:6 * q2 + 7:2, :]
                        kd = KS[:, q2, :, :]
                        if k == "c3":
                            dst = dst.rearrange("p t (r j) -> p t r j", r=2)
                            kd = KS[:, q2, :, 0:128].rearrange("p t (r j) -> p t r j", r=2)
                        g.tensor_copy(dst, dilated_rows(bd, T_CQ, q, P)[64:128]).then_inc(staged, 1)
                        pool.wait_ge(staged, done + 1)
                        carrier()
                        g.tensor_copy(kd, dilated_rows(bd, T_CK, q, 192)).then_inc(staged, 1)
                    else:
                        t0_ = (T_BQ, T_CQ, T_AQ)[q]
                        qt = QK[:, t0_:t0_ + nh // 2, bass.ds(i * P, P)]
                        for par in (1, 0):
                            g.tensor_copy(QS[64 * par:64 * par + 64, 6 * q + par:6 * q + nh:2, :],
                                          qt[64 * par:64 * par + 64]).then_inc(staged, 1)

                def mean_powers(fam, b, copies):
                    pool.wait_ge(gvar_s[fam], b + 1)
                    pool.wait_ge(staged, copies)
                    carrier()
                    g.tensor_tensor(grstd[:, fam:fam + 1], gvare[:, fam:fam + 1], neghalf[:, :],
                                    ALU.pow).then_inc(grstd_s[fam], 1)

                def pool_body(bd, nxt, before):
                    b = bd["i"]
                    if dilated(bd):
                        for q in range(4):
                            stage(bd, before, q, (lambda: pool.wait_ge(v_ones, 3)) if q == 0 else (lambda: None))
                        return
                    powers = bd["kind"] not in ("b0", "b1")
                    if powers:
                        mean_powers(1, b - 2, bd["Q"])
                    stage(bd, before, 0, (lambda: pool.wait_ge(grstd_s[1], b - 1)) if powers else (lambda: None))
                    if powers:
                        mean_powers(0, b - 2, bd["Q"] + 2)
                    stage(bd, before, 1, (lambda: pool.wait_ge(grstd_s[0], b - 1)) if powers else (lambda: None))
                    if powers:
                        mean_powers(2, b - 2, bd["Q"] + 4)
                    stage(bd, before, 2, (lambda: pool.wait_ge(grstd_s[2], b - 1)) if powers else (lambda: None))

                pool.wait_ge(qk_s, 2 * QT)
                run(pool, pool_body)
                for b in (MT - 2, MT - 1):
                    for fam in (1, 0, 2):
                        mean_powers(fam, b, plan[-1][0]["Q"] + 6)

            @block.tensor
            def _(pe):
                t = nc.tensor

                def three(dst, sh, sl, mh, ml, start, stop):
                    t.matmul(dst, sh, mh, start=start, stop=False)
                    t.matmul(dst, sh, ml, start=False, stop=False)
                    return t.matmul(dst, sl, mh, start=False, stop=stop)

                def norm(n, hb):
                    for j in range(16):
                        hf, k = j // 8, j % 8
                        if k == 0:
                            pe.wait_ge(xn_s, 8 * n + 4 * hf + 4)
                        if hf:
                            pe.wait_ge(h_lo, hb + j - 8 + 1)
                        elif n and k >= 4:
                            pe.wait_ge(x_add, 8 + k + 1)
                        for i in range(4):
                            last = t.transpose(bank[j % 8][:, P * i:P * i + P], XN[:, 4 * hf + i, P * k:P * k + P], ident[:, :])
                        last.then_inc(xt_s, 1)

                def moving(ch, n, hb, bank_wait):
                    for k in range(KD):
                        p = 8 * ch + k
                        pe.wait_ge(piece_lo, p + 1)
                        for m in range(MT):
                            if hb is not None and (m == 0 or hb == 8 and k == 0):
                                pe.wait_ge(h_lo, hb + max(k, m) + 1)
                            if k == 0 and bank_wait:
                                bank_wait(m)
                            ins = three(bank[m][:, 0:n], HH[:, k, P * m:P * m + P], HL[:, k, P * m:P * m + P],
                                        PH[:, p % 4, 0:n], PL[:, p % 4, 0:n], k == 0, k == KD - 1)
                            if k == KD - 1 or m == MT - 1:
                                ins.then_inc(moved, 1)

                norm(0, 0)
                moving(0, V_N, 8, None)
                moving(1, V_N, None, lambda m: pe.wait_ge(v_stored, m + 1))

                def half_unit(u, slot, hf, dst):
                    for k in range(KD):
                        last = three(dst, UH[:, slot, k, :], UL[:, slot, k, :], HH[:, k, 512 * hf:512 * hf + 512],
                                     HL[:, k, 512 * hf:512 * hf + 512], k == 0, k == KD - 1)
                    last.then_inc(stat, 1)

                def square_sums(i, slot):
                    pe.wait_ge(sq_s, i + 1)
                    if needed(i - 1):
                        pe.wait_ge(rmsq_s, i - 1)
                    t.matmul(bank[4 + slot][:, :], bones[:, :], SQ[:, slot, :], start=True, stop=True).then_inc(ss_s, 1)

                def qk_unit_steps(u, par, first=False):
                    pe.wait_ge(unit_lo, u + 1)
                    if needed(2 * u - 3):
                        pe.wait_ge(qk_s, 2 * u - 3)
                    half_unit(u, par, 0, bank[2 * par][:, :])
                    if not first:
                        square_sums(2 * u - 1, 1)
                    if needed(2 * u - 2):
                        pe.wait_ge(qk_s, 2 * u - 2)
                    half_unit(u, par, 1, bank[2 * par + 1][:, :])
                    square_sums(2 * u, 0)

                pe.wait_ge(v_stored, 16)
                qk_unit_steps(0, 0, first=True)
                qk_unit_steps(1, 1)
                with loop(pe, 1, QT // 2) as i:
                    qk_unit_steps(2 * i, 0)
                    qk_unit_steps(2 * i + 1, 1)
                square_sums(2 * QT - 1, 1)

                def score(bd, s):
                    pe.wait_ge(staged, bd["Q"] + 2 * (s // 6 + 1))
                    if dilated(bd):
                        pe.wait_ge(staged_low, bd["G"] + s // 6 + 1)
                    slot = s % 2
                    if needed(bd["T"] + s - 1):
                        pe.wait_ge(tmin_s, bd["T"] + s - 1)
                    for j, kk in enumerate(keys(bd, s)):
                        w = kk.shape[-1]
                        last = t.matmul(score2[slot][:, 512 * j:512 * j + w], QS[:, s % 12 if dilated(bd) else s, :], kk, start=True, stop=True)
                    last.then_inc(scored, 1)

                def unit(bd, idx, ev, b_now):
                    dst = bank[4 + idx % 2]
                    if ev[1] == "p":
                        pe.wait_ge(exp_s, bd["T"] + ev[0] + 1)
                        srcs = [T[:, ev[0] % 4, c:c + P] for c, _ in ev[2]]
                    else:
                        fam, c0, n = ev[2]
                        t0_, _, fi = FAM[fam]
                        pe.wait_ge(y_s[fi], b_now + 1)
                        srcs = [Y[:, (t0_ + c0 + i) * P:(t0_ + c0 + i + 1) * P] for i in range(n)]
                    if needed(bd["half_U"] + idx // 2):
                        pe.wait_ge(pt_copied[idx % 2], bd["half_U"] + idx // 2)
                    for i, src in enumerate(srcs):
                        last = t.transpose(dst[0:src.shape[-1], P * i:P * i + P], src, ident[:, :])
                    last.then_inc(pt_made, 1)

                def weigh(bd, s):
                    k = bd["kind"]
                    for idx in tile_units(bd, s):
                        pe.wait_ge(pt_copied[idx % 2], bd["half_U"] + idx // 2 + 1)
                    if s % 6 == 0:
                        if dilated(bd):
                            pe.wait_ge(vr_in[s // 6], (32 if k == "c3" else 16) * (bd["i"] + 1) + (64 if k == "c2" else 0))
                        if k == "b0" and s == 6:
                            pe.wait_ge(vc_in, 48)
                            pe.wait_ge(v_ones, 3)
                        stored = bd["G"] + s // 6 - 1 + (1 if s == 0 and not dilated(bd) and k != "b0" else 0)
                        if needed(stored):
                            pe.wait_ge(grp_s, stored)
                    place_ = group_buf(bd, s)[1]
                    chs = chunks_of(bd, s)
                    for c, (col, n) in enumerate(chs):
                        last = t.matmul(group_bank(bd, s)[:, place_ * V1:place_ * V1 + V1],
                                        PT[0:n, s % 4, P * c:P * c + P], values(bd, s, c, n),
                                        start=(c == 0), stop=(c == len(chs) - 1))
                    last.then_inc(pv_s, 1)

                def pe_body(bd, nxt, prev):
                    evs = events(bd)
                    nt = n_tiles(bd)
                    for s in range(nt):
                        if s + 2 < nt:
                            score(bd, s + 2)
                        elif nxt is not None:
                            score(nxt, s + 2 - nt)
                        for idx, ev in enumerate(evs):
                            if ev[0] == s:
                                unit(bd, idx, ev, bd["i"] - 1)
                        if s >= 2:
                            weigh(bd, s - 2)
                        elif prev is not None:
                            weigh(prev, n_tiles(prev) + s - 2)

                score(plan[0][0], 0)
                score(plan[0][0], 1)
                run(pe, pe_body)
                weigh(plan[-1][0], 14)
                weigh(plan[-1][0], 15)
                tail = dict(plan[-1][0], U=UNITS - len(Y_TAIL), half_U=(UNITS - len(Y_TAIL)) // 2)
                for idx, ev in enumerate(Y_TAIL):
                    unit(tail, idx, ev, MT - 1)

                moving(2, 512, 16, None)
                moving(3, 512, None, lambda m: pe.wait_ge(x_add, m + 1))
                norm(1, 24)
                pe.wait_ge(h_lo, 40)

                def gate_up(j):
                    u = QT + 2 * j
                    for gu in range(2):
                        pe.wait_ge(unit_lo, u + gu + 1)
                        for hf in range(2):
                            if needed(2 * (j - 1) + hf + 1):
                                pe.wait_ge(mul_s if gu else silu_s, 2 * (j - 1) + hf + 1)
                            half_unit(u + gu, gu, hf, bank[2 * gu + hf][:, :])

                def down(g, par):
                    pe.wait_ge(g_lo, 4 * g + 4)
                    for c in range(2):
                        pe.wait_ge(piece_lo, 32 + 4 * g + 2 * c + 2)
                        for m in range(MT):
                            pe.wait_ge(x_add, 16 + 16 * g + 8 * c + m - 4 + 1)
                            for kk in range(2):
                                i = 2 * c + kk
                                last = three(bank[4 + m % 4][:, :], GH[:, par, kk, P * m:P * m + P],
                                             GL[:, par, kk, P * m:P * m + P], PH[:, i, :], PL[:, i, :], kk == 0, kk == 1)
                            last.then_inc(moved, 1)

                gate_up(0)
                gate_up(1)
                with loop(pe, 0, NG // 2) as i:
                    gate_up(4 * i + 2)
                    gate_up(4 * i + 3)
                    down(2 * i, 0)
                    gate_up(4 * i + 4)
                    gate_up(4 * i + 5)
                    down(2 * i + 1, 1)
                down(NG - 1, 0)

            programs.close()
            nc.all_engine_barrier(sems_to_clear=range(sems[0].num, sems[-1].num + 1))

        with ExitStack() as end:
            out_s = end.enter_context(nc.semaphore("out_written"))
            block = end.enter_context(nc.Block())

            @block.sync
            def _(sp):
                sp.dma_start(outr, X[:, :, :]).then_inc(out_s, 16)
                sp.wait_ge(out_s, 16)


def kernel(x, attn_norm, w_in, qk_gain, rpb, sink, out_gain, w_out, ffn_norm, w_gu, w_down):
    import numpy as np
    import concourse.bacc as bacc
    from concourse import mybir as mb
    from concourse.bass_utils import run_bass_kernel_spmd as run

    nc = bacc.Bacc("TRN2", target_bir_lowering=False, num_devices=1, dynamic_dma_scratch_size=1024)
    rpb = np.asarray(rpb)
    padded = np.zeros(rpb.shape[:3] + (127,), rpb.dtype)
    padded[..., 48:79] = rpb[..., ::-1]
    ins = dict(x=x, attn_norm=attn_norm, w_in=w_in, qk_gain=qk_gain, rpb=padded, sink=sink, out_gain=out_gain,
               w_out=w_out, ffn_norm=ffn_norm, w_gu=w_gu, w_down=w_down)
    arrays, args = {}, []
    for name, a in ins.items():
        a = np.ascontiguousarray(a)
        arrays[f"in_{name}"] = a
        args.append(nc.dram_tensor(f"in_{name}", a.shape, mb.dt.from_np(a.dtype), kind="ExternalInput").ap())
    args.append(nc.dram_tensor("result", x.shape, mb.dt.float32, kind="ExternalOutput").ap())
    build_program(nc, *args)
    return run(nc, [arrays], core_ids=[0]).results[0]["result"]
```

```python
from contextlib import ExitStack

import concourse.bass as bass
from concourse import mybir

F32, F32R = mybir.dt.float32, mybir.dt.float32r
ALU = mybir.AluOpType
ACT = mybir.ActivationFunctionType
P = 128


def build_program(nc, x, attn_norm, w_in, qk_gain, rpb, sink, out_gain, w_out, ffn_norm, w_gu, w_down, out):
    depth, D = attn_norm.shape
    S = x.shape[1]
    MT = S // P
    KD = D // P
    HID = w_down.shape[1]
    HD = 64
    V1 = HD + 1
    A_H, B_H, C_H = 4, 6, 6
    GW = 64
    EPS = 1e-6
    BIG, BIGD = 1e30, 1e34
    SLOPES = [2.0 ** (-8.0 * (i + 1) / (B_H + C_H)) for i in range(B_H + C_H)]
    B_ORDER = [0, 3, 1, 4, 2, 5]
    AQ, AV, BQ, BV, CQ, CV = 0, 512, 768, 1280, 1408, 2176
    T_CQ, T_CK, T_BQ, T_BK, T_AQ, T_AK = 0, 3, 6, 9, 10, 12
    QT = 14
    Y_TILE = [10, 11, 6, 7, 8, 0, 1, 2]
    NCH = HID // P
    NG = NCH // 2
    GR = 6 * V1 + 6
    TA_S = 23

    xr = x.rearrange("b (m p) d -> p (b m) d", p=P)
    outr = out.rearrange("b (m p) d -> p (b m) d", p=P)
    dram = lambda n, s: nc.dram_tensor(n, s, F32, kind="Internal").ap()
    x_res = dram("x_res", (S, D)).rearrange("(m p) d -> p m d", p=P)
    v_c = dram("v_c", (S, C_H * V1))
    g_dil = [dram("g_d4", (S, GR)), dram("g_d16", (S, GR))]
    distances = dram("distances", (P, 384 + 256 + 128))

    ctx = ExitStack()
    with ctx:
        base = -(-nc.sbuf_base // 64) * 64
        place = {}
        for name, size in (("CONST", 4096), ("H", 65536), ("R", 24576), ("U", 24576),
                           ("X", 32768), ("F", 57344), ("W", 10240), ("Q", 8192)):
            place[name] = base
            base += size
        at = dict(place)

        def sb(name, shape, dt, region, offset=None):
            if offset is None:
                offset = at[region] - place[region]
                n = 4
                for d in shape[1:]:
                    n *= d
                at[region] += -(-n // 32) * 32
            return nc.alloc_sbuf_tensor_at(name, shape, dt, offset=place[region] + offset)

        ident = sb("ident", [P, P], F32, "CONST")
        bones = sb("bones", [P, P], F32, "CONST")
        g_attn = sb("g_attn", [P, depth * KD], F32, "CONST")
        g_ffn = sb("g_ffn", [P, depth * KD], F32, "CONST")
        g_out = sb("g_out", [P, depth * KD], F32, "CONST")
        g_raw = sb("g_raw", [P, depth * 6], F32, "CONST")
        g_qk = sb("g_qk", [P, depth * QT], F32, "CONST")
        eps = sb("eps", [P, 1], F32, "CONST")
        neghalf = sb("neghalf", [P, 1], F32, "CONST")
        col_mask = sb("col_mask", [P, GW], F32, "CONST")
        sinks = sb("sinks", [P, depth * B_H], F32, "CONST")
        nsink = sb("nsink", [P, depth * B_H], F32, "CONST")
        warm = sb("warm", [P, 1], F32, "CONST")
        sumsq = sb("sumsq", [P, MT], F32, "CONST")
        sumsq_left = sb("sumsq_left", [P, MT], F32, "CONST")
        rms = sb("rms", [P, MT], F32, "CONST")
        rstd = sb("rstd", [P, MT], F32, "CONST")
        nmin = sb("nmin", [P, 6], F32, "CONST")
        shift_b = sb("shift_b", [P, 2, 6], F32, "CONST")
        shift_c = sb("shift_c", [P, 3, 6], F32, "CONST")
        fac_b = sb("fac_b", [P, 2, 6], F32, "CONST")
        fac_c = sb("fac_c", [P, 3, 6], F32, "CONST")
        den = sb("den", [P, 3, 6], F32, "CONST")
        coef = sb("coef", [P, 3, 6], F32, "CONST")
        gvar = sb("gvar", [P, 3], F32, "CONST")
        gvare = sb("gvare", [P, 3], F32, "CONST")
        grstd = sb("grstd", [P, 3], F32, "CONST")

        HH = sb("HH", [P, KD, S], F32R, "H", 0)
        HL = sb("HL", [P, KD, S], F32R, "H", 32768)
        TA = sb("TA", [P, A_H, TA_S, GW], F32, "H")
        RM_LAST = sb("RM_LAST", [P, 2, 512], F32, "H", 4 * A_H * TA_S * GW)
        TB = sb("TB", [P, B_H, 384], F32, "H")
        VC = sb("VC", [P, MT + 1, C_H, V1], F32, "H")
        VR = sb("VR", [P, 4, 2, C_H * V1], F32, "H")
        junk = sb("junk", [P, 384], F32, "H")
        PR = sb("PR", [P, 4, 512], F32, "R")
        PH = sb("PH", [P, 4, 512], F32R, "R")
        PL = sb("PL", [P, 4, 512], F32R, "R")
        PT = sb("PT", [P, 4, 640], F32, "R", 8192)
        UR = sb("UR", [P, 2, KD, P], F32, "U")
        UH = sb("UH", [P, 2, KD, P], F32R, "U")
        UL = sb("UL", [P, 2, KD, P], F32R, "U")
        TC3 = sb("TC3", [P, C_H, 128], F32, "R", 18432)
        TC2 = sb("TC2", [P, C_H, 256], F32, "U", 8192 + 3072)
        TC1 = sb("TC1", [P, C_H, 256], F32, "U", 8192 + 3072 + 6144)
        X = sb("X", [P, MT, D], F32, "X", 0)
        VA = sb("VA", [P, MT, A_H, V1], F32, "X")
        VB = sb("VB", [P, MT, 2, V1], F32, "X")
        GB = sb("GB", [P, GR], F32, "X")
        G4 = sb("G4", [P, 4, GR], F32, "X")
        GC, GA = G4[:, 0:3, :], G4[:, 3, :]
        Y = sb("Y", [P, D], F32, "X")
        KS = sb("KS", [P, 2, 3, 192], F32, "X")
        DIST = sb("DIST", [P, 768], F32, "X")
        QK = sb("QK", [P, QT, S], F32, "F", 0)
        VS = sb("VS", [P, MT, C_H, V1], F32, "F", 40960)
        XN = sb("XN", [P, MT, D], F32, "F", 24576)
        GH = sb("GH", [P, 2, 2, S], F32R, "F", 0)
        GL = sb("GL", [P, 2, 2, S], F32R, "F", 16384)
        D0 = sb("D0", [P, 768], F32, "F", 0)
        D_N = sb("D_N", [P, 384], F32, "F", 4096)
        SQ = sb("SQ", [P, 2, 512], F32, "W", 0)
        RM = sb("RM", [P, 2, 512], F32, "W", 4096)
        SI = sb("SI", [P, 2, 512], F32, "W", 0)
        GT = sb("GT", [P, 2, 512], F32, "W", 4096)
        T = sb("T", [P, 4, 640], F32, "W", 0)
        QS = sb("QS", [P, 16, P], F32, "Q")

        psum = ctx.enter_context(nc.psum_tensor("psum", [P, 8 * 512], F32))
        bank = [psum[:, 512 * i:512 * i + 512] for i in range(8)]
        score2 = [psum[:, 1024 * i:1024 * i + 1024] for i in range(2)]

        with ExitStack() as setup:
            sem = lambda n: setup.enter_context(nc.semaphore(n))
            x_in, gains_in, dist_out, pool_seq = sem("x_in"), sem("gains_in"), sem("dist_out"), sem("pool_seq")
            block = setup.enter_context(nc.Block())
            dist_made = sem("dist_made")

            @block.sync
            def _(sp):
                sp.dma_start(X[:, :, :], xr).then_inc(x_in, 16)
                sp.wait_ge(dist_made, 1)
                sp.dma_start(distances, D0[:, :]).then_inc(dist_out, 16)
                sp.wait_ge(dist_out, 16)
                sp.wait_ge(x_in, 16)

            @block.scalar
            def _(act):
                with nc.allow_non_contiguous_dma(reason="gain vectors, a few KB"):
                    act.dma_start(g_attn[:, :].rearrange("p (l k) -> p l k", l=depth),
                                  attn_norm.rearrange("l (k p) -> p l k", p=P)).then_inc(gains_in, 16)
                    act.dma_start(g_ffn[:, :].rearrange("p (l k) -> p l k", l=depth),
                                  ffn_norm.rearrange("l (k p) -> p l k", p=P)).then_inc(gains_in, 16)
                    act.dma_start(g_out[:, :].rearrange("p (l k) -> p l k", l=depth),
                                  out_gain.rearrange("l (k p) -> p l k", p=P)).then_inc(gains_in, 16)
                    for half in range(2):
                        act.dma_start(g_raw[64 * half:64 * half + 64, :],
                                      qk_gain.rearrange("l f q d -> d (l f q)")).then_inc(gains_in, 16)
                    act.dma_start(sinks[:, :], sink.rearrange("l h -> (l h)").partition_broadcast(P)).then_inc(gains_in, 16)
                act.wait_ge(gains_in, 96)

            @block.gpsimd
            def _(pool):
                count = [0]

                def step(ins):
                    count[0] += 1
                    ins.then_inc(pool_seq, 1)
                    pool.wait_ge(pool_seq, count[0])

                g = nc.gpsimd
                step(g.memset(QS[:, :, :], 0.0))
                step(g.memset(ident[:, :], 0.0))
                step(g.affine_select(out=ident[:, :], in_=ident[:, :], compare_op=ALU.not_equal, fill=1.0,
                                     base=0, pattern=[[-1, P]], channel_multiplier=1))
                step(g.memset(bones[:, :], 0.0))
                step(g.memset(bones[0:64, 0:64], 1.0))
                step(g.memset(bones[64:128, 64:128], 1.0))
                step(g.memset(eps[:, :], EPS))
                step(g.memset(neghalf[:, :], -0.5))
                step(g.memset(col_mask[:, :], 0.0))
                for half in range(2):
                    low, high = col_mask[64 * half:64 * half + 64, 0:48], col_mask[64 * half:64 * half + 64, 16:64]
                    step(g.affine_select(out=low, in_=low, compare_op=ALU.is_ge, fill=BIG, base=8,
                                         pattern=[[1, 48]], channel_multiplier=-1))
                    step(g.affine_select(out=high, in_=high, compare_op=ALU.is_ge, fill=BIG, base=-9,
                                         pattern=[[-1, 48]], channel_multiplier=1))
                for first, w, hw in ((0, 384, 128), (384, 256, 64), (640, 128, 0)):
                    dist = D0[:, first:first + w]
                    step(g.iota(dist, pattern=[[1, w]], base=-hw, channel_multiplier=-1,
                                allow_small_or_imprecise_dtypes=True))
                    step(g.tensor_scalar(D_N[:, 0:w], dist, -1.0, None, ALU.mult))
                    step(g.affine_select(out=dist, in_=dist, compare_op=ALU.is_ge, fill=0.0,
                                         base=-hw, pattern=[[1, w]], channel_multiplier=-1))
                    step(g.affine_select(out=D_N[:, 0:w], in_=D_N[:, 0:w], compare_op=ALU.is_ge, fill=0.0,
                                         base=hw, pattern=[[-1, w]], channel_multiplier=1))
                    step(g.tensor_tensor(dist, dist, D_N[:, 0:w], ALU.add))
                    if hw:
                        step(g.affine_select(out=dist, in_=dist, compare_op=ALU.is_ge, fill=BIGD,
                                             base=0, pattern=[[1, w]], channel_multiplier=-1))
                        step(g.affine_select(out=dist, in_=dist, compare_op=ALU.is_ge, fill=BIGD,
                                             base=2 * hw, pattern=[[-1, w]], channel_multiplier=1))
                step(g.memset(D0[0:64, 704:768], BIGD))
                g.memset(D0[64:128, 640:704], BIGD).then_inc(dist_made, 1)

            @block.vector
            def _(dve):
                v = nc.vector
                v.memset(T[:, :, :], 0.0)
                dve.wait_ge(gains_in, 96)
                v.tensor_scalar(nsink[:, :].rearrange("p (l a g) -> p l a g", l=depth, a=3),
                                sinks[:, :].rearrange("p (l g a) -> p l a g", l=depth, a=3), -1.0, None, ALU.mult)
                for l in range(depth):
                    for fam, q0, nq, nk in ((0, T_AQ, 2, 2), (1, T_BQ, 3, 1), (2, T_CQ, 3, 3)):
                        for i in range(nq + nk):
                            src = g_raw[:, l * 6 + fam * 2 + (i >= nq):l * 6 + fam * 2 + (i >= nq) + 1]
                            v.tensor_scalar(g_qk[:, l * QT + q0 + i:l * QT + q0 + i + 1], src,
                                            -(HD ** -0.5) if i < nq else 1.0, None, ALU.mult)

        with nc.Fori(0, depth) as l, ExitStack() as layer:
            sems = []

            def sem(name):
                sems.append(layer.enter_context(nc.semaphore(name)))
                return sems[-1]

            x_stored, x_back = sem("x_stored"), sem("x_back")
            piece_raw = [sem(f"piece_raw{i}") for i in range(4)]
            unit_raw = [sem(f"unit_raw{i}") for i in range(2)]
            piece_hi, piece_lo, unit_hi, unit_lo = sem("piece_hi"), sem("piece_lo"), sem("unit_hi"), sem("unit_lo")
            moved = sem("moved")
            stat = sem("stat")
            sumsq_act, sumsq_dve, rms_s, rstd_s = sem("sumsq_act"), sem("sumsq_dve"), sem("rms_s"), sem("rstd_s")
            xn_act, xn_dve = sem("xn_act"), sem("xn_dve")
            xt_s, h_hi, h_lo = sem("xt_s"), sem("h_hi"), sem("h_lo")
            v_stored, v_ones, vs_out = sem("v_stored"), sem("v_ones"), sem("vs_out")
            sq_s, ss_s, rmsq_s, rec_s, qk_s = sem("sq_s"), sem("ss_s"), sem("rmsq_s"), sem("rec_s"), sem("qk_s")
            x_add = sem("x_add")
            silu_s, mul_s, g_hi, g_lo = sem("silu_s"), sem("mul_s"), sem("g_hi"), sem("g_lo")
            dist_in, table_s, vc_in = sem("dist_in"), sem("table_s"), sem("vc_in")
            rpb_in, ta_sub, ta_made = sem("rpb_in"), sem("ta_sub"), sem("ta_made")
            vr_in = [sem(f"vr_in{i}") for i in range(4)]
            g_out_s = [sem(f"g_out{i}") for i in range(4)]
            g_back = sem("g_back")
            staged, scored, tmin_s, exp_s = sem("staged"), sem("scored"), sem("tmin_s"), sem("exp_s")
            pt_made, pv_s, grp_s = sem("pt_made"), sem("pv_s"), sem("grp_s")
            pt_copied = [sem("pt_copied_dve"), sem("pt_copied_act")]
            staged_low = sem("staged_low")
            b_shift, b_fac, c_shift, c_fac, c_merged = (sem(n) for n in ("b_shift", "b_fac", "c_shift", "c_fac", "c_merged"))
            gvar_s, grstd_s, y_s = ([sem(f"{n}_{f}") for f in "abc"] for n in ("gvar_s", "grstd_s", "y_s"))
            dve_seq = sem("dve_seq")
            tail_squares, early_hi = sem("tail_squares"), sem("early_hi")
            dve_gate, pool_gate = sem("dve_gate"), sem("pool_gate")

            def needed(value):
                return not isinstance(value, int) or value > 0

            def loop(eng, n0, n1):
                return eng.Fori(n0, n1)

            programs = ExitStack()
            block = programs.enter_context(nc.Block())

            def raw_need(p):
                return 16 * (p // 4 + 1) + 16 * max(0, min(2, p // 4 - 1))

            def piece_done(p):
                if p < 0:
                    return 0
                if p < 32:
                    ch, k = p // 8, p % 8
                    return 15 * ch + (k + 1 if k < 7 else 15)
                g, c = (p - 32) // 4, (p - 32) % 4 // 2
                return 60 + 16 * g + 8 * c + 8

            def hi_piece(act, p, n=512):
                act.wait_ge(piece_raw[p % 4], raw_need(p))
                if needed(piece_done(p - 4)):
                    act.wait_ge(moved, piece_done(p - 4))
                nc.scalar.activation(PH[:, p % 4, 0:n], PR[:, p % 4, 0:n], ACT.Copy).then_inc(piece_hi, 1)

            def lo_piece(dve, p, n=512):
                dve.wait_ge(piece_hi, p + 1)
                nc.vector.tensor_tensor(PL[:, p % 4, 0:n], PR[:, p % 4, 0:n], PH[:, p % 4, 0:n].bitcast(F32),
                                        ALU.subtract).then_inc(piece_lo, 1)

            def hi_unit(act, u, slot):
                act.wait_ge(unit_raw[slot], (u - slot) * 16 + 32)
                if needed(2 * u - 2):
                    act.wait_ge(stat, 2 * u - 2)
                nc.scalar.activation(UH[:, slot, :, :], UR[:, slot, :, :], ACT.Copy).then_inc(unit_hi, 1)

            def lo_unit(dve, u, slot):
                dve.wait_ge(unit_hi, u + 1)
                nc.vector.tensor_tensor(UL[:, slot, :, :], UR[:, slot, :, :], UH[:, slot, :, :].bitcast(F32),
                                        ALU.subtract).then_inc(unit_lo, 1)

            V_N = 384

            def product_bank(u, hf, par):
                return bank[2 * hf + par] if isinstance(u, int) and u >= QT - 2 else bank[2 * par + hf]

            def rms_of(i, slot):
                return RM_LAST[:, slot, :] if isinstance(i, int) and i >= 2 * QT - 2 else RM[:, slot, :]

            def body(kind, i, T0, U0, G0, Q0):
                return dict(kind=kind, i=i, T=T0, U=U0, G=G0, Q=Q0, half_U=U0 // 2)

            def dilated(bd):
                return bd["kind"] in ("c3", "c2")

            def n_tiles(bd):
                return 24 if dilated(bd) else 16

            def chunks_of(bd, s):
                k = bd["kind"]
                if k == "c3":
                    return [(0, 128)]
                if k == "c2":
                    return [(0, 128), (128, 64 if s // 6 % 2 == 0 else 128)]
                if s < 6:
                    return [(0, 128), (128, 128)] + ([] if k in ("b0", "b7") else [(256, 128)])
                if s < 12:
                    return [(0, 128), (128, 64 if k == "b7" else 128)]
                return [(128 * c, 128) for c in range(4)] + ([(512, 64)] if k == "mid" else [])

            def units_of(bd, s):
                ch = chunks_of(bd, s)
                return [ch[0:4], ch[4:]] if len(ch) > 4 else [ch]

            LINKS_OWN, LINKS_LATE = 5, 15
            TAIL_LINKS = (LINKS_OWN + LINKS_LATE) * MT - LINKS_LATE
            EARLY = S - P
            Y_AT = {"b": 8, "a": 11, "c": 15}
            Y_TAIL = [(16, "y", ("b", 0, 2)), (16, "y", ("b", 2, 1)), (16, "y", ("a", 0, 2)), (16, "y", ("c", 0, 3))]

            def events(bd):
                ev = []
                for s in range(n_tiles(bd)):
                    for u in units_of(bd, s):
                        ev.append((s, "p", u))
                    if dilated(bd) or bd["kind"] == "b0":
                        continue
                    if s == Y_AT["b"]:
                        ev.append((s, "y", ("b", 0, 2)))
                    if s == Y_AT["b"] + 1:
                        ev.append((s, "y", ("b", 2, 1)))
                    if s == Y_AT["a"]:
                        ev.append((s, "y", ("a", 0, 2)))
                    if s == Y_AT["c"]:
                        ev.append((s, "y", ("c", 0, 3)))
                return ev

            def tile_units(bd, s):
                return [i for i, e in enumerate(events(bd)) if e[0] == s and e[1] == "p"]

            plan = []
            t0 = u0 = g0 = q0 = 0
            for kind, rounds, b0 in (("c3", 2, 0), ("c2", 2, 0), ("b0", 1, 0), ("b1", 1, 1), ("mid", 4, 2),
                                     ("b6", 1, 6), ("b7", 1, 7)):
                bd = body(kind, b0, t0, u0, g0, q0)
                nt, nu = n_tiles(bd), len(events(bd))
                ng, nq = (4, 8) if kind in ("c3", "c2") else (3, 6)
                plan.append((bd, rounds, (nt, nu, ng, nq)))
                t0, u0, g0, q0 = t0 + rounds * nt, u0 + rounds * nu, g0 + rounds * ng, q0 + rounds * nq
            TILES, UNITS = t0, u0 + len(Y_TAIL)
            C_GROUPS = 16

            def shifted(entry, r):
                bd, _, (nt, nu, ng, nq) = entry
                if isinstance(r, int) and r == 0:
                    return bd
                return dict(bd, i=bd["i"] + r, T=bd["T"] + r * nt, U=bd["U"] + r * nu, G=bd["G"] + r * ng,
                            Q=bd["Q"] + r * nq, half_U=bd["half_U"] + r * (nu // 2))

            def run(eng, program):
                for n, entry in enumerate(plan):
                    rounds = entry[1]
                    after = plan[n + 1][0] if n + 1 < len(plan) else None
                    before = shifted(plan[n - 1], plan[n - 1][1] - 1) if n else None
                    if rounds == 1:
                        program(entry[0], after, before)
                    elif dilated(entry[0]):
                        program(entry[0], shifted(entry, 1), before)
                        program(shifted(entry, 1), after, entry[0])
                    else:
                        program(entry[0], shifted(entry, 1), before)
                        with loop(eng, 1, rounds) as r:
                            program(shifted(entry, r), shifted(entry, r + 1), shifted(entry, r - 1))

            def width(bd, s):
                k = bd["kind"]
                if k == "c3":
                    return 128, 0
                if k == "c2":
                    return 192, (0 if s // 6 % 2 == 0 else 64)
                if s < 6:
                    return (256 if k in ("b0", "b7") else 384), 0
                if s < 12:
                    return (192 if k in ("b0", "b7") else 256), (64 if k == "b0" else 0)
                return (576 if k == "mid" else 512), 0

            def a_row0(bd):
                k = bd["kind"]
                if k == "mid":
                    return 2 * bd["i"] - 4, 14
                row0 = 0 if k in ("b0", "b1") else MT * 2 - 8
                return row0, row0 - 2 * bd["i"] + 6

            def keys(bd, s):
                k, b, (w, _) = bd["kind"], bd["i"], width(bd, s)
                if k == "c3":
                    return [KS[:, s // 6 % 2, s % 6 // 2, 0:128]]
                if k == "c2":
                    return [KS[:, s // 6 % 2, s % 6 // 2, 0:192]]
                if s < 6:
                    return [QK[:, T_BK, bass.ds(0 if k == "b0" else b * P - P, w)]]
                if s < 12:
                    return [QK[:, T_CK + (s - 6) // 2, bass.ds(0 if k == "b0" else b * P - 64, w)]]
                t0 = a_row0(bd)[0] * GW
                return [QK[:, T_AK + (s - 12) // 2, bass.ds(t0 + j, min(512, w - j))] for j in range(0, w, 512)]

            def table(bd, s):
                k, (w, _) = bd["kind"], width(bd, s)
                if k == "c3":
                    return TC3[:, s % 6, :]
                if k == "c2":
                    return TC2[:, s % 6, 64:256] if s // 6 % 2 == 0 else TC2[:, s % 6, 0:192]
                if s < 6:
                    j0 = 128 if k == "b0" else 0
                    return TB[:, s, j0:j0 + w]
                if s < 12:
                    j0 = 64 if k == "b0" else 0
                    return TC1[:, s - 6, j0:j0 + w]
                s0 = a_row0(bd)[1]
                return TA[:, s - 12, s0:s0 + w // GW, ::-1]

            def group_buf(bd, s):
                if bd["kind"] in ("c3", "c2"):
                    return G4[:, s // 6, :], s % 6
                return (GB[:, :], s) if s < 6 else (GC[:, 0, :], s - 6) if s < 12 else (GA, s - 12)

            def group_bank(bd, s):
                if bd["kind"] in ("c3", "c2"):
                    return bank[6 + s // 6 % 2]
                return bank[7] if 6 <= s < 12 else bank[6]

            def values(bd, s, c, n):
                k, b = bd["kind"], bd["i"]
                if k in ("c3", "c2"):
                    return VR[0:n, s // 6, c, (s % 6) * V1:(s % 6 + 1) * V1]
                if s < 6:
                    return VB[0:n, bass.ds((0 if k == "b0" else b - 1) + c, 1), s % 2, :].rearrange("p a d -> p (a d)")
                if s < 12:
                    return VC[0:n, bass.ds(b + c, 1), s - 6, :].rearrange("p a d -> p (a d)")
                t0 = b - 2 if k == "mid" else a_row0(bd)[0] // 2
                return VA[0:n, bass.ds(t0 + c, 1), s - 12, :].rearrange("p a d -> p (a d)")

            def dilated_rows(bd, t, q, n):
                i = bd["i"]
                if bd["kind"] == "c3":
                    return QK[:, t:t + 3, :].rearrange("p t (j r) -> p t r j", r=16)[:, :, bass.ds(8 * i + 2 * q, 2), :]
                seq_ = QK[:, t:t + 3, :].rearrange("p t (j r) -> p t r j", r=4)[:, :, bass.ds(2 * i + q // 2, 1), :]
                first = (S // 4 - n) * (q % 2)
                return seq_.rearrange("p t a j -> p t (a j)")[:, :, first:first + n]

            FAM = {"a": (0, 2, 0), "b": (2, 3, 1), "c": (5, 3, 2)}

            @block.sync
            def _(sp):
                def piece(p, parts):
                    if needed(p - 3):
                        sp.wait_ge(piece_lo, p - 3)
                    for dst, src in parts:
                        sp.dma_start(PR[:, p % 4, dst[0]:dst[1]], src).then_inc(piece_raw[p % 4], 16)

                def unit(u, slot, parts):
                    if needed(u - 1):
                        sp.wait_ge(unit_lo, u - 1)
                    for dst, src in parts:
                        sp.dma_start(dst, src).then_inc(unit_raw[slot], 16)

                def halves(slot, src):
                    return [(UR[:, slot, 4 * i:4 * i + 4, :], src[:, 4 * i:4 * i + 4, :]) for i in range(2)]

                wi = w_in[bass.ds(l, 1)].rearrange("a (k p) n -> p (a k) n", p=P)
                wo = w_out[bass.ds(l, 1)].rearrange("a (k p) n -> p (a k) n", p=P)
                wg = w_gu[bass.ds(l, 1)].rearrange("a (k p) n -> p (a k) n", p=P)
                wd = w_down[bass.ds(l, 1)].rearrange("a (k p) n -> p (a k) n", p=P)
                for k in range(8):
                    if k == 4:
                        sp.dma_start(x_res, X[:, :, :]).then_inc(x_stored, 16)
                    piece(k, [((0, 384), wi[:, k, CV:CV + 384])])
                for k in range(8):
                    piece(8 + k, [((0, 256), wi[:, k, AV:AV + 256]), ((256, 384), wi[:, k, BV:BV + 128])])

                def qk_unit(t):
                    if T_BQ <= t < T_BK:
                        a = t - T_BQ
                        unit(t, t % 2, [(UR[:, t % 2, :, 64 * g:64 * g + 64],
                                         wi[:, :, BQ + (3 * g + a) * 64:BQ + (3 * g + a) * 64 + 64]) for g in range(2)])
                    else:
                        col = CQ + t * P if t < T_BQ else BQ + 384 if t == T_BK else AQ + (t - T_AQ) * P
                        unit(t, t % 2, halves(t % 2, wi[:, :, col:col + P]))

                qk_unit(0)
                qk_unit(1)
                sp.wait_ge(x_stored, 16)
                sp.wait_ge(xn_act, 2)
                sp.wait_ge(xn_dve, 6)
                sp.dma_start(DIST[:, :], distances).then_inc(dist_in, 16)
                sp.wait_ge(v_stored, 8)
                sp.wait_ge(v_ones, 1)
                sp.dma_start(v_c.rearrange("(m p) c -> p m c", p=P),
                             VS[:, :, :, :].rearrange("p m h d -> p m (h d)")).then_inc(vs_out, 16)
                for t in range(2, QT):
                    qk_unit(t)
                for k in range(4):
                    piece(16 + k, [((0, 512), wo[:, k, 0:512])])
                for u in range(2):
                    unit(QT + u, u, halves(u, wg[:, :, u * HID:u * HID + P]))
                sp.wait_ge(stat, 2 * QT)
                sp.wait_ge(vs_out, 16)

                def load_bias(h):
                    for half in range(2):
                        for s0, n, dr in ((0, 14, 1 - half), (14, 9, 3 - half)):
                            head = rpb[bass.ds(l, 1)].rearrange("a h r c -> (a h) r c")[h]
                            src = bass.AP(head.tensor, head.offset + dr * 127, [[1, GW], [127, n], [1, GW]])
                            sp.dma_start(TA[64 * half:64 * half + 64, h, s0:s0 + n, :], src).then_inc(rpb_in, 16)

                def load_values(gi):
                    slot = gi % 4
                    if gi >= 4:
                        sp.wait_ge(pv_s, 6 * (gi - 3))
                    if gi < 8:
                        v16 = v_c.rearrange("(j r) c -> r j c", r=16)
                        for rr in range(2):
                            sp.dma_start(VR[64 * rr:64 * rr + 64, slot, 0, :], v16[2 * gi + rr]).then_inc(vr_in[slot], 16)
                    else:
                        v4 = v_c.rearrange("(t p r) c -> r p t c", p=P, r=4)
                        sp.dma_start(VR[:, slot, :, :], v4[(gi - 8) // 2]).then_inc(vr_in[slot], 16)

                def store_group(gi):
                    sp.wait_ge(grp_s, gi + 1)
                    slot = gi % 4
                    if gi < 8:
                        g16 = g_dil[1].rearrange("(j r) c -> r j c", r=16)
                        for rr in range(2):
                            sp.dma_start(g16[2 * gi + rr], G4[64 * rr:64 * rr + 64, slot, :]).then_inc(g_out_s[slot], 16)
                    else:
                        g4 = g_dil[0].rearrange("(t p r) c -> r t p c", p=P, r=4)
                        sp.dma_start(g4[(gi - 8) // 2, gi % 2], G4[:, slot, :]).then_inc(g_out_s[slot], 16)

                for gi in range(4):
                    load_values(gi)
                vsh = v_c[64:S - 64, :].rearrange("(m p) c -> p m c", p=P)
                sp.dma_start(VC[:, 1:MT, :, :].rearrange("p m h d -> p m (h d)"), vsh).then_inc(vc_in, 16)
                sp.dma_start(VC[64:128, 0, :, :].rearrange("p h d -> p (h d)"), v_c[0:64, :]).then_inc(vc_in, 16)
                sp.dma_start(VC[0:64, MT, :, :].rearrange("p h d -> p (h d)"), v_c[S - 64:S, :]).then_inc(vc_in, 16)
                for gi in range(C_GROUPS):
                    store_group(gi)
                    if gi + 4 < C_GROUPS:
                        load_values(gi + 4)
                    if gi < A_H:
                        load_bias(gi)
                for slot in range(4):
                    sp.wait_ge(g_out_s[slot], 16 * 6)
                for b in range(MT):
                    if needed(b):
                        sp.wait_ge(c_merged, b)
                    for n in range(2):
                        sp.dma_start(GC[:, 1 + n, :], g_dil[n][b * P:b * P + P, :]).then_inc(g_back, 16)
                for parity in range(2):
                    sp.wait_ge(pt_copied[parity], UNITS // 2)
                sp.dma_start(X[:, :, :], x_res).then_inc(x_back, 16)
                for p in range(20, 32):
                    piece(p, [((0, 512), wo[:, p % 8, 512 * (p // 8 - 2):512 * (p // 8 - 1)])])

                def down_pieces(g):
                    for i in range(4):
                        sp.wait_ge(piece_lo, 32 + 4 * g + i - 3)
                        sp.dma_start(PR[:, i, :], wd[:, bass.ds(2 * g + i % 2, 1), 512 * (i // 2):512 * (i // 2) + 512]
                                     .rearrange("p a n -> p (a n)")).then_inc(piece_raw[i], 16)

                def gu_units(j):
                    for u in range(2):
                        sp.wait_ge(unit_lo, QT + 2 * j + u - 1)
                        for i in range(2):
                            sp.dma_start(UR[:, u, 4 * i:4 * i + 4, :],
                                         wg[:, 4 * i:4 * i + 4, bass.ds(j * P + u * HID, P)]).then_inc(unit_raw[u], 16)

                gu_units(1)
                down_pieces(0)
                with loop(sp, 0, NG // 2) as i:
                    gu_units(4 * i + 2)
                    gu_units(4 * i + 3)
                    down_pieces(2 * i + 1)
                    gu_units(4 * i + 4)
                    gu_units(4 * i + 5)
                    down_pieces(2 * i + 2)

            @block.scalar
            def _(act):
                a = nc.scalar

                def norm(n, gain):
                    def squares(half):
                        if n:
                            for m in range(4 * half, 4 * half + 4):
                                act.wait_ge(x_add, 8 + m + 1)
                                a.activation(XN[:, m, 512:D], X[:, m, 512:D], ACT.Square,
                                             accum_out=sumsq[:, m:m + 1]).then_inc(sumsq_act, 1)
                        else:
                            for m in (4 * half, 4 * half + 2):
                                a.activation(XN[:, m, :], X[:, m, :], ACT.Square,
                                             accum_out=sumsq[:, m:m + 1]).then_inc(sumsq_act, 1)

                    def root(half):
                        act.wait_ge(sumsq_dve, 4 + half + 1 if n else 2 * half + 2)
                        if not n:
                            act.wait_ge(sumsq_act, 2 * half + 2)
                        h4 = slice(4 * half, 4 * half + 4)
                        a.activation(rms[:, h4], sumsq[:, h4], ACT.Sqrt, bias=eps[:, :], scale=1.0 / D).then_inc(rms_s, 1)
                        if not n:
                            act.wait_ge(rstd_s, half + 1)
                            m = 4 * half
                            a.activation(XN[:, m, :], X[:, m, :], ACT.Copy, scale=rstd[:, m:m + 1]).then_inc(xn_act, 1)

                    a.activation(warm[:, :], eps[:, :], ACT.Sqrt)
                    squares(0)
                    root(0)
                    if not n:
                        for p in range(4):
                            hi_piece(act, p, V_N)
                    squares(1)
                    root(1)
                    for j in range(16):
                        hf, k = j // 8, j % 8
                        act.wait_ge(xt_s, 16 * n + j + 1)
                        a.activation(HH[:, k, 512 * hf:512 * hf + 512], bank[j % 8][:, :], ACT.Identity,
                                     scale=gain[:, bass.ds(l * KD + k, 1)]).then_inc(h_hi, 1)

                norm(0, g_attn)
                for p in range(4, 11):
                    hi_piece(act, p, V_N)
                for m in range(MT):
                    act.wait_ge(moved, 8 + m)
                    a.activation(VS[:, m, :, 0:HD], bank[m][:, 0:384].rearrange("p (h d) -> p h d", d=HD),
                                 ACT.Copy).then_inc(v_stored, 1)
                for p in range(11, 16):
                    hi_piece(act, p, V_N)
                for u in range(2):
                    hi_unit(act, u, u)
                act.wait_ge(x_stored, 16)
                for m in range(MT):
                    act.wait_ge(moved, 15 + 8 + m)
                    a.activation(VA[:, m, :, 0:HD], bank[m][:, 0:256].rearrange("p (h d) -> p h d", d=HD), ACT.Copy)
                    a.activation(VB[:, m, :, 0:HD], bank[m][:, 256:384].rearrange("p (h d) -> p h d", d=HD),
                                 ACT.Copy).then_inc(v_stored, 1)

                def distance_table(tab, first, w, slope):
                    a.activation(tab, DIST[:, first:first + w], ACT.Copy, scale=slope).then_inc(table_s, 1)

                act.wait_ge(dist_in, 16)
                for h in range(C_H):
                    distance_table(TC3[:, h, :], 640, 128, 16 * SLOPES[B_H + h])

                def qk_square(u, hf, par):
                    i = 2 * u + hf
                    act.wait_ge(stat, i + 1)
                    if needed(i - 1):
                        act.wait_ge(ss_s, i - 1)
                    a.activation(SQ[:, hf, :], product_bank(u, hf, par)[:, :], ACT.Square).then_inc(sq_s, 1)

                def qk_rms(i, slot):
                    act.wait_ge(ss_s, i + 1)
                    if needed(i - 1):
                        act.wait_ge(qk_s, i - 1)
                    a.activation(rms_of(i, slot), bank[4 + slot][:, :], ACT.Sqrt, bias=eps[:, :],
                                 scale=1.0 / HD).then_inc(rmsq_s, 1)

                def qk_unit_steps(u, par, first=False, last=False):
                    qk_square(u, 0, par)
                    if not first:
                        qk_rms(2 * u - 1, 1)
                    qk_square(u, 1, par)
                    if not last:
                        hi_unit(act, u + 2, par)
                    qk_rms(2 * u, 0)

                qk_unit_steps(0, 0, first=True)
                qk_unit_steps(1, 1)
                with loop(act, 1, QT // 2 - 1) as i:
                    qk_unit_steps(2 * i, 0)
                    qk_unit_steps(2 * i + 1, 1)
                qk_unit_steps(QT - 2, 0, last=True)
                qk_unit_steps(QT - 1, 1, last=True)
                qk_rms(2 * QT - 1, 1)

                def store_result(bd, s):
                    G, n = group_buf(bd, s)
                    act.wait_ge(pv_s, bd["T"] + s + 1)
                    w = V1 * (n + 1)
                    a.activation(G[:, 0:w], group_bank(bd, s)[:, 0:w], ACT.Copy).then_inc(grp_s, 1)

                def exponential(bd, s):
                    n = bd["T"] + s
                    w, off = width(bd, s)
                    G, place_ = group_buf(bd, s)
                    act.wait_ge(tmin_s, n + 1)
                    a.activation(T[:, s % 4, off:off + w], T[:, s % 4, off:off + w], ACT.Exp, scale=-1.0,
                                 bias=G[:, 6 * V1 + place_:6 * V1 + place_ + 1]).then_inc(exp_s, 1)

                def branch_factors(b):
                    act.wait_ge(c_shift, b + 1)
                    a.activation(fac_c[:, :, :], shift_c[:, :, :], ACT.Exp).then_inc(c_fac, 1)

                def copy_unit(bd, idx, ev, b_now):
                    act.wait_ge(pt_made, bd["U"] + idx + 1)
                    if ev[1] == "p":
                        c0, w = ev[2][0][0], P * len(ev[2])
                        a.activation(PT[:, ev[0] % 4, c0:c0 + w], bank[5][:, 0:w], ACT.Copy).then_inc(pt_copied[1], 1)
                    else:
                        fam, c0, n = ev[2]
                        t0_ = Y_TILE[FAM[fam][0] + c0]
                        a.activation(QK[:, t0_:t0_ + n, bass.ds(b_now * P, P)],
                                     bank[5][:, 0:n * P].rearrange("p (t n) -> p t n", n=P),
                                     ACT.Copy).then_inc(pt_copied[1], 1)

                def act_body(bd, nxt, prev):
                    blocks = not dilated(bd)
                    for s in range(n_tiles(bd)):
                        if s + 1 < n_tiles(bd):
                            exponential(bd, s + 1)
                        elif nxt is not None:
                            exponential(nxt, 0)
                        if dilated(bd) and s % 4 == 1:
                            h = s // 4
                            if bd["kind"] == "c3" and bd["i"] == 0:
                                distance_table(TC2[:, h, :], 384, 256, 4 * SLOPES[B_H + h])
                            elif bd["kind"] == "c3":
                                distance_table(TC1[:, h, :], 384, 256, SLOPES[B_H + h])
                            elif bd["i"] == 0:
                                distance_table(TB[:, h, :], 0, 384, SLOPES[B_ORDER[h]])
                        if s == 2 and prev is not None:
                            store_result(prev, n_tiles(prev) - 1)
                        if s in ((8, 14) if blocks else (8, 14, 20)):
                            store_result(bd, s - 3)
                        if s == 3 and blocks and bd["kind"] != "b0":
                            branch_factors(bd["i"] - 1)
                        if s == 12 and blocks:
                            act.wait_ge(b_shift, bd["i"] + 1)
                            a.activation(fac_b[:, :, :], shift_b[:, :, :], ACT.Exp).then_inc(b_fac, 1)
                        for idx, ev in enumerate(events(bd)):
                            if ev[0] == s and idx % 2 == 1:
                                copy_unit(bd, idx, ev, bd["i"] - 1)

                act.wait_ge(stat, 2 * QT)
                exponential(plan[0][0], 0)
                run(act, act_body)
                last_bd = shifted(plan[-1], 0)
                store_result(last_bd, 15)
                branch_factors(MT - 1)

                def tail_square(fam, links):
                    t, n, i = FAM[fam]
                    act.wait_ge(dve_seq, TAIL_LINKS + links)
                    a.activation(T[:, i, 0:n * P], Y[:, t * P:(t + n) * P], ACT.Square,
                                 accum_out=gvar[:, i:i + 1]).then_inc(tail_squares, 1)

                def tail_scale(fam):
                    t, n, i = FAM[fam]
                    act.wait_ge(grstd_s[i], MT)
                    a.activation(Y[:, t * P:(t + n) * P], Y[:, t * P:(t + n) * P], ACT.Copy,
                                 scale=grstd[:, i:i + 1]).then_inc(y_s[i], 1)

                tail = dict(last_bd, U=UNITS - len(Y_TAIL))
                tail_square("b", 3)
                hi_piece(act, 16)
                tail_square("a", 8)
                tail_scale("b")
                hi_piece(act, 17)
                tail_scale("a")
                tail_square("c", 12)
                act.wait_ge(pt_copied[0], UNITS // 2 - 2)
                a.activation(HH[:, 0, 0:EARLY], QK[:, Y_TILE[0], 0:EARLY], ACT.Identity,
                             scale=g_out[:, bass.ds(l * KD, 1)]).then_inc(early_hi, 1)
                tail_scale("c")
                for idx, ev in enumerate(Y_TAIL):
                    if idx % 2 == 1:
                        copy_unit(tail, idx, ev, MT - 1)

                for parity in range(2):
                    act.wait_ge(pt_copied[parity], UNITS // 2)
                for f in range(KD):
                    first = 0 if f else EARLY
                    a.activation(HH[:, f, first:S], QK[:, Y_TILE[f], first:S], ACT.Identity,
                                 scale=g_out[:, bass.ds(l * KD + f, 1)]).then_inc(h_hi, 1)
                    if f in (0, 1):
                        hi_piece(act, 18 + f)
                for u in range(2):
                    hi_unit(act, QT + u, u)
                for p in range(20, 28):
                    hi_piece(act, p)
                for m in range(MT):
                    act.wait_ge(x_add, m + 1)
                    a.activation(XN[:, m, 0:512], X[:, m, 0:512], ACT.Square,
                                 accum_out=sumsq_left[:, m:m + 1]).then_inc(sumsq_act, 1)
                for p in range(28, 35):
                    hi_piece(act, p)
                norm(1, g_ffn)
                hi_piece(act, 35)

                def gate_up(j, par, cc, more=True):
                    u = QT + 2 * j
                    for hf in range(2):
                        act.wait_ge(stat, 2 * u + hf + 1)
                        if needed(2 * (j - 1) + hf + 1):
                            act.wait_ge(mul_s, 2 * (j - 1) + hf + 1)
                        a.activation(SI[:, hf, :], bank[hf][:, :], ACT.Silu).then_inc(silu_s, 1)
                    if more:
                        hi_unit(act, u + 2, 0)
                        hi_unit(act, u + 3, 1)
                    for hf in range(2):
                        act.wait_ge(mul_s, 2 * j + hf + 1)
                        a.activation(GH[:, par, cc, 512 * hf:512 * hf + 512], GT[:, hf, :], ACT.Copy).then_inc(g_hi, 1)

                def down_hi(g):
                    for i in range(4):
                        act.wait_ge(piece_raw[i], 16 * (9 + g + 1) + 32)
                        act.wait_ge(moved, 60 + 16 * g + 8 * (i // 2) + 8)
                        a.activation(PH[:, i, :], PR[:, i, :], ACT.Copy).then_inc(piece_hi, 1)

                gate_up(0, 0, 0)
                gate_up(1, 0, 1)
                with loop(act, 0, NG // 2 - 1) as i:
                    gate_up(4 * i + 2, 1, 0)
                    gate_up(4 * i + 3, 1, 1)
                    down_hi(2 * i)
                    gate_up(4 * i + 4, 0, 0)
                    gate_up(4 * i + 5, 0, 1)
                    down_hi(2 * i + 1)
                gate_up(NCH - 4, 1, 0)
                gate_up(NCH - 3, 1, 1)
                down_hi(NG - 3)
                gate_up(NCH - 2, 0, 0)
                gate_up(NCH - 1, 0, 1, more=False)
                down_hi(NG - 2)

            @block.vector
            def _(dve):
                v = nc.vector

                def norm(n, gain, hb):
                    for half in range(2):
                        h4 = slice(4 * half, 4 * half + 4)
                        if n:
                            dve.wait_ge(sumsq_act, 12 + 4 * half + 4)
                            v.tensor_tensor(sumsq[:, h4], sumsq[:, h4], sumsq_left[:, h4], ALU.add).then_inc(sumsq_dve, 1)
                        else:
                            for m in (4 * half + 1, 4 * half + 3):
                                v.tensor_tensor_reduce(out=XN[:, m, :], in0=X[:, m, :], in1=X[:, m, :], scale=1.0,
                                                       scalar=0.0, op0=ALU.mult, op1=ALU.add,
                                                       accum_out=sumsq[:, m:m + 1]).then_inc(sumsq_dve, 1)
                        dve.wait_ge(rms_s, 2 * n + half + 1)
                        v.reciprocal(rstd[:, h4], rms[:, h4]).then_inc(rstd_s, 1)
                        dve.wait_ge(rstd_s, 2 * n + half + 1)
                        for m in range(4 * half + (0 if n else 1), 4 * half + 4):
                            v.tensor_scalar(XN[:, m, :], X[:, m, :], rstd[:, m:m + 1], None, ALU.mult).then_inc(xn_dve, 1)
                        if not (n or half):
                            for p in range(4):
                                lo_piece(dve, p, V_N)
                    for j in range(16):
                        hf, k = j // 8, j % 8
                        dve.wait_ge(h_hi, hb + j + 1)
                        v.scalar_tensor_tensor(HL[:, k, 512 * hf:512 * hf + 512], bank[j % 8][:, :],
                                               gain[:, bass.ds(l * KD + k, 1)],
                                               HH[:, k, 512 * hf:512 * hf + 512].bitcast(F32),
                                               op0=ALU.mult, op1=ALU.subtract).then_inc(h_lo, 1)

                norm(0, g_attn, 0)
                for p in range(4, 16):
                    lo_piece(dve, p, V_N)
                for u in range(2):
                    lo_unit(dve, u, u)

                def stage_low(bd, q):
                    qt = dilated_rows(bd, T_CQ, q, P)[0:64]
                    dst = QS[0:64, 6 * (q % 2):6 * (q % 2) + 6:2, :]
                    if bd["kind"] == "c3":
                        dst = dst.rearrange("p t (r j) -> p t r j", r=2)
                    v.tensor_scalar(dst, qt, 1.0, None, ALU.mult).then_inc(staged_low, 1)

                def qk_finish(u, hf, par):
                    i = 2 * u + hf
                    dve.wait_ge(rmsq_s, i + 1)
                    v.reciprocal(RM[:, hf, :], RM[:, hf, :]).then_inc(rec_s, 1)
                    dve.wait_ge(rec_s, i + 1)
                    v.scalar_tensor_tensor(QK[:, bass.ds(u, 1), 512 * hf:512 * hf + 512].rearrange("p a n -> p (a n)"),
                                           product_bank(u, hf, par)[:, :], g_qk[:, bass.ds(l * QT + u, 1)], RM[:, hf, :],
                                           op0=ALU.mult, op1=ALU.mult).then_inc(qk_s, 1)

                def qk_unit_steps(u, par, first=False, last=False):
                    if not first:
                        qk_finish(u - 1, 1, 1 - par)
                    if not last:
                        lo_unit(dve, u + 2, par)
                    if not last or u < QT - 1:
                        qk_finish(u, 0, par)

                qk_unit_steps(0, 0, first=True)
                qk_unit_steps(1, 1)
                dve.wait_ge(vs_out, 16)
                with loop(dve, 1, QT // 2 - 1) as i:
                    qk_unit_steps(2 * i, 0)
                    qk_unit_steps(2 * i + 1, 1)
                stage_low(plan[0][0], 0)
                qk_unit_steps(QT - 2, 0, last=True)
                qk_unit_steps(QT - 1, 1, last=True)

                def finish_last(s):
                    hf, part = (s - 3) // 6, (s - 3) % 6
                    if not (s >= 3 and hf < 2 and part < 5):
                        return
                    i = 2 * QT - 2 + hf
                    if part < 4:
                        r = RM_LAST[:, hf, 128 * part:128 * part + 128]
                        dve.wait_ge(rmsq_s, i + 1)
                        v.reciprocal(r, r).then_inc(rec_s, 1)
                    else:
                        dve.wait_ge(rec_s, 2 * QT - 2 + 4 * (hf + 1))
                        v.scalar_tensor_tensor(QK[:, QT - 1, 512 * hf:512 * hf + 512],
                                               product_bank(QT - 1, hf, 1)[:, :], g_qk[:, bass.ds(l * QT + QT - 1, 1)],
                                               RM_LAST[:, hf, :], op0=ALU.mult, op1=ALU.mult).then_inc(qk_s, 1)

                def tmin(bd, s, gate):
                    w, off = width(bd, s)
                    G, place_ = group_buf(bd, s)
                    k = bd["kind"]
                    if gate:
                        dve.wait_ge(scored, bd["T"] + s + 1)
                    last_out = None
                    if place_ == 0 and dilated(bd):
                        last_out = 32 * bd["i"] if k == "c3" else 64 + 16 * bd["i"]
                        if needed(last_out):
                            dve.wait_ge(g_out_s[s // 6], last_out)
                    if k == "b0" and s in (6, 12):
                        last_out = 96
                        dve.wait_ge(g_out_s[0 if s == 6 else 3], last_out)
                    if gate or last_out is not None:
                        dve.sem_inc(dve_gate, 1)
                    if off:
                        v.memset(T[:, s % 4, 0:off], 0.0)
                    acc = G[:, 6 * V1 + place_:6 * V1 + place_ + 1]
                    tt, sc = T[:, s % 4, off:off + w], score2[s % 2][:, 0:w]
                    if not dilated(bd) and s >= 12:
                        tt, sc = (t_.rearrange("p (s c) -> p s c", c=GW) for t_ in (tt, sc))
                    v.tensor_tensor_reduce(out=tt, in0=table(bd, s), in1=sc,
                                           scale=1.0, scalar=3.0e38, op0=ALU.add, op1=ALU.min,
                                           accum_out=acc).then_inc(tmin_s, 1)

                seq = dict(base=0, n=0)

                def links():
                    return seq["base"] + seq["n"]

                def link(ins):
                    seq["n"] += 1
                    ins.then_inc(dve_seq, 1)

                def heads(G, n):
                    return G[:, 0:n * V1].rearrange("p (h d) -> p h d", d=V1)

                def spread(c, n):
                    return c.unsqueeze(2).broadcast_to([P, n, HD])

                NS = l * B_H
                YB, YC, YA = Y[:, 256:640], Y[:, 640:1024], Y[:, 0:256]
                gb, ga, gc0 = heads(GB[:, :], 6), heads(GA, 4), heads(GC[:, 0, :], 6)

                def max_of(i):
                    return GC[:, i, 6 * V1:6 * V1 + 6]

                def squares(fam, cols, n):
                    link(v.tensor_tensor_reduce(out=junk[:, 0:n], in0=cols, in1=cols, scale=1.0, scalar=0.0,
                                                op0=ALU.mult, op1=ALU.add, accum_out=gvar[:, fam:fam + 1]))

                def mean(fam, n):
                    v.tensor_scalar(gvare[:, fam:fam + 1], gvar[:, fam:fam + 1], 1.0 / n, EPS, ALU.mult,
                                    ALU.add).then_inc(gvar_s[fam], 1)

                def scale_y(fam, b):
                    t, n, i = FAM[fam]
                    dve.wait_ge(grstd_s[i], b + 1)
                    v.tensor_scalar(Y[:, t * P:(t + n) * P], Y[:, t * P:(t + n) * P], grstd[:, i:i + 1], None,
                                    ALU.mult).then_inc(y_s[i], 1)

                def own_finish(b, s):
                    nm, sk = GB[:, 6 * V1:6 * V1 + 6], nsink[:, bass.ds(NS, 6)]
                    if s == 10:
                        dve.wait_ge(grp_s, C_GROUPS + 3 * b + 1)
                        if needed(links()):
                            dve.wait_ge(dve_seq, links())
                        link(v.tensor_tensor(nmin[:, :], nm, sk, ALU.min))
                    elif s == 11:
                        dve.wait_ge(dve_seq, links())
                        v.tensor_tensor(shift_b[:, 0, :], nmin[:, :], nm, ALU.subtract)
                        v.tensor_tensor(shift_b[:, 1, :], nmin[:, :], sk, ALU.subtract).then_inc(b_shift, 1)
                    elif s == 13:
                        dve.wait_ge(b_fac, b + 1)
                        link(v.tensor_tensor(den[:, 0, :].unsqueeze(2), gb[:, :, HD:V1],
                                             fac_b[:, 0, :].unsqueeze(2), ALU.mult))
                    elif s == 14:
                        dve.wait_ge(dve_seq, links())
                        link(v.tensor_tensor(den[:, 0, :], den[:, 0, :], fac_b[:, 1, :], ALU.add))
                    elif s == 15:
                        dve.wait_ge(dve_seq, links())
                        link(v.reciprocal(den[:, 0, :], den[:, 0, :]))
                        dve.wait_ge(grp_s, C_GROUPS + 3 * b + 2)
                        dve.wait_ge(g_back, 32 * (b + 1))
                        link(v.tensor_tensor(nmin[:, :], max_of(0), max_of(1), ALU.min))

                def late_finish(b, s, tail=False):
                    if s in (0, 1, 2, 3, 4, 5, 6, 7, 8, 9, 10, 11):
                        dve.wait_ge(dve_seq, links())
                    if s == 0:
                        link(v.tensor_tensor(coef[:, 0, :], den[:, 0, :], fac_b[:, 0, :], ALU.mult))
                        link(v.tensor_tensor(nmin[:, :], nmin[:, :], max_of(2), ALU.min))
                    elif s == 1:
                        link(v.tensor_tensor(YB.rearrange("p (g a d) -> p a g d", g=2, a=3),
                                             gb[:, :, 0:HD].rearrange("p (a g) d -> p a g d", g=2),
                                             coef[:, 0, :].rearrange("p (a g) -> p a g", g=2).unsqueeze(3)
                                             .broadcast_to([P, 3, 2, HD]), ALU.mult))
                        v.tensor_tensor(shift_c[:, :, :], nmin[:, :].unsqueeze(1).broadcast_to([P, 3, 6]),
                                        GC[:, :, 6 * V1:6 * V1 + 6], ALU.subtract).then_inc(c_shift, 1)
                    elif s == 2:
                        squares(1, YB, 384)
                    elif s == 3:
                        if tail:
                            dve.wait_ge(tail_squares, 1)
                        mean(1, 384)
                    elif s in (4, 5):
                        if s == 4:
                            dve.wait_ge(c_fac, b + 1)
                        for i in ((0,) if s == 4 else (1, 2)):
                            link(v.tensor_tensor(heads(GC[:, i, :], 6), heads(GC[:, i, :], 6),
                                                 fac_c[:, i, :].unsqueeze(2).broadcast_to([P, 6, V1]), ALU.mult))
                        if s == 4:
                            dve.wait_ge(grp_s, C_GROUPS + 3 * b + 3)
                            link(v.reciprocal(den[:, 1, 0:4].unsqueeze(2), ga[:, :, HD:V1]))
                        else:
                            link(v.tensor_tensor(YA.rearrange("p (h d) -> p h d", d=HD), ga[:, :, 0:HD],
                                                 spread(den[:, 1, 0:4], 4), ALU.mult))
                            if not tail:
                                scale_y("b", b)
                    elif s in (6, 7):
                        link(v.tensor_tensor(GC[:, 0, 0:6 * V1], GC[:, 0, 0:6 * V1], GC[:, s - 5, 0:6 * V1], ALU.add))
                        if s == 6 and not tail:
                            squares(0, YA, 256)
                        elif s == 7:
                            if tail:
                                dve.wait_ge(tail_squares, 2)
                            mean(0, 256)
                    elif s == 8:
                        link(v.reciprocal(den[:, 2, :].unsqueeze(2), gc0[:, :, HD:V1]))
                    elif s == 9:
                        link(v.tensor_tensor(YC.rearrange("p (h d) -> p h d", d=HD), gc0[:, :, 0:HD],
                                             spread(den[:, 2, :], 6), ALU.mult))
                        if not tail:
                            scale_y("a", b)
                    elif s == 10:
                        dve.sem_inc(c_merged, 1)
                        squares(2, YC, 384)
                    elif s == 11:
                        if tail:
                            dve.wait_ge(tail_squares, 3)
                        mean(2, 384)
                    elif s == 12:
                        scale_y("c", b)

                def copy_unit(bd, idx, ev, b_now):
                    dve.wait_ge(pt_made, bd["U"] + idx + 1)
                    if ev[1] == "p":
                        c0, w = ev[2][0][0], P * len(ev[2])
                        v.tensor_copy(PT[:, ev[0] % 4, c0:c0 + w], bank[4][:, 0:w]).then_inc(pt_copied[0], 1)
                    else:
                        fam, c0, n = ev[2]
                        t0_ = Y_TILE[FAM[fam][0] + c0]
                        v.tensor_scalar(QK[:, t0_:t0_ + n, bass.ds(b_now * P, P)],
                                        bank[4][:, 0:n * P].rearrange("p (t n) -> p t n", n=P), 1.0, None,
                                        ALU.mult).then_inc(pt_copied[0], 1)

                def bias_table(h):
                    dve.wait_ge(rpb_in, 64 * (h + 1))
                    v.tensor_tensor(TA[:, h, :, :], col_mask[:, ::-1].unsqueeze(1).broadcast_to([P, TA_S, GW]),
                                    TA[:, h, :, :], ALU.subtract).then_inc(ta_sub, 1)
                    dve.wait_ge(ta_sub, h + 1)
                    v.memset(TA[0:64, h, 22, :], BIG)
                    v.memset(TA[64:128, h, 14, :], BIG).then_inc(ta_made, 1)

                def dve_body(bd, nxt):
                    b = bd["i"]
                    for s in range(n_tiles(bd)):
                        even = [(idx, ev) for idx, ev in enumerate(events(bd)) if ev[0] == s and idx % 2 == 0]
                        for idx, ev in even:
                            copy_unit(bd, idx, ev, b - 1)
                        if s + 2 < n_tiles(bd):
                            tmin(bd, s + 2, not even)
                        elif nxt is not None:
                            if s + 2 == n_tiles(bd) and nxt["kind"] == "b0":
                                dve.wait_ge(ta_made, A_H)
                                dve.sem_inc(dve_gate, 1)
                            if s + 2 == n_tiles(bd) and nxt["kind"] in ("c2", "b0") and bd["kind"] != nxt["kind"]:
                                dve.wait_ge(table_s, 12 if nxt["kind"] == "c2" else 24)
                                dve.sem_inc(dve_gate, 1)
                            tmin(nxt, s + 2 - n_tiles(bd), not even)
                        if dilated(bd):
                            if bd["kind"] == "c3" and b == 0:
                                finish_last(s)
                            if bd["kind"] == "c2" and b == 1 and s % 6 == 1:
                                bias_table(s // 6)
                            if s % 6 == 2:
                                if s < 18:
                                    stage_low(bd, s // 6 + 1)
                                elif dilated(nxt):
                                    stage_low(nxt, 0)
                            continue
                        own_finish(b, s)
                        if bd["kind"] != "b0":
                            late_finish(b - 1, s)

                dve.wait_ge(table_s, C_H)
                dve.sem_inc(dve_gate, 1)
                tmin(plan[0][0], 0, True)
                tmin(plan[0][0], 1, True)

                def dve_round(bd, nxt, before):
                    seq["n"] = 0
                    seq["base"] = 0
                    if not dilated(bd) and bd["kind"] != "b0":
                        seq["base"] = (LINKS_OWN + LINKS_LATE) * bd["i"] - LINKS_LATE
                    dve_body(bd, nxt)
                    if not dilated(bd):
                        assert seq["n"] == LINKS_OWN + (LINKS_LATE if bd["kind"] != "b0" else 0), seq

                run(dve, dve_round)
                seq["base"], seq["n"] = TAIL_LINKS, 0
                tail = dict(plan[-1][0], U=UNITS - len(Y_TAIL))
                for s in (0, 1, 4, 5, 3, 6, 7, 8, 9):
                    late_finish(MT - 1, s, tail=True)
                lo_piece(dve, 16)
                dve.sem_inc(c_merged, 1)
                late_finish(MT - 1, 11, tail=True)

                def lo_mixed(f, first, last):
                    return v.scalar_tensor_tensor(HL[:, f, first:last], QK[:, Y_TILE[f], first:last],
                                                  g_out[:, bass.ds(l * KD + f, 1)], HH[:, f, first:last].bitcast(F32),
                                                  op0=ALU.mult, op1=ALU.subtract)

                for idx, ev in enumerate(Y_TAIL):
                    if idx % 2 == 0:
                        copy_unit(tail, idx, ev, MT - 1)
                    if idx == 1:
                        dve.wait_ge(pv_s, TILES)
                        dve.wait_ge(early_hi, 1)
                        lo_mixed(0, 0, EARLY)
                for f in range(KD):
                    dve.wait_ge(h_hi, 16 + f + 1)
                    lo_mixed(f, 0 if f else EARLY, S).then_inc(h_lo, 1)
                    if f < 3:
                        lo_piece(dve, 17 + f)
                for u in range(2):
                    lo_unit(dve, QT + u, u)
                for p in range(20, 27):
                    lo_piece(dve, p)

                def add_out(ch):
                    for m in range(MT):
                        dve.wait_ge(moved, 15 * ch + 8 + m)
                        xs = X[:, m, 512 * (ch - 2):512 * (ch - 1)]
                        v.tensor_tensor(xs, xs, bank[m][:, :], ALU.add).then_inc(x_add, 1)

                dve.wait_ge(x_back, 16)
                add_out(2)
                for p in range(27, 35):
                    lo_piece(dve, p)
                add_out(3)
                norm(1, g_ffn, 24)
                lo_piece(dve, 35)

                def gate_up(j, par, cc, more=True):
                    u = QT + 2 * j
                    if more:
                        lo_unit(dve, u + 2, 0)
                        lo_unit(dve, u + 3, 1)
                    for hf in range(2):
                        dve.wait_ge(stat, 2 * u + 2 + hf + 1)
                        dve.wait_ge(silu_s, 2 * j + hf + 1)
                        if needed(2 * (j - 1) + hf + 1):
                            dve.wait_ge(g_lo, 2 * (j - 1) + hf + 1)
                        v.tensor_tensor(GT[:, hf, :], SI[:, hf, :], bank[2 + hf][:, :], ALU.mult).then_inc(mul_s, 1)
                    for hf in range(2):
                        dve.wait_ge(g_hi, 2 * j + hf + 1)
                        v.tensor_tensor(GL[:, par, cc, 512 * hf:512 * hf + 512], GT[:, hf, :],
                                        GH[:, par, cc, 512 * hf:512 * hf + 512].bitcast(F32),
                                        ALU.subtract).then_inc(g_lo, 1)

                def down(g, more=True):
                    for c in range(2):
                        for m in range(MT):
                            dve.wait_ge(moved, 60 + 16 * g + 8 * c + m + 1)
                            xs = X[:, m, 512 * c:512 * c + 512]
                            v.tensor_tensor(xs, xs, bank[4 + m % 4][:, :], ALU.add).then_inc(x_add, 1)
                        for i in range(2):
                            if more:
                                dve.wait_ge(piece_hi, 32 + 4 * (g + 1) + 2 * c + i + 1)
                                v.tensor_tensor(PL[:, 2 * c + i, :], PR[:, 2 * c + i, :],
                                                PH[:, 2 * c + i, :].bitcast(F32), ALU.subtract).then_inc(piece_lo, 1)

                gate_up(0, 0, 0)
                gate_up(1, 0, 1)
                with loop(dve, 0, NG // 2 - 1) as i:
                    gate_up(4 * i + 2, 1, 0)
                    gate_up(4 * i + 3, 1, 1)
                    down(2 * i)
                    gate_up(4 * i + 4, 0, 0)
                    gate_up(4 * i + 5, 0, 1)
                    down(2 * i + 1)
                gate_up(NCH - 4, 1, 0)
                gate_up(NCH - 3, 1, 1)
                down(NG - 3)
                gate_up(NCH - 2, 0, 0)
                gate_up(NCH - 1, 0, 1, more=False)
                down(NG - 2)
                down(NG - 1, more=False)

            @block.gpsimd
            def _(pool):
                g = nc.gpsimd
                pool.wait_ge(xt_s, 16)
                g.memset(VS[:, :, :, HD:V1], 1.0).then_inc(v_ones, 1)
                pool.wait_ge(x_stored, 16)
                pool.wait_ge(xn_act, 2)
                pool.wait_ge(xn_dve, 6)
                g.memset(VA[:, :, :, HD:V1], 1.0)
                g.memset(VB[:, :, :, HD:V1], 1.0).then_inc(v_ones, 1)

                def carrier():
                    pool.sem_inc(pool_gate, 1)

                def stage(bd, before, q, after_powers):
                    k, i = bd["kind"], bd["i"]
                    nh = 4 if q == 2 and not dilated(bd) else 6
                    q2 = q % 2 if dilated(bd) else q
                    if dilated(bd) and q >= 2:
                        pool.wait_ge(scored, bd["T"] + 6 * (q - 1))
                    elif before is not None:
                        last = 6 * q + 18 if dilated(before) else 6 * q + nh
                        pool.wait_ge(scored, before["T"] + min(last, n_tiles(before)))
                    done = bd["Q"] + 2 * q
                    if needed(done):
                        pool.wait_ge(staged, done)
                    after_powers()
                    carrier()
                    if dilated(bd):
                        dst = QS[64:128, 6 * q2 + 1:6 * q2 + 7:2, :]
                        kd = KS[:, q2, :, :]
                        if k == "c3":
                            dst = dst.rearrange("p t (r j) -> p t r j", r=2)
                            kd = KS[:, q2, :, 0:128].rearrange("p t (r j) -> p t r j", r=2)
                        g.tensor_copy(dst, dilated_rows(bd, T_CQ, q, P)[64:128]).then_inc(staged, 1)
                        pool.wait_ge(staged, done + 1)
                        carrier()
                        g.tensor_copy(kd, dilated_rows(bd, T_CK, q, 192)).then_inc(staged, 1)
                    else:
                        t0_ = (T_BQ, T_CQ, T_AQ)[q]
                        qt = QK[:, t0_:t0_ + nh // 2, bass.ds(i * P, P)]
                        for par in (1, 0):
                            g.tensor_copy(QS[64 * par:64 * par + 64, 6 * q + par:6 * q + nh:2, :],
                                          qt[64 * par:64 * par + 64]).then_inc(staged, 1)

                def mean_powers(fam, b, copies):
                    pool.wait_ge(gvar_s[fam], b + 1)
                    pool.wait_ge(staged, copies)
                    carrier()
                    g.tensor_tensor(grstd[:, fam:fam + 1], gvare[:, fam:fam + 1], neghalf[:, :],
                                    ALU.pow).then_inc(grstd_s[fam], 1)

                def pool_body(bd, nxt, before):
                    b = bd["i"]
                    if dilated(bd):
                        first = bd["kind"] == "c3" and before is None
                        for q in range(4):
                            stage(bd, before, q, (lambda: pool.wait_ge(v_ones, 3 if bd["kind"] == "c2" else 2))
                                  if q == 0 else (lambda: None))
                            if first and q == 1:
                                pool.wait_ge(stat, 2 * QT)
                                pool.wait_ge(staged, 4)
                                g.memset(VC[0:64, 0, :, :], 0.0).then_inc(v_ones, 1)
                        return
                    if bd["kind"] == "b0":
                        pool.wait_ge(qk_s, 2 * QT)
                    powers = bd["kind"] not in ("b0", "b1")
                    if powers:
                        mean_powers(1, b - 2, bd["Q"])
                    stage(bd, before, 0, (lambda: pool.wait_ge(grstd_s[1], b - 1)) if powers else (lambda: None))
                    if powers:
                        mean_powers(0, b - 2, bd["Q"] + 2)
                        mean_powers(2, b - 2, bd["Q"] + 2)
                    stage(bd, before, 1, (lambda: pool.wait_ge(grstd_s[2], b - 1)) if powers else (lambda: None))
                    stage(bd, before, 2, lambda: None)

                pool.wait_ge(qk_s, 2 * T_BQ)
                run(pool, pool_body)
                for b in (MT - 2, MT - 1):
                    for fam in (1, 0, 2):
                        mean_powers(fam, b, plan[-1][0]["Q"] + 6)

            @block.tensor
            def _(pe):
                t = nc.tensor

                def three(dst, sh, sl, mh, ml, start, stop):
                    t.matmul(dst, sh, mh, start=start, stop=False)
                    t.matmul(dst, sh, ml, start=False, stop=False)
                    return t.matmul(dst, sl, mh, start=False, stop=stop)

                def norm(n, hb):
                    for j in range(16):
                        hf, k = j // 8, j % 8
                        if k == 0:
                            if not n:
                                pe.wait_ge(xn_act, hf + 1)
                            pe.wait_ge(xn_dve, 6 + 4 * hf + 4 if n else 3 * hf + 3)
                        if hf:
                            pe.wait_ge(h_lo, hb + j - 8 + 1)
                        elif n and k >= 4:
                            pe.wait_ge(x_add, 8 + k + 1)
                        for i in range(4):
                            last = t.transpose(bank[j % 8][:, P * i:P * i + P], XN[:, 4 * hf + i, P * k:P * k + P], ident[:, :])
                        last.then_inc(xt_s, 1)

                def moving(ch, n, hb, bank_wait):
                    for k in range(KD):
                        p = 8 * ch + k
                        pe.wait_ge(piece_lo, p + 1)
                        for m in range(MT):
                            if hb is not None and (m == 0 or hb == 8 and k == 0):
                                pe.wait_ge(h_lo, hb + max(k, m) + 1)
                            if k == 0 and bank_wait:
                                bank_wait(m)
                            ins = three(bank[m][:, 0:n], HH[:, k, P * m:P * m + P], HL[:, k, P * m:P * m + P],
                                        PH[:, p % 4, 0:n], PL[:, p % 4, 0:n], k == 0, k == KD - 1)
                            if k == KD - 1 or m == MT - 1:
                                ins.then_inc(moved, 1)

                norm(0, 0)
                moving(0, V_N, 8, None)
                moving(1, V_N, None, lambda m: pe.wait_ge(v_stored, m + 1))

                def half_unit(u, slot, hf, dst, hb=None):
                    for k in range(KD):
                        if hb is not None:
                            pe.wait_ge(h_lo, hb + (8 if hf else 0) + k + 1)
                        last = three(dst, UH[:, slot, k, :], UL[:, slot, k, :], HH[:, k, 512 * hf:512 * hf + 512],
                                     HL[:, k, 512 * hf:512 * hf + 512], k == 0, k == KD - 1)
                    last.then_inc(stat, 1)

                def square_sums(i, slot):
                    pe.wait_ge(sq_s, i + 1)
                    if needed(i - 1):
                        pe.wait_ge(rmsq_s, i - 1)
                    t.matmul(bank[4 + slot][:, :], bones[:, :], SQ[:, slot, :], start=True, stop=True).then_inc(ss_s, 1)

                def qk_unit_steps(u, par, first=False, last=False):
                    pe.wait_ge(unit_lo, u + 1)
                    if needed(2 * u - 3):
                        pe.wait_ge(qk_s, 2 * u - 3)
                    half_unit(u, par, 0, product_bank(u, 0, par)[:, :])
                    if not first:
                        square_sums(2 * u - 1, 1)
                    if needed(2 * u - 2):
                        pe.wait_ge(qk_s, 2 * u - 2 + (1 if last and par == 0 else 0))
                    half_unit(u, par, 1, product_bank(u, 1, par)[:, :])
                    square_sums(2 * u, 0)

                pe.wait_ge(v_stored, 16)
                qk_unit_steps(0, 0, first=True)
                qk_unit_steps(1, 1)
                with loop(pe, 1, QT // 2 - 1) as i:
                    qk_unit_steps(2 * i, 0)
                    qk_unit_steps(2 * i + 1, 1)
                qk_unit_steps(QT - 2, 0, last=True)
                qk_unit_steps(QT - 1, 1, last=True)
                square_sums(2 * QT - 1, 1)

                def score(bd, s):
                    if s % 6 == 0:
                        pe.wait_ge(staged, bd["Q"] + 2 * (s // 6 + 1))
                        if dilated(bd):
                            pe.wait_ge(staged_low, bd["G"] + s // 6 + 1)
                    slot = s % 2
                    if needed(bd["T"] + s - 1):
                        pe.wait_ge(tmin_s, bd["T"] + s - 1)
                    for j, kk in enumerate(keys(bd, s)):
                        w = kk.shape[-1]
                        last = t.matmul(score2[slot][:, 512 * j:512 * j + w], QS[:, s % 12 if dilated(bd) else s, :], kk, start=True, stop=True)
                    last.then_inc(scored, 1)

                def unit(bd, idx, ev, b_now):
                    dst = bank[4 + idx % 2]
                    if ev[1] == "p":
                        pe.wait_ge(exp_s, bd["T"] + ev[0] + 1)
                        srcs = [T[:, ev[0] % 4, c:c + P] for c, _ in ev[2]]
                    else:
                        fam, c0, n = ev[2]
                        t0_, _, fi = FAM[fam]
                        pe.wait_ge(y_s[fi], b_now + 1)
                        srcs = [Y[:, (t0_ + c0 + i) * P:(t0_ + c0 + i + 1) * P] for i in range(n)]
                    if needed(bd["half_U"] + idx // 2):
                        pe.wait_ge(pt_copied[idx % 2], bd["half_U"] + idx // 2)
                    for i, src in enumerate(srcs):
                        last = t.transpose(dst[0:src.shape[-1], P * i:P * i + P], src, ident[:, :])
                    last.then_inc(pt_made, 1)

                def weigh(bd, s):
                    k = bd["kind"]
                    for idx in tile_units(bd, s):
                        pe.wait_ge(pt_copied[idx % 2], bd["half_U"] + idx // 2 + 1)
                    if s % 6 == 0:
                        if dilated(bd):
                            pe.wait_ge(vr_in[s // 6], (32 if k == "c3" else 16) * (bd["i"] + 1) + (64 if k == "c2" else 0))
                        if k == "b0" and s == 6:
                            pe.wait_ge(vc_in, 48)
                            pe.wait_ge(v_ones, 3)
                        stored = bd["G"] + s // 6 - 1 + (1 if s == 0 and not dilated(bd) and k != "b0" else 0)
                        if needed(stored):
                            pe.wait_ge(grp_s, stored)
                    place_ = group_buf(bd, s)[1]
                    chs = chunks_of(bd, s)
                    for c, (col, n) in enumerate(chs):
                        last = t.matmul(group_bank(bd, s)[:, place_ * V1:place_ * V1 + V1],
                                        PT[0:n, s % 4, P * c:P * c + P], values(bd, s, c, n),
                                        start=(c == 0), stop=(c == len(chs) - 1))
                    last.then_inc(pv_s, 1)

                def pe_body(bd, nxt, prev):
                    evs = events(bd)
                    nt = n_tiles(bd)
                    for s in range(nt):
                        if s + 2 < nt:
                            score(bd, s + 2)
                        elif nxt is not None:
                            score(nxt, s + 2 - nt)
                        for idx, ev in enumerate(evs):
                            if ev[0] == s:
                                unit(bd, idx, ev, bd["i"] - 1)
                        if s >= 2:
                            weigh(bd, s - 2)
                        elif prev is not None:
                            weigh(prev, n_tiles(prev) + s - 2)

                pe.wait_ge(qk_s, 2 * QT - 2)
                score(plan[0][0], 0)
                score(plan[0][0], 1)
                run(pe, pe_body)
                weigh(plan[-1][0], 14)
                weigh(plan[-1][0], 15)
                tail = dict(plan[-1][0], U=UNITS - len(Y_TAIL), half_U=(UNITS - len(Y_TAIL)) // 2)
                for idx, ev in enumerate(Y_TAIL):
                    unit(tail, idx, ev, MT - 1)

                moving(2, 512, 16, None)
                moving(3, 512, None, lambda m: pe.wait_ge(x_add, m + 1))
                norm(1, 24)

                def gate_up(j, first=False):
                    u = QT + 2 * j
                    for gu in range(2):
                        pe.wait_ge(unit_lo, u + gu + 1)
                        for hf in range(2):
                            if first and gu == 0:
                                pe.wait_ge(h_lo, 24 + 8 + hf + 1)
                            if needed(2 * (j - 1) + hf + 1):
                                pe.wait_ge(mul_s if gu else silu_s, 2 * (j - 1) + hf + 1)
                            half_unit(u + gu, gu, hf, bank[2 * gu + hf][:, :], 24 if first and gu == 0 else None)

                def down(g, par):
                    pe.wait_ge(g_lo, 4 * g + 4)
                    for c in range(2):
                        pe.wait_ge(piece_lo, 32 + 4 * g + 2 * c + 2)
                        for m in range(MT):
                            pe.wait_ge(x_add, 16 + 16 * g + 8 * c + m - 4 + 1)
                            for kk in range(2):
                                i = 2 * c + kk
                                last = three(bank[4 + m % 4][:, :], GH[:, par, kk, P * m:P * m + P],
                                             GL[:, par, kk, P * m:P * m + P], PH[:, i, :], PL[:, i, :], kk == 0, kk == 1)
                            last.then_inc(moved, 1)

                gate_up(0, first=True)
                gate_up(1)
                with loop(pe, 0, NG // 2) as i:
                    gate_up(4 * i + 2)
                    gate_up(4 * i + 3)
                    down(2 * i, 0)
                    gate_up(4 * i + 4)
                    gate_up(4 * i + 5)
                    down(2 * i + 1, 1)
                down(NG - 1, 0)

            programs.close()
            nc.all_engine_barrier(sems_to_clear=range(sems[0].num, sems[-1].num + 1))

        with ExitStack() as end:
            out_s = end.enter_context(nc.semaphore("out_written"))
            block = end.enter_context(nc.Block())

            @block.sync
            def _(sp):
                sp.dma_start(outr, X[:, :, :]).then_inc(out_s, 16)
                sp.wait_ge(out_s, 16)


def kernel(x, attn_norm, w_in, qk_gain, rpb, sink, out_gain, w_out, ffn_norm, w_gu, w_down):
    import numpy as np
    import concourse.bacc as bacc
    from concourse import mybir as mb
    from concourse.bass_utils import run_bass_kernel_spmd as run

    nc = bacc.Bacc("TRN2", target_bir_lowering=False, num_devices=1, dynamic_dma_scratch_size=1024)
    rpb = np.asarray(rpb)
    padded = np.zeros(rpb.shape[:3] + (127,), rpb.dtype)
    padded[..., 48:79] = rpb[..., ::-1]
    ins = dict(x=x, attn_norm=attn_norm, w_in=w_in, qk_gain=qk_gain, rpb=padded, sink=sink, out_gain=out_gain,
               w_out=w_out, ffn_norm=ffn_norm, w_gu=w_gu, w_down=w_down)
    arrays, args = {}, []
    for name, a in ins.items():
        a = np.ascontiguousarray(a)
        arrays[f"in_{name}"] = a
        args.append(nc.dram_tensor(f"in_{name}", a.shape, mb.dt.from_np(a.dtype), kind="ExternalInput").ap())
    args.append(nc.dram_tensor("result", x.shape, mb.dt.float32, kind="ExternalOutput").ap())
    build_program(nc, *args)
    return run(nc, [arrays], core_ids=[0]).results[0]["result"]
```
